# Optimizing a Trainium2 kernel written in Bass

```python
import jax, jax.numpy as jnp
from jax import lax
import numpy as np

D_MODEL = 1024
BATCH = 1
SEQ = 1024
DEPTH = 1

D_MIX = D_MODEL
A_WIDTH = D_MIX // 2
A_HEADS = 4
A_HEAD_DIM = A_WIDTH // A_HEADS
A_CHUNK = 128
B_WIDTH = D_MIX - A_WIDTH
B_HEADS = 4
B_V_DIM = B_WIDTH // B_HEADS
B_K_DIM = B_V_DIM // 2
B_KEY_WIDTH = B_HEADS * B_K_DIM
B_GATE_RANK = 16
B_GATE_TAU = 16.0
B_CHUNK = 64
IN_WIDTHS = (A_WIDTH, A_WIDTH, B_KEY_WIDTH, B_KEY_WIDTH, B_WIDTH, B_WIDTH, B_GATE_RANK)
IN_OFFSETS = tuple(int(o) for o in np.cumsum((0,) + IN_WIDTHS))
P_IN = IN_OFFSETS[-1]
N_GROUPS = 4
EXPERTS_PER_GROUP = 8
N_EXPERTS = N_GROUPS * EXPERTS_PER_GROUP
TOP_K_INNER = 2
D_EXPERT = 512
MOE_BLOCK = 256
EPS = 1e-6

kernel_name = "hymba_sgu_gla_hmoe_adaln_trunk"

def rms_norm(x, gain):
    x32 = x.astype(jnp.float32)
    y = x32 * lax.rsqrt(jnp.mean(x32 * x32, axis=-1, keepdims=True) + EPS)
    return (y * gain.astype(jnp.float32)).astype(x.dtype)

def sgu_mixer(u, v, v_gain, w_s, b_s):
    bsz, s, _ = u.shape
    nc = s // A_CHUNK
    v = rms_norm(v, v_gain).reshape(bsz, nc, A_CHUNK, A_HEADS, A_HEAD_DIM)
    causal = jnp.tril(jnp.ones((A_CHUNK, A_CHUNK), dtype=bool))
    w = jnp.where(causal[None], w_s, 0.0).astype(v.dtype)
    z = jnp.einsum('hts,bcshd->bcthd', w, v) + b_s.T.astype(v.dtype)[:, :, None]
    return u * z.reshape(bsz, s, A_WIDTH)

def gla_mixer(q, k, v, r, a_low, w_alpha, b_alpha, out_gain):
    f32 = jnp.float32
    bsz, s, _ = q.shape
    nc = s // B_CHUNK
    q = q.astype(f32).reshape(bsz, s, B_HEADS, B_K_DIM) * (B_K_DIM ** -0.5)
    k = k.astype(f32).reshape(bsz, s, B_HEADS, B_K_DIM)
    v = v.astype(f32).reshape(bsz, s, B_HEADS, B_V_DIM)
    log_a = jax.nn.log_sigmoid((a_low @ w_alpha + b_alpha).astype(f32)) / B_GATE_TAU
    log_a = log_a.reshape(bsz, s, B_HEADS, B_K_DIM)

    def chunks(t):
        return t.reshape(bsz, nc, B_CHUNK, *t.shape[2:]).swapaxes(0, 1)

    causal = jnp.tril(jnp.ones((B_CHUNK, B_CHUNK), dtype=bool))[None, :, :, None, None]

    def step(state, inp):
        qc, kc, vc, gc = inp
        bcum = jnp.cumsum(gc, axis=1)
        blast = bcum[:, -1]
        o_inter = jnp.einsum('bthk,bhkv->bthv', qc * jnp.exp(bcum), state)
        diff = jnp.where(causal, bcum[:, :, None] - bcum[:, None, :], -jnp.inf)
        scores = jnp.einsum('bthk,bshk,btshk->btsh', qc, kc, jnp.exp(diff))
        o_intra = jnp.einsum('btsh,bshv->bthv', scores, vc)
        k_dec = kc * jnp.exp(blast[:, None] - bcum)
        state = state * jnp.exp(blast)[..., None] + jnp.einsum('bshk,bshv->bhkv', k_dec, vc)
        return state, o_inter + o_intra

    state0 = jnp.zeros((bsz, B_HEADS, B_K_DIM, B_V_DIM), f32)
    _, o = lax.scan(step, state0, (chunks(q), chunks(k), chunks(v), chunks(log_a)))
    o = o.swapaxes(0, 1).reshape(bsz, s, B_HEADS, B_V_DIM)
    o = o * lax.rsqrt(jnp.mean(o * o, axis=-1, keepdims=True) + EPS)
    o = o * out_gain.astype(f32).reshape(B_HEADS, B_V_DIM)
    o = o.reshape(bsz, s, B_WIDTH) * jax.nn.silu(r.astype(f32))
    return o.astype(r.dtype)

def hier_moe(h, w_group, b_group, w_router, b_router, w1, w3, w2):
    bsz, s, d = h.shape
    t = bsz * s
    ht = h.reshape(t, d)
    g_logits = (ht @ w_group + b_group).astype(jnp.float32)
    g_prob = jax.nn.softmax(g_logits, axis=-1)
    grp = jnp.argmax(g_logits, axis=-1)
    p_grp = jnp.take_along_axis(g_prob, grp[:, None], axis=1)[:, 0]
    e_logits = (ht @ w_router + b_router).astype(jnp.float32).reshape(t, N_GROUPS, EXPERTS_PER_GROUP)
    e_sel = jnp.take_along_axis(e_logits, grp[:, None, None], axis=1)[:, 0]
    top_v, top_i = lax.top_k(e_sel, TOP_K_INNER)
    gate = jax.nn.softmax(top_v, axis=-1) * p_grp[:, None]
    expert = grp[:, None] * EXPERTS_PER_GROUP + top_i

    n_assign = t * TOP_K_INNER
    e_flat = expert.reshape(-1)
    tok = jnp.repeat(jnp.arange(t, dtype=jnp.int32), TOP_K_INNER)
    wt = gate.reshape(-1)
    order = jnp.argsort(e_flat)
    e_sorted = e_flat[order]
    tok_sorted = tok[order]
    counts = jax.ops.segment_sum(jnp.ones((n_assign,), jnp.int32), e_flat, num_segments=N_EXPERTS)
    starts = jnp.cumsum(counts) - counts
    padded = ((counts + MOE_BLOCK - 1) // MOE_BLOCK) * MOE_BLOCK
    pad_ends = jnp.cumsum(padded)
    pad_starts = pad_ends - padded
    dest = pad_starts[e_sorted] + (jnp.arange(n_assign, dtype=jnp.int32) - starts[e_sorted])
    n_blocks = (n_assign + MOE_BLOCK - 1) // MOE_BLOCK + N_EXPERTS
    total = n_blocks * MOE_BLOCK
    x_pad = jnp.zeros((total, d), h.dtype).at[dest].set(ht[tok_sorted])
    block_start = jnp.arange(n_blocks, dtype=jnp.int32) * MOE_BLOCK
    block_expert = jnp.minimum(jnp.searchsorted(pad_ends, block_start, side='right'), N_EXPERTS - 1)

    def run_block(args):
        xb, e = args
        return (jax.nn.silu(xb @ w1[e]) * (xb @ w3[e])) @ w2[e]

    y_pad = lax.map(run_block, (x_pad.reshape(n_blocks, MOE_BLOCK, d), block_expert))
    y = y_pad.reshape(total, d)[dest] * wt[order][:, None].astype(h.dtype)
    out = jnp.zeros((t, d), h.dtype).at[tok_sorted].add(y.astype(h.dtype))
    return out.reshape(bsz, s, d)

def setup_inputs(seed: int = 0) -> dict:
    key = jax.random.key(seed)
    ks = jax.random.split(key, 24)
    f32 = jnp.float32
    nrm = lambda k, shape, scale: jax.random.normal(k, shape, f32) * scale
    return {
        "x": nrm(ks[0], (BATCH, SEQ, D_MODEL), 1.0),
        "c": nrm(ks[1], (BATCH, D_MODEL), 1.0),
        "w_ada": nrm(ks[2], (DEPTH, D_MODEL, 6 * D_MODEL), 0.5 * D_MODEL ** -0.5),
        "b_ada": nrm(ks[3], (DEPTH, 6 * D_MODEL), 0.02),
        "norm1_gain": 1.0 + nrm(ks[4], (DEPTH, D_MODEL), 0.02),
        "norm2_gain": 1.0 + nrm(ks[5], (DEPTH, D_MODEL), 0.02),
        "w_in": nrm(ks[6], (DEPTH, D_MODEL, P_IN), D_MODEL ** -0.5),
        "a_v_gain": 1.0 + nrm(ks[7], (DEPTH, A_WIDTH), 0.02),
        "a_w_s": nrm(ks[8], (DEPTH, A_HEADS, A_CHUNK, A_CHUNK), A_CHUNK ** -0.5),
        "a_b_s": 1.0 + nrm(ks[9], (DEPTH, A_HEADS, A_CHUNK), 0.02),
        "b_w_alpha": nrm(ks[10], (DEPTH, B_GATE_RANK, B_KEY_WIDTH), B_GATE_RANK ** -0.5),
        "b_b_alpha": nrm(ks[11], (DEPTH, B_KEY_WIDTH), 0.1),
        "b_out_gain": 1.0 + nrm(ks[12], (DEPTH, B_WIDTH), 0.02),
        "w_out": nrm(ks[13], (DEPTH, D_MIX, D_MODEL), D_MIX ** -0.5),
        "w_group": nrm(ks[14], (DEPTH, D_MODEL, N_GROUPS), D_MODEL ** -0.5),
        "b_group": nrm(ks[15], (DEPTH, N_GROUPS), 0.01),
        "w_router": nrm(ks[16], (DEPTH, D_MODEL, N_EXPERTS), D_MODEL ** -0.5),
        "b_router": nrm(ks[17], (DEPTH, N_EXPERTS), 0.01),
        "w1": nrm(ks[18], (DEPTH, N_EXPERTS, D_MODEL, D_EXPERT), D_MODEL ** -0.5),
        "w3": nrm(ks[19], (DEPTH, N_EXPERTS, D_MODEL, D_EXPERT), D_MODEL ** -0.5),
        "w2": nrm(ks[20], (DEPTH, N_EXPERTS, D_EXPERT, D_MODEL), D_EXPERT ** -0.5),
        "final_gain": 1.0 + nrm(ks[21], (D_MODEL,), 0.02),
    }

def reference(x, c, w_ada, b_ada, norm1_gain, norm2_gain, w_in, a_v_gain, a_w_s, a_b_s,
              b_w_alpha, b_b_alpha, b_out_gain, w_out, w_group, b_group, w_router, b_router,
              w1, w3, w2, final_gain):
    o = IN_OFFSETS
    c_act = jax.nn.silu(c)
    for l in range(DEPTH):
        mod = c_act @ w_ada[l] + b_ada[l]
        sh1, sc1, g1, sh2, sc2, g2 = [m[:, None, :] for m in jnp.split(mod, 6, axis=-1)]
        h = rms_norm(x, norm1_gain[l]) * (1.0 + sc1) + sh1
        proj = h @ w_in[l]
        a_u = jax.nn.gelu(proj[..., o[0]:o[1]])
        a_v = jax.nn.gelu(proj[..., o[1]:o[2]])
        y_a = sgu_mixer(a_u, a_v, a_v_gain[l], a_w_s[l], a_b_s[l])
        y_b = gla_mixer(proj[..., o[2]:o[3]], proj[..., o[3]:o[4]], proj[..., o[4]:o[5]],
                        proj[..., o[5]:o[6]], proj[..., o[6]:o[7]],
                        b_w_alpha[l], b_b_alpha[l], b_out_gain[l])
        mixed = jnp.concatenate([y_a, y_b], axis=-1) @ w_out[l]
        x = x + g1 * mixed
        h2 = rms_norm(x, norm2_gain[l]) * (1.0 + sc2) + sh2
        x = x + g2 * hier_moe(h2, w_group[l], b_group[l], w_router[l], b_router[l],
                              w1[l], w3[l], w2[l])
    return rms_norm(x, final_gain)


_drawn_inputs = setup_inputs


def setup_inputs(seed=0):
    import zlib

    import numpy as np

    out = dict(_drawn_inputs(seed))
    spreads = {}
    factors = {'norm1_gain': 5.885,
     'norm2_gain': 5.479,
     'a_v_gain': 8.0,
     'a_b_s': 8.0,
     'b_b_alpha': 6.322,
     'b_out_gain': 8.0,
     'b_group': 200.0,
     'b_router': 29.773,
     'final_gain': 21.064}
    for name, (base, spread) in spreads.items():
        noise = np.random.default_rng([zlib.crc32(name.encode()), seed]).standard_normal(out[name].shape)
        drawn = base * np.exp(spread * noise) if base else spread * noise
        out[name] = __import__('jax').numpy.asarray(drawn.astype(out[name].dtype))
    for name, factor in factors.items():
        out[name] = (out[name] * factor).astype(out[name].dtype)
    return out
```

```python
import concourse.bass as bass
from concourse import mybir
from contextlib import ExitStack

F32 = mybir.dt.float32
I32 = mybir.dt.int32
ACT = mybir.ActivationFunctionType
ALU = mybir.AluOpType
AX = mybir.AxisListType

P = 128
D = 1024
SEQ = 1024
NT = SEQ // P
KT = D // P
HALF = 512
AH = 4
BK = 64
RANK = 16
TAU = 16.0
C_U, C_AV, C_Q, C_K, C_V, C_R, C_A, P_IN = 0, 512, 1024, 1280, 1536, 2048, 2560, 2576
NG, EPG, NE = 4, 8, 32
FE = 512
FKT = FE // P
MAXEXTRA = 2 * SEQ // P
NBLK = NE + MAXEXTRA
EPS = 1e-6
NLOG = NG + NE
BIG = 1e30
(A_QI, A_KD, A_L64, A_L32, A_QD, A_KG) = range(6)


def trunk(nc, x, c, w_ada, b_ada, norm1_gain, norm2_gain, w_in, a_v_gain, a_w_s, a_b_s, b_w_alpha,
          b_b_alpha, b_out_gain, w_out, w_group, b_group, w_router, b_router, w1, w3, w2,
          final_gain, out):
    x1_dram = nc.dram_tensor("x1_scratch", (SEQ, D), F32, kind="Internal").ap()
    xn2_dram = nc.dram_tensor("xn2_scratch", (SEQ, D), F32, kind="Internal").ap()
    table_dram = nc.dram_tensor("slot_token_scratch", (NBLK * P, 1), F32, kind="Internal").ap()
    y_dram = nc.dram_tensor("expert_out_scratch", (NBLK * P, D), F32, kind="Internal").ap()

    ctx = ExitStack()
    with ctx:
        def sb(name, shape, dt=F32):
            return ctx.enter_context(nc.sbuf_tensor(name, shape, dt))

        def sem(name):
            return ctx.enter_context(nc.semaphore(name))

        big = sb("big", [P, KT * P_IN + KT * D])
        win = big[:, 0:KT * P_IN].rearrange("p (k n) -> p k n", k=KT)
        wout = big[:, KT * P_IN:KT * P_IN + KT * D].rearrange("p (k n) -> p k n", k=KT)
        ada_w = big[:, KT * P_IN:KT * P_IN + KT * D].rearrange("p (b k n) -> p b k n", b=2, k=KT)
        EW = KT * FE
        W1 = [big[:, (3 * b) * EW:(3 * b + 1) * EW].rearrange("p (k n) -> p k n", k=KT) for b in range(2)]
        W3 = [big[:, (3 * b + 1) * EW:(3 * b + 2) * EW].rearrange("p (k n) -> p k n", k=KT) for b in range(2)]
        W2 = [big[:, (3 * b + 2) * EW:(3 * b + 3) * EW].rearrange("p (k n) -> p k n", k=FKT) for b in range(2)]

        WORK = 17 * 1024
        work = sb("work", [P, WORK])
        at = [0]

        def carve(words):
            at[0] += words
            assert at[0] <= WORK, at[0]
            return work[:, at[0] - words:at[0]]

        xa = carve(D)
        xn = carve(D)
        xb = carve(D)
        hT = [carve(D).rearrange("p (k t) -> p k t", k=KT) for _ in range(2)]
        u_sb = carve(HALF)
        av_sb = carve(HALF)
        v_sb = carve(HALF)
        rg = carve(HALF)
        rtmp = carve(HALF)
        y_sb = carve(D)
        yT = carve(D).rearrange("p (k t) -> p k t", k=KT)
        xn2 = carve(D)
        h2T = yT
        qT = carve(2 * P).rearrange("p (c t) -> p c t", c=2)
        kT = carve(2 * P).rearrange("p (c t) -> p c t", c=2)
        az = carve(2 * P).rearrange("p (c t) -> p c t", c=2)
        zb = carve(2 * P).rearrange("p (c t) -> p c t", c=2)
        lneg = carve(2 * P).rearrange("p (c t) -> p c t", c=2)
        la = carve(2 * P).rearrange("p (c t) -> p c t", c=2)
        ex = carve(6 * 2 * P).rearrange("p (a c t) -> p a c t", a=6, c=2)
        pT = carve(AH * P).rearrange("p (h t) -> p h t", h=AH)
        pT4 = pT.rearrange("p (c l) t -> p c l t", c=2)
        kdT = carve(2 * P).rearrange("p (c k) -> p c k", c=2)
        state = carve(2 * 2 * P).rearrange("p (c v) -> p c v", c=2)
        stage = y_sb[0:1, :]
        stage2 = xn2[0:1, :]
        stages = [stage, stage2]
        brow = [xb[0:1, 0:HALF], xb[0:1, HALF:D]]
        at[0] = 0
        xr = [carve(D), carve(D)]
        xT = [carve(D).rearrange("p (k t) -> p k t", k=KT) for _ in range(2)]
        yb = [carve(D), carve(D)]
        silu_sb = carve(FE)
        hid = carve(FE)
        hidT = carve(FE).rearrange("p (k t) -> p k t", k=FKT)
        fx = carve(NT * D).rearrange("p (i n) -> p i n", i=NT)
        at[0] = 0
        fy1 = [carve(D), carve(D)]
        fy2 = [carve(D), carve(D)]
        fo = [carve(D), carve(D)]
        spare = [6 * EW]

        def route(*shape):
            words = 1
            for d in shape:
                words *= d
            spare[0] += words
            assert spare[0] <= KT * P_IN + KT * D
            v = big[:, spare[0] - words:spare[0]]
            if len(shape) == 2:
                v = v.rearrange("p (a b) -> p a b", a=shape[0])
            if len(shape) == 3:
                v = v.rearrange("p (a b c) -> p a b c", a=shape[0], b=shape[1])
            return v

        t4 = route(NT, NG)
        gs8 = route(NT)
        gm8 = route(NT)
        pg = route(NT)
        ohg = route(NT, NG)
        esel = route(NT, EPG)
        eprod = route(NT, NG, EPG)
        e2 = route(NT, EPG)
        t8 = route(NT, EPG)
        oh1 = route(NT, EPG)
        oh2 = route(NT, EPG)
        m1 = route(NT)
        m2 = route(NT)
        full1 = route(NT, NG, EPG)
        full2 = route(NT, NG, EPG)
        both = route(NT, NE)
        rank = route(NT, NE)
        rank2 = route(NT, NE)
        prev = route(NT, NE)
        count = route(NE)
        nex = route(NE)
        ebi = route(NE)
        base2 = route(NE)
        cmpx = route(NE, EPG)
        cmpj = route(MAXEXTRA, NE)
        sl = route(2, NT)
        exf = route(MAXEXTRA)
        rs_arg = route(NT)

        g1b = sb("gate1_rows", [P, D])
        g2b = sb("gate2_rows", [P, D])
        fgb = g1b
        vgb = sb("v_gain_rows", [P, HALF])
        ogb = sb("out_gain_rows", [P, HALF])
        wsT = sb("spatial_T", [P, AH, P])
        ws_raw = rtmp.rearrange("p (h s) -> p h s", h=AH)
        wal = sb("w_alpha", [RANK, 2 * P])
        alT = sb("a_low_T", [RANK, P])
        wr = sb("w_route", [P, KT, NLOG])
        brb = sb("b_route_rows", [P, NLOG])
        ident = sb("ident", [P, P])
        lstrict = sb("strict_before", [P, P])
        tri = sb("tri32", [P, 32])
        ones = sb("ones", [P, P])
        zeros = sb("zeros", [P, P])
        cT = sb("c_cols", [P, KT])
        cE = sb("c_exp", [P, KT])
        gain1 = sb("gain1", [P, KT])
        gain2 = sb("gain2", [P, KT])
        a1 = sb("a1", [P, KT])
        sh1 = sb("sh1", [P, KT])
        a2 = sb("a2", [P, KT])
        sh2 = sb("sh2", [P, KT])
        bal = sb("b_alpha_cols", [P, 2])
        bsT = sb("b_spatial_cols", [P, AH])
        eps = sb("eps", [P, 1])
        junk = sb("unused_squares", [P, D], mybir.dt.bfloat16)
        dec = sb("state_decay", [P, 2])
        ss1 = sb("ss1", [P, 1])
        rs1 = sb("rs1", [P, 1])
        ssv = sb("ssv", [P, 1])
        rsv = sb("rsv", [P, 1])
        sso = sb("sso", [P, AH])
        rso = sb("rso", [P, AH])
        ss2 = sb("ss2", [P, 1])
        rs2 = sb("rs2", [P, 1])
        lg = sb("logits", [P, NT, NLOG])
        iota4 = sb("iota4", [P, NT, NG])
        iota8 = sb("iota8", [P, NT, EPG])
        io4 = sb("io4", [P, NG], I32)
        io8 = sb("io8", [P, EPG], I32)
        ioj = sb("ioj", [P, MAXEXTRA], I32)
        iojf = sb("iojf", [P, MAXEXTRA])
        ioe = sb("ioe", [P, NE], I32)
        base1 = sb("base1", [P, NE])
        iok = sb("iok", [P, EPG], I32)
        thr = sb("thr", [P, EPG])
        toki = sb("token_id_i", [P, NT], I32)
        tokf = sb("token_id", [P, NT])
        gt1 = sb("gate_first", [P, NT])
        gt2 = sb("gate_second", [P, NT])
        sli = sb("slot_i", [P, 2, NT], I32)
        exi = sb("extra_expert", [P, MAXEXTRA], I32)
        nxi = sb("n_extra", [P, 1], I32)
        tbl = sb("table_rows", [NBLK, P])
        idx = sb("block_tokens", [P, NBLK], I32)
        idc = [sb("block_col0", [P, 1], I32), sb("block_col1", [P, 1], I32)]
        idp = sb("block_col_copy", [P, 1], I32)
        fss = sb("fss", [P, 1])
        frs = sb("frs", [P, 1])

        def bank(name):
            return ctx.enter_context(nc.psum_tensor(name, [P, HALF], F32))

        PJ0, PJ1, T0, T1, SC0, SC1, SC2, OB = [bank(n) for n in
                                              ("PJ0", "PJ1", "T0", "T1", "SC0", "SC1", "SC2", "OB")]
        T4 = [T0[:, :].rearrange("p (k t) -> p k t", k=4), T1[:, :].rearrange("p (k t) -> p k t", k=4)]
        S4 = [SC0[:, :].rearrange("p (k t) -> p k t", k=4), SC1[:, :].rearrange("p (k t) -> p k t", k=4)]
        QK = PJ0[:, :].rearrange("p (c t) -> p c t", c=4)
        ALOW = PJ1[0:RANK, 0:P]
        ZA = PJ1[:, P:3 * P].rearrange("p (c t) -> p c t", c=2)
        SCO = [a[:, :].rearrange("p (l c t) -> p l c t", l=2, c=2) for a in (SC0, SC1)]
        L64 = [a[0:64, 0:P].rearrange("p (c t) -> p c t", c=2) for a in (SC2, OB)]
        KDT = SC2[:, 256:512].rearrange("p (c k) -> p c k", c=2)
        COLS = SC0[:, 0:4 * KT]

        const_in = sem("const_in")
        norms_in = sem("norms_in")
        adaw_in = [sem("adaw_in0"), sem("adaw_in1")]
        win_in = sem("win_in")
        wout_in = sem("wout_in")
        consts_made = sem("consts_made")
        spatial_made = sem("spatial_made")
        cact_made = sem("cact_made")
        ada_mm = sem("ada_mm")
        ada_row = sem("ada_row")
        ada_spread = sem("ada_spread")
        ada_taken = sem("ada_taken")
        ws_mm = sem("ws_mm")
        xa_in = sem("xa_in")
        xb_in = sem("xb_in")
        rs1_made = sem("rs1_made")
        xn_made = sem("xn_made")
        xT_mm = sem("xT_mm")
        hT_made = sem("hT_made")
        qk_mm = sem("qk_mm")
        qk_ev = sem("qk_ev")
        alow_mm = sem("alow_mm")
        alow_ev = sem("alow_ev")
        za_mm = sem("za_mm")
        za_ev = sem("za_ev")
        ln_made = sem("ln_made")
        ex_args = sem("ex_args")
        ex_exp = sem("ex_exp")
        ex_made = sem("ex_made")
        sc_mm = sem("sc_mm")
        sc_off = sem("sc_off")
        sc_diag = sem("sc_diag")
        kdt_mm = sem("kdt_mm")
        kdt_ev = sem("kdt_ev")
        o_mm = sem("o_mm")
        st_mm = sem("st_mm")
        st_made = sem("st_made")
        sg_mm = sem("sg_mm")
        v_mm = sem("v_mm")
        v_ev = sem("v_ev")
        av_mm = sem("av_mm")
        av_ev = sem("av_ev")
        vn_made = sem("vn_made")
        rsv_made = sem("rsv_made")
        u_mm = sem("u_mm")
        u_ev = sem("u_ev")
        r_mm = sem("r_mm")
        r_exp = sem("r_exp")
        rg_made = sem("rg_made")
        rso_made = sem("rso_made")
        y_made = sem("y_made")
        yT_mm = sem("yT_mm")
        yT_ev = sem("yT_ev")
        mix_mm = sem("mix_mm")
        x1_made = sem("x1_made")
        rs2_made = sem("rs2_made")
        xn2_made = sem("xn2_made")
        x1_out = sem("x1_out")
        xn2_out = sem("xn2_out")
        h2T_mm = sem("h2T_mm")
        h2T_ev = sem("h2T_ev")
        lg_mm = sem("lg_mm")
        ob_free = sem("ob_free")
        dve_done = sem("dve_done")
        act_done = sem("act_done")
        pool_done = sem("pool_done")
        both_made = sem("both_made")
        rank_mm = sem("rank_mm")
        route_arg = sem("route_arg")
        route_exp = sem("route_exp")
        route_arg2 = sem("route_arg2")
        slots_made = sem("slots_made")
        table_zero = sem("table_zero")
        table_out = sem("table_out")
        table_in = sem("table_in")
        table_mm = sem("table_mm")
        idx_made = sem("idx_made")
        extra_made = sem("extra_made")
        w13_in = [sem("w13_in0"), sem("w13_in1")]
        w2_in = [sem("w2_in0"), sem("w2_in1")]
        idc_made = sem("idc_made")
        xg_in = [sem("xg_in0"), sem("xg_in1")]
        xg_mm = sem("xg_mm")
        xg_ev = sem("xg_ev")
        up_mm = sem("up_mm")
        silu_made = sem("silu_made")
        hid_made = sem("hid_made")
        hidT_mm = sem("hidT_mm")
        hidT_ev = sem("hidT_ev")
        dn_mm = sem("dn_mm")
        dn_ev = sem("dn_ev")
        y_zero = sem("y_zero")
        y_out = [sem("y_out0"), sem("y_out1")]
        fy_in = [sem("fy_in0"), sem("fy_in1")]
        fx_in = sem("fx_in")
        experts_left = sem("experts_left")
        fgb_in = sem("fgb_in")
        x2_made = sem("x2_made")
        frs_made = sem("frs_made")
        fo_made = sem("fo_made")
        out_out = [sem("out_out0"), sem("out_out1")]
        block = ctx.enter_context(nc.Block())

        class Chain:

            def __init__(self, eng, done):
                self.eng, self.done, self.base, self.n = eng, done, 0, 0

            def link(self, ins):
                self.n += 1
                ins.then_inc(self.done, 1)
                self.eng.wait_ge(self.done, self.base + self.n)

        N_CONST = 10
        DVE_STEP = 8
        ACT_STEP = 14

        @block.sync
        def _(sp):
            sp.dma_start(cT[:, :], c.rearrange("a (p k) -> (a p) k", k=KT)).then_inc(norms_in, 16)
            sp.dma_start(gain1[:, :], norm1_gain.rearrange("a (p k) -> (a p) k", k=KT)).then_inc(norms_in, 16)
            sp.dma_start(gain2[:, :], norm2_gain.rearrange("a (p k) -> (a p) k", k=KT)).then_inc(norms_in, 16)
            ada_v = w_ada[0, :, :].rearrange("(p k) n -> p k n", k=KT)
            for n in range(12):
                if n >= 2:
                    sp.wait_ge(ada_mm, n - 1)
                sp.dma_start(ada_w[:, n % 2, :, :], ada_v[:, :, n * HALF:(n + 1) * HALF]).then_inc(adaw_in[n % 2], 16)
                sp.dma_start(brow[n % 2], b_ada[0:1, n * HALF:(n + 1) * HALF]).then_inc(adaw_in[n % 2], 16)
                if n == 1:
                    sp.dma_start(xa[:, :], x[0, 0:P, :]).then_inc(xa_in, 16)
                    with nc.allow_non_contiguous_dma(reason="small constants"):
                        sp.dma_start(bal[:, :], b_b_alpha[0, :].rearrange("(c p) -> p c", p=P)).then_inc(const_in, 16)
                        sp.dma_start(bsT[:, :], a_b_s[0, :, :].rearrange("h t -> t h")).then_inc(const_in, 16)
                        sp.dma_start(wr[:, :, 0:NG], w_group[0, :, :].rearrange("(p k) n -> p k n", k=KT)).then_inc(const_in, 16)
                        sp.dma_start(wr[:, :, NG:NLOG], w_router[0, :, :].rearrange("(p k) n -> p k n", k=KT)).then_inc(const_in, 16)
                    sp.dma_start(wal[:, :], b_w_alpha[0, :, :]).then_inc(const_in, 16)
                    sp.dma_start(ws_raw[:, :, :], a_w_s[0, :, :, :].rearrange("h t s -> t h s")).then_inc(const_in, 16)
                    sp.dma_start(vgb[:, :], a_v_gain[0, :].partition_broadcast(P)).then_inc(const_in, 16)
                    sp.dma_start(ogb[:, :], b_out_gain[0, :].partition_broadcast(P)).then_inc(const_in, 16)
                    sp.dma_start(brb[:, 0:NG], b_group[0, :].partition_broadcast(P)).then_inc(const_in, 16)
                    sp.dma_start(brb[:, NG:NLOG], b_router[0, :].partition_broadcast(P)).then_inc(const_in, 16)
                if n == 5:
                    sp.dma_start(win, w_in[0, :, :].rearrange("(p k) n -> p k n", k=KT)).then_inc(win_in, 16)
            sp.wait_ge(ada_mm, 12)
            sp.dma_start(wout, w_out[0, :, :].rearrange("(p k) n -> p k n", k=KT)).then_inc(wout_in, 16)
            sp.dma_start(xb[:, :], x[0, 0:P, :]).then_inc(xb_in, 16)

            def load_xa(i):
                sp.wait_ge(xn_made, i)
                sp.dma_start(xa[:, :], x[0, bass.ts(i, P), :]).then_inc(xa_in, 16)

            def tile_out(i, more):
                sp.wait_ge(x1_made, i + 1)
                sp.dma_start(x1_dram[bass.ts(i, P), :], xb[:, :]).then_inc(x1_out, 16)
                sp.wait_ge(xn2_made, i + 1)
                sp.dma_start(xn2_dram[bass.ts(i, P), :], xn2[:, :]).then_inc(xn2_out, 16)
                if more:
                    sp.wait_ge(x1_out, 16 * (i + 1))
                    sp.dma_start(xb[:, :], x[0, bass.ts(i + 1, P), :]).then_inc(xb_in, 16)

            load_xa(1)
            sp.wait_ge(consts_made, 1)
            zero_src = zeros[:, :].rearrange("p (m n) -> p m n", m=1).broadcast_to([P, 4 * D // P, P])
            for j in range(MAXEXTRA // 4):
                dst = y_dram[(NE + 4 * j) * P:(NE + 4 * j + 4) * P, :]
                sp.dma_start(dst.rearrange("(p b) (m n) -> p (b m) n", p=P, n=P), zero_src).then_inc(y_zero, 16)
            with sp.Fori(0, NT - 2) as i:
                load_xa(i + 2)
                tile_out(i, True)
            tile_out(NT - 2, True)
            tile_out(NT - 1, False)

            def weights(b, r, par, e, first):
                if not first:
                    sp.wait_ge(up_mm, b - 1)
                sp.dma_start(W1[par], w1[0, e, :, :].rearrange("(p k) n -> p k n", k=KT)).then_inc(w13_in[par], 16)
                sp.dma_start(W3[par], w3[0, e, :, :].rearrange("(p k) n -> p k n", k=KT)).then_inc(w13_in[par], 16)
                if not first:
                    sp.wait_ge(dn_mm, b - 1)
                sp.dma_start(W2[par], w2[0, e, :, :].rearrange("(p k) n -> p k n", k=FKT)).then_inc(w2_in[par], 16)

            sp.wait_ge(mix_mm, NT)
            weights(0, 0, 0, 0, True)
            weights(1, 0, 1, 1, True)
            sp.wait_ge(x1_made, NT)
            sp.dma_start(fgb[:, :], final_gain.partition_broadcast(P)).then_inc(fgb_in, 16)
            sp.wait_ge(x1_out, 16 * NT)
            sp.wait_ge(xn2_out, 16 * NT)
            sp.wait_ge(ob_free, NT + 1)
            sp.dma_start(fx, x1_dram.rearrange("(i p) n -> p i n", p=P)).then_inc(fx_in, 16)
            sp.wait_ge(table_out, 16 * 2 * NT)
            sp.dma_start(tbl[:, :], table_dram.rearrange("(b p) a -> b (p a)", p=P)).then_inc(table_in, 16)
            with sp.Fori(1, NE // 2) as q:
                weights(2 * q, q, 0, 2 * q, False)
                weights(2 * q + 1, q, 1, 2 * q + 1, False)
            sp.wait_ge(extra_made, 1)
            n_extra = sp.value_load(nxi[0:1, 0:1], min_val=0, max_val=MAXEXTRA)
            with sp.Fori(0, MAXEXTRA // 2) as q:
                for par in range(2):
                    with sp.If(n_extra > 2 * q + par):
                        e = sp.value_load(exi[0:1, bass.ds(2 * q + par, 1)], min_val=0, max_val=NE - 1)
                        weights(2 * q + par + NE, q + NE // 2, par, e, False)
            sp.wait_ge(out_out[0], 16 * NT // 2)
            sp.wait_ge(out_out[1], 16 * NT // 2)

        @block.gpsimd
        def _(pool):
            g = nc.gpsimd
            chain = Chain(pool, pool_done)
            link = chain.link
            g.memset(eps[:, :], EPS)
            g.memset(state, 0.0)
            g.memset(pT, 0.0)
            g.memset(ones[:, :], 1.0)
            g.memset(zeros[:, :], 0.0)
            link(g.memset(ident[:, :], 1.0))
            link(g.affine_select(out=ident[:, :], in_=ident[:, :], compare_op=ALU.is_equal, fill=0.0,
                                 base=0, pattern=[[-1, P]], channel_multiplier=1))
            link(g.affine_select(out=lstrict[:, :], in_=ones[:, :], compare_op=ALU.is_gt, fill=0.0,
                                 base=0, pattern=[[1, P]], channel_multiplier=-1))
            for j in range(4):
                link(g.affine_select(out=tri[32 * j:32 * j + 32, :], in_=ones[32 * j:32 * j + 32, 0:32],
                                     compare_op=ALU.is_ge, fill=0.0, base=0, pattern=[[1, 32]],
                                     channel_multiplier=-1))
            g.iota(io4[:, :], [[1, NG]], 0, 0)
            g.iota(io8[:, :], [[1, EPG]], 0, 0)
            g.iota(ioj[:, :], [[1, MAXEXTRA]], 0, 0)
            g.iota(ioe[:, :], [[P, NE]], 0, 0)
            g.iota(iok[:, :], [[P, EPG]], P, 0)
            g.iota(toki[:, :], [[P, NT]], 0, 1).then_inc(consts_made, 1)
            pool.wait_ge(const_in, 16 * N_CONST)
            g.affine_select(out=ws_raw, in_=ws_raw, compare_op=ALU.is_ge, fill=0.0, base=0,
                            pattern=[[0, AH], [-1, P]], channel_multiplier=1).then_inc(spatial_made, 1)
            link(g.memset(tbl[:, :], 0.0))
            pool.dma_start(table_dram.rearrange("(b p) a -> b (p a)", p=P), tbl[:, :]).then_inc(table_zero, 16)
            pool.wait_ge(table_zero, 16)
            pool.wait_ge(slots_made, 1)
            for i in range(NT):
                for j in range(2):
                    pool.indirect_dma_start(out=table_dram, out_offset=bass.IndirectOffsetOnAxis(
                        ap=sli[:, j, i:i + 1], axis=0), in_=tokf[:, i:i + 1], in_offset=None).then_inc(table_out, 16)

            def gather(b, r, par, first):
                if not first:
                    pool.wait_ge(xg_mm, b - 1)
                    pool.wait_ge(xg_in[par], 16 * r)
                g.tensor_copy(idc[par][:, :], idx[:, bass.ds(b, 1)]).then_inc(idc_made, 1)
                pool.wait_ge(idc_made, b + 1)
                g.tensor_tensor(idp[:, :], idc[par][:, :], idc[par][:, :], ALU.add)
                pool.indirect_dma_start(out=xr[par], out_offset=None, in_=xn2_dram,
                                        in_offset=bass.IndirectOffsetOnAxis(ap=idc[par][:, 0:1], axis=0)
                                        ).then_inc(xg_in[par], 16)

            pool.wait_ge(idx_made, 1)
            pool.wait_ge(xn2_out, 16 * NT)
            gather(0, 0, 0, True)
            gather(1, 0, 1, True)
            with pool.Fori(1, NE // 2) as q:
                gather(2 * q, q, 0, False)
                gather(2 * q + 1, q, 1, False)
            pool.wait_ge(extra_made, 1)
            n_extra = pool.value_load(nxi[0:1, 0:1], min_val=0, max_val=MAXEXTRA)
            with pool.Fori(0, MAXEXTRA // 2) as q:
                for par in range(2):
                    with pool.If(n_extra > 2 * q + par):
                        gather(2 * q + par + NE, q + NE // 2, par, False)
            pool.wait_ge(experts_left, 3)
            for i in range(NT):
                if i >= 2:
                    pool.wait_ge(fo_made, i - 1)
                for j, dst in enumerate((fy1, fy2)):
                    pool.indirect_dma_start(out=dst[i % 2], out_offset=None, in_=y_dram,
                                            in_offset=bass.IndirectOffsetOnAxis(ap=sli[:, j, i:i + 1], axis=0)
                                            ).then_inc(fy_in[i % 2], 16)

        @block.tensor
        def _(pe):
            mm = nc.tensor.matmul
            tp = nc.tensor.transpose
            pe.wait_ge(consts_made, 1)
            pe.wait_ge(cact_made, 1)

            def spread(v):
                pe.wait_ge(ada_row, 2 * (v + 1))
                st = stages[v % 2]
                if v:
                    pe.wait_ge(ada_taken, v)
                if v in (2, 5):
                    mm(T0[:, :], ones[0:1, :], st[:, 0:HALF], start=True, stop=True)
                    mm(T1[:, :], ones[0:1, :], st[:, HALF:D], start=True, stop=True).then_inc(ada_spread, 1)
                else:
                    slot = {0: 0, 1: 1, 3: 2, 4: 3}[v]
                    cols = st.rearrange("a (p k) -> a k p", k=KT)
                    for k in range(KT):
                        last = mm(COLS[:, slot * KT + k:slot * KT + k + 1], cols[:, k, :], ones[0:1, 0:1],
                                  start=True, stop=True)
                    last.then_inc(ada_spread, 1)

            for n in range(12):
                pe.wait_ge(adaw_in[n % 2], 32 * (n // 2 + 1))
                acc = (PJ0, PJ1)[n % 2]
                if n >= 2:
                    pe.wait_ge(ada_row, n - 1)
                for k in range(KT):
                    mm(acc[0:1, :], cT[:, k:k + 1], ada_w[:, n % 2, k, :], start=(k == 0), stop=False)
                mm(acc[0:1, :], ones[0:1, 0:1], brow[n % 2], start=False, stop=True).then_inc(ada_mm, 1)
                if n % 2 == 0 and n >= 2:
                    spread(n // 2 - 1)
            spread(5)
            pe.wait_ge(spatial_made, 1)
            for h in range(AH):
                last = tp(OB[:, h * P:(h + 1) * P], ws_raw[:, h, :], ident[:, :])
            last.then_inc(ws_mm, 1)

            def x_transposes(i, first):
                pe.wait_ge(xn_made, i + 1)
                if not first:
                    pe.wait_ge(yT_ev, i - 1)
                cols = xn.rearrange("p (m k) -> p k m", k=KT)
                for k in range(KT):
                    last = tp(T4[k // 4][:, k % 4, :], cols[:, k, :], ident[:, :])
                last.then_inc(xT_mm, 1)

            def project(acc, c0, hTs):
                for k in range(KT):
                    last = mm(acc[:, :], hTs[:, k, :], win[:, k, c0:c0 + HALF], start=(k == 0), stop=(k == KT - 1))
                return last

            def step(s, par, first=False, head=True, tail=True, nxt=True):
                hTs = hT[par]
                if head:
                    pe.wait_ge(hT_made, s + 1)
                    if not first:
                        pe.wait_ge(u_ev, s)
                    for m in range(4):
                        for k in range(KT):
                            last = mm(QK[:, m, :], win[:, k, C_Q + m * P:C_Q + (m + 1) * P], hTs[:, k, :],
                                      start=(k == 0), stop=(k == KT - 1))
                    last.then_inc(qk_mm, 1)
                    if not first:
                        pe.wait_ge(rg_made, s)
                    for k in range(KT):
                        last = mm(ALOW, win[:, k, C_A:P_IN], hTs[:, k, :], start=(k == 0), stop=(k == KT - 1))
                    last.then_inc(alow_mm, 1)
                if tail:
                    pe.wait_ge(ex_made, s)
                    pe.wait_ge(ob_free, s)
                    for cc in range(2):
                        for half in range(2):
                            rows = slice(64 * half, 64 * half + 64)
                            mm(SCO[half][:, 0, cc, :], ex[rows, A_KG, cc, :], ex[rows, A_QD, cc, :], start=True,
                               stop=True)
                            mm(SCO[half][:, 1, cc, :], ex[rows, A_L32, cc, :], ex[rows, A_L32, cc, :], start=True,
                               stop=True)
                            last = mm(L64[half][:, cc, :], ex[rows, A_L64, cc, 0:64], ex[rows, A_L64, cc, 64:P],
                                      start=True, stop=True)
                    last.then_inc(sc_mm, 1)
                if head:
                    pe.wait_ge(qk_ev, s + 1)
                    project(PJ0, C_V, hTs).then_inc(v_mm, 1)
                    pe.wait_ge(alow_ev, s + 1)
                    for cc in range(2):
                        last = mm(ZA[:, cc, :], wal[:, cc * P:(cc + 1) * P], alT[:, :], start=True, stop=True)
                    last.then_inc(za_mm, 1)
                if tail:
                    pe.wait_ge(sc_off, s)
                    for cc in range(2):
                        last = tp(KDT[:, cc, :], ex[:, A_KD, cc, :], ident[:, :])
                    last.then_inc(kdt_mm, 1)
                    pe.wait_ge(sc_diag, s)
                    pe.wait_ge(st_made, s)
                    for cc in range(2):
                        mm(OB[:, 256 * cc:256 * cc + 256], ex[:, A_QI, cc, :], state[:, cc, :], start=(cc == 0),
                           stop=False)
                    for h in range(AH):
                        last = mm(OB[:, h * P:(h + 1) * P], pT[:, h, :], v_sb[:, h * P:(h + 1) * P], start=False,
                                  stop=(h == AH - 1))
                    last.then_inc(o_mm, 1)
                    pe.wait_ge(kdt_ev, s)
                    for cc in range(2):
                        last = mm(SC1[:, 256 * cc:256 * cc + 256], kdT[:, cc, :], v_sb[:, 256 * cc:256 * cc + 256],
                                  start=True, stop=True)
                    last.then_inc(st_mm, 1)
                    pe.wait_ge(vn_made, s)
                    for h in range(AH):
                        last = mm(SC0[:, h * P:(h + 1) * P], wsT[:, h, :], av_sb[:, h * P:(h + 1) * P], start=True,
                                  stop=True)
                    last.then_inc(sg_mm, 1)
                if head:
                    pe.wait_ge(za_ev, s + 1)
                    project(PJ1, C_AV, hTs).then_inc(av_mm, 1)
                if tail:
                    pe.wait_ge(y_made, s)
                    cols = y_sb.rearrange("p (m k) -> p k m", k=KT)
                    for k in range(KT):
                        last = tp(T4[k // 4][:, k % 4, :], cols[:, k, :], ident[:, :])
                    last.then_inc(yT_mm, 1)
                if head:
                    pe.wait_ge(v_ev, s + 1)
                    project(PJ0, C_U, hTs).then_inc(u_mm, 1)
                if tail:
                    pe.wait_ge(yT_ev, s)
                    pe.wait_ge(st_made, s + 1)
                    for hf in range(2):
                        for k in range(KT):
                            last = mm((SC0, SC1)[hf][:, :], yT[:, k, :], wout[:, k, hf * HALF:(hf + 1) * HALF],
                                      start=(k == 0), stop=(k == KT - 1))
                    last.then_inc(mix_mm, 1)
                if nxt:
                    x_transposes(s + 1, first)
                if head:
                    pe.wait_ge(av_ev, s + 1)
                    project(PJ1, C_R, hTs).then_inc(r_mm, 1)
                if tail:
                    pe.wait_ge(xn2_made, s)
                    cols = xn2.rearrange("p (m k) -> p k m", k=KT)
                    for k in range(KT):
                        last = tp(S4[k // 4][:, k % 4, :], cols[:, k, :], ident[:, :])
                    last.then_inc(h2T_mm, 1)
                    pe.wait_ge(h2T_ev, s)
                    for k in range(KT):
                        last = mm(OB[:, 0:NLOG], h2T[:, k, :], wr[:, k, :], start=(k == 0), stop=(k == KT - 1))
                    last.then_inc(lg_mm, 1)

            pe.wait_ge(ada_taken, 6)
            x_transposes(0, True)
            pe.wait_ge(win_in, 16)
            step(0, 0, first=True, tail=False)
            pe.wait_ge(wout_in, 16)
            with pe.Fori(0, (NT - 2) // 2) as j:
                step(2 * j + 1, 1)
                step(2 * j + 2, 0)
            step(NT - 1, (NT - 1) % 2, nxt=False)
            step(NT, 0, head=False, nxt=False)

            pe.wait_ge(both_made, 1)
            bothf = both.rearrange("p a b -> p (a b)")
            mm(SC0[:, 0:NT * NE], lstrict[:, :], bothf, start=True, stop=True)
            mm(SC1[:, 0:NT * NE], ones[:, :], bothf, start=True, stop=True).then_inc(rank_mm, 1)
            pe.wait_ge(table_in, 16)
            tp(SC2[:, 0:NBLK], tbl[:, :], ident[0:NBLK, 0:NBLK]).then_inc(table_mm, 1)

            def row_transposes(b, r, par, first=False):
                pe.wait_ge(xg_in[par], 16 * (r + 1))
                if not first:
                    pe.wait_ge(xg_ev, b)
                cols = xr[par].rearrange("p (m k) -> p k m", k=KT)
                for k in range(KT):
                    last = tp(T4[k // 4][:, k % 4, :], cols[:, k, :], ident[:, :])
                last.then_inc(xg_mm, 1)

            def up(b, r, par, first=False):
                pe.wait_ge(xg_ev, b + 1)
                pe.wait_ge(w13_in[par], 32 * (r + 1))
                if not first:
                    pe.wait_ge(hid_made, b)
                for acc, w in ((PJ0, W1[par]), (PJ1, W3[par])):
                    for k in range(KT):
                        last = mm(acc[:, :], xT[par][:, k, :], w[:, k, :], start=(k == 0), stop=(k == KT - 1))
                last.then_inc(up_mm, 1)

            def hidden_transposes(b, r, par):
                pe.wait_ge(hid_made, b + 1)
                cols = hid.rearrange("p (m k) -> p k m", k=FKT)
                for k in range(FKT):
                    last = tp(SC2[:, k * P:(k + 1) * P], cols[:, k, :], ident[:, :])
                last.then_inc(hidT_mm, 1)

            def down(b, r, par, first=False):
                pe.wait_ge(hidT_ev, b + 1)
                pe.wait_ge(w2_in[par], 16 * (r + 1))
                if not first:
                    pe.wait_ge(dn_ev, b)
                for hf in range(2):
                    for k in range(FKT):
                        last = mm((SC0, SC1)[hf][:, :], hidT[:, k, :], W2[par][:, k, hf * HALF:(hf + 1) * HALF],
                                  start=(k == 0), stop=(k == FKT - 1))
                last.then_inc(dn_mm, 1)

            pe.wait_ge(idx_made, 1)
            row_transposes(0, 0, 0, True)
            up(0, 0, 0, True)
            row_transposes(1, 0, 1)
            hidden_transposes(0, 0, 0)

            def block_step(b, r, par, first=False, nxt=True):
                up(b, r, par)
                if nxt:
                    row_transposes(b + 1, r + par, 1 - par)
                down(b - 1, r - 1 + par, 1 - par, first)
                hidden_transposes(b, r, par)

            block_step(1, 0, 1, first=True)
            with pe.Fori(1, NE // 2 - 1) as q:
                block_step(2 * q, q, 0)
                block_step(2 * q + 1, q, 1)
            block_step(NE - 2, NE // 2 - 1, 0)
            block_step(NE - 1, NE // 2 - 1, 1, nxt=False)
            down(NE - 1, NE // 2 - 1, 1)
            pe.wait_ge(extra_made, 1)
            n_extra = pe.value_load(nxi[0:1, 0:1], min_val=0, max_val=MAXEXTRA)
            with pe.Fori(0, MAXEXTRA // 2) as q:
                for par in range(2):
                    with pe.If(n_extra > 2 * q + par):
                        b, r = 2 * q + par + NE, q + NE // 2
                        row_transposes(b, r, par)
                        up(b, r, par)
                        hidden_transposes(b, r, par)
                        down(b, r, par)
            pe.nop().then_inc(experts_left, 1)

        @block.scalar
        def _(act):
            f = nc.scalar.activation
            chain = Chain(act, act_done)
            link = chain.link

            def rstd(ss, rs, width):
                link(f(rs, ss, ACT.Ln, bias=eps[:, :], scale=1.0 / width))
                return f(rs, rs, ACT.Exp, scale=-0.5)

            act.wait_ge(norms_in, 48)
            act.wait_ge(consts_made, 1)
            f(cE[:, :], cT[:, :], ACT.Exp, scale=-1.0).then_inc(act_done, 1)
            chain.n += 1
            for n in range(12):
                act.wait_ge(ada_mm, n + 1)
                v = n // 2
                if v >= 2 and n % 2 == 0:
                    act.wait_ge(ada_spread, v - 1)
                f(stages[v % 2][:, (n % 2) * HALF:(n % 2 + 1) * HALF], (PJ0, PJ1)[n % 2][0:1, :],
                  ACT.Copy).then_inc(ada_row, 1)
            act.wait_ge(ws_mm, 1)
            f(wsT[:, :, :].rearrange("p h t -> p (h t)"), OB[:, :], ACT.Copy).then_inc(ob_free, 1)

            def x_norm(i):
                act.wait_ge(xa_in, 16 * (i + 1))
                link(f(junk[:, :], xa, ACT.Square, accum_out=ss1[:, :]))
                rstd(ss1[:, :], rs1[:, :], D).then_inc(rs1_made, 1)

            def step(s, first=False, head=True, tail=True, nxt=True):
                if head:
                    act.wait_ge(qk_mm, s + 1)
                    if not first:
                        act.wait_ge(ex_made, s)
                    f(qT, QK[:, 0:2, :], ACT.Copy, scale=BK ** -0.5)
                    f(kT, QK[:, 2:4, :], ACT.Copy).then_inc(qk_ev, 1)
                    act.wait_ge(alow_mm, s + 1)
                    f(alT[:, :], ALOW, ACT.Copy).then_inc(alow_ev, 1)
                if tail:
                    act.wait_ge(sc_diag, s)
                    for half in range(2):
                        f(pT4[0:64, :, half, 64:P], L64[half], ACT.Copy)
                        f(pT4[0:32, :, half, 32:64], SCO[half][0:32, 1, :, 32:64], ACT.Copy)
                        last = f(pT4[64:96, :, half, 96:P], SCO[half][64:96, 1, :, 96:P], ACT.Copy)
                    last.then_inc(sc_off, 1)
                    act.wait_ge(kdt_mm, s)
                    f(kdT, KDT, ACT.Copy).then_inc(kdt_ev, 1)
                if head:
                    act.wait_ge(za_mm, s + 1)
                    for cc in range(2):
                        last = f(zb[:, cc, :], ZA[:, cc, :], ACT.Identity, bias=bal[:, cc:cc + 1])
                    last.then_inc(za_ev, 1)
                    act.wait_ge(za_ev, s + 1)
                    link(f(az, zb, ACT.Abs))
                    link(f(az, az, ACT.Exp, scale=-1.0))
                    f(lneg, az, ACT.Ln, bias=1.0).then_inc(ln_made, 1)
                if tail:
                    act.wait_ge(o_mm, s)
                    for h in range(AH):
                        link(f(junk[:, 0:P], OB[:, h * P:(h + 1) * P], ACT.Square, accum_out=sso[:, h:h + 1]))
                    rstd(sso[:, :], rso[:, :], P).then_inc(rso_made, 1)
                if head:
                    act.wait_ge(ex_args, s + 1)
                    f(ex, ex, ACT.Exp, scale=1.0 / TAU).then_inc(ex_exp, 1)
                    act.wait_ge(av_mm, s + 1)
                    if not first:
                        act.wait_ge(sg_mm, s)
                    f(av_sb, PJ1[:, :], ACT.Copy).then_inc(av_ev, 1)
                if tail:
                    act.wait_ge(yT_mm, s)
                    f(yT[:, 0:4, :], T4[0], ACT.Copy)
                    f(yT[:, 4:8, :], T4[1], ACT.Copy).then_inc(yT_ev, 1)
                if nxt:
                    x_norm(s + 1)
                if head:
                    act.wait_ge(u_mm, s + 1)
                    if not first:
                        act.wait_ge(y_made, s)
                    f(u_sb, PJ0[:, :], ACT.Gelu_apprx_tanh).then_inc(u_ev, 1)
                    act.wait_ge(av_ev, s + 1)
                    link(f(av_sb, av_sb, ACT.Gelu_apprx_tanh))
                    link(f(junk[:, 0:HALF], av_sb, ACT.Square, accum_out=ssv[:, :]))
                    rstd(ssv[:, :], rsv[:, :], HALF).then_inc(rsv_made, 1)
                if tail:
                    act.wait_ge(x1_made, s)
                    link(f(junk[:, :], xb, ACT.Square, accum_out=ss2[:, :]))
                    rstd(ss2[:, :], rs2[:, :], D).then_inc(rs2_made, 1)
                if head:
                    act.wait_ge(r_mm, s + 1)
                    if not first:
                        act.wait_ge(rg_made, s)
                    f(rtmp, PJ1[:, :], ACT.Exp, scale=-1.0).then_inc(r_exp, 1)

            x_norm(0)
            step(0, first=True, tail=False)
            with act.Fori(0, (NT - 2) // 2) as j:
                n0 = chain.base + chain.n
                chain.base, chain.n = n0 + 2 * ACT_STEP * j, 0
                step(2 * j + 1)
                assert chain.n == ACT_STEP, ("ACT_STEP", chain.n)
                chain.base, chain.n = n0 + ACT_STEP + 2 * ACT_STEP * j, 0
                step(2 * j + 2)
            chain.base, chain.n = n0 + (NT - 2) * ACT_STEP, 0
            step(NT - 1, nxt=False)
            step(NT, head=False, nxt=False)

            act.wait_ge(route_arg, 1)
            f(t4, t4, ACT.Exp).then_inc(route_exp, 1)
            act.wait_ge(route_arg, 2)
            f(rs_arg, rs_arg, ACT.Exp).then_inc(route_exp, 1)

            def silu(b, first=False):
                act.wait_ge(up_mm, b + 1)
                if not first:
                    act.wait_ge(hid_made, b)
                f(silu_sb, PJ0[:, :], ACT.Silu).then_inc(silu_made, 1)

            def store(b, r, par, first=False):
                act.wait_ge(dn_mm, b + 1)
                if not first:
                    act.wait_ge(y_out[par], 16 * r)
                f(yb[par][:, 0:HALF], SC0[:, :], ACT.Copy)
                f(yb[par][:, HALF:D], SC1[:, :], ACT.Copy).then_inc(dn_ev, 1)
                act.wait_ge(dn_ev, b + 1)
                act.dma_start(y_dram[bass.ts(b, P), :], yb[par]).then_inc(y_out[par], 16)

            silu(0, True)
            silu(1)
            store(0, 0, 0, True)
            silu(2)
            store(1, 0, 1, True)
            with act.Fori(1, NE // 2 - 1) as q:
                silu(2 * q + 1)
                store(2 * q, q, 0)
                silu(2 * q + 2)
                store(2 * q + 1, q, 1)
            silu(NE - 1)
            store(NE - 2, NE // 2 - 1, 0)
            store(NE - 1, NE // 2 - 1, 1)
            act.wait_ge(extra_made, 1)
            act.wait_ge(y_zero, 16 * (MAXEXTRA // 4))
            n_extra = act.value_load(nxi[0:1, 0:1], min_val=0, max_val=MAXEXTRA)
            with act.Fori(0, MAXEXTRA // 2) as q:
                for par in range(2):
                    with act.If(n_extra > 2 * q + par):
                        b, r = 2 * q + par + NE, q + NE // 2
                        silu(b)
                        store(b, r, par)
                        act.wait_ge(y_out[par], 16 * (r + 1))
                        f(ssv[:, :], eps[:, :], ACT.Copy)
            for par in range(2):
                act.wait_ge(y_out[par], 16 * NE // 2)
            act.nop().then_inc(experts_left, 1)

            def store_out(i):
                act.wait_ge(fo_made, i + 1)
                act.dma_start(out[0, i * P:(i + 1) * P, :], fo[i % 2]).then_inc(out_out[i % 2], 16)

            for i in range(NT):
                act.wait_ge(x2_made, i + 1)
                link(f(junk[:, :], fy1[i % 2], ACT.Square, accum_out=fss[:, :]))
                if i:
                    act.wait_ge(fo_made, i)
                rstd(fss[:, :], frs[:, :], D).then_inc(frs_made, 1)
                if i:
                    store_out(i - 1)
            store_out(NT - 1)

        @block.vector
        def _(dve):
            v = nc.vector
            tt, ts, stt, cp = v.tensor_tensor, v.tensor_scalar, v.scalar_tensor_tensor, v.tensor_copy
            chain = Chain(dve, dve_done)
            link = chain.link

            dve.wait_ge(act_done, 1)
            link(ts(cE[:, :], cE[:, :], 1.0, None, ALU.add))
            link(v.reciprocal(cE[:, :], cE[:, :]))
            tt(cT[:, :], cT[:, :], cE[:, :], ALU.mult).then_inc(cact_made, 1)
            for vec in range(6):
                dve.wait_ge(ada_spread, vec + 1)
                if vec == 0:
                    last = cp(sh1[:, :], COLS[:, 0:KT])
                if vec == 1:
                    last = stt(a1[:, :], COLS[:, KT:2 * KT], 1.0, gain1[:, :], ALU.add, ALU.mult)
                if vec == 3:
                    last = cp(sh2[:, :], COLS[:, 2 * KT:3 * KT])
                if vec == 4:
                    last = stt(a2[:, :], COLS[:, 3 * KT:4 * KT], 1.0, gain2[:, :], ALU.add, ALU.mult)
                if vec in (2, 5):
                    gb = g1b if vec == 2 else g2b
                    cp(gb[:, 0:HALF], T0[:, :])
                    last = cp(gb[:, HALF:D], T1[:, :])
                last.then_inc(ada_taken, 1)
            dve.wait_ge(consts_made, 1)
            cp(iojf[:, :], ioj[:, :])
            cp(base1[:, :], ioe[:, :])
            cp(thr[:, :], iok[:, :])
            cp(tokf[:, :], toki[:, :])
            for i in range(NT):
                cp(iota4[:, i, :], io4[:, :])
                cp(iota8[:, i, :], io8[:, :])
            dve.wait_ge(const_in, 16 * N_CONST)
            link(v.memset(dec[:, :], 1.0))

            def x_norm(i):
                dve.wait_ge(rs1_made, i + 1)
                dve.wait_ge(xa_in, 16 * (i + 1))
                ts(xn, xa, rs1[:, 0:1], None, ALU.mult).then_inc(xn_made, 1)

            def modulate_xT(i, par):
                dve.wait_ge(xT_mm, i + 1)
                for k in range(KT):
                    last = ts(hT[par][:, k, :], T4[k // 4][:, k % 4, :], a1[:, k:k + 1], sh1[:, k:k + 1],
                              ALU.mult, ALU.add)
                last.then_inc(hT_made, 1)

            B = ex[:, A_QI, :, :]

            def step(s, par, first=False, head=True, tail=True, nxt=True):
                if tail:
                    dve.wait_ge(sc_mm, s)
                    for j in range(4):
                        r = slice(32 * j, 32 * j + 32)
                        for half in range(2):
                            last = tt(pT4[r, :, half, r], SCO[half][r, 0, :, r],
                                      tri[r, :].rearrange("p (a t) -> p a t", a=1).broadcast_to([32, 2, 32]), ALU.mult)
                    last.then_inc(sc_diag, 1)
                if head:
                    dve.wait_ge(za_ev, s + 1)
                    link(ts(la, zb, 0.0, None, ALU.min))
                    dve.wait_ge(ln_made, s + 1)
                    link(tt(la, la, lneg, ALU.subtract))
                    if not first:
                        dve.wait_ge(o_mm, s)
                    for cc in range(2):
                        last = v.tensor_tensor_scan(B[:, cc, :], ones[:, :], la[:, cc, :], 0.0, ALU.mult, ALU.add)
                    link(last)
                    full = [P, 2, P]
                    tt(ex[:, A_KD, :, :], B[:, :, P - 1:P].broadcast_to(full), B, ALU.subtract)
                    tt(ex[:, A_L64, :, 64:P], B[:, :, 64:P], B[:, :, 63:64].broadcast_to([P, 2, 64]), ALU.subtract)
                    tt(ex[:, A_L64, :, 0:64], B[:, :, 63:64].broadcast_to([P, 2, 64]), B[:, :, 0:64], ALU.subtract)
                    b64 = B.rearrange("p c (j t) -> p c j t", j=2)
                    l32 = ex[:, A_L32, :, :].rearrange("p c (j t) -> p c j t", j=2)
                    mid = b64[:, :, :, 31:32].broadcast_to([P, 2, 2, 32])
                    tt(l32[:, :, :, 32:64], b64[:, :, :, 32:64], mid, ALU.subtract)
                    tt(l32[:, :, :, 0:32], mid, b64[:, :, :, 0:32], ALU.subtract)
                    b32 = B.rearrange("p c (j t) -> p (c j) t", j=4)
                    ref = b32[:, :, 15:16].broadcast_to([P, 8, 32])
                    tt(ex[:, A_QD, :, :].rearrange("p c (j t) -> p (c j) t", j=4), b32, ref, ALU.subtract)
                    tt(ex[:, A_KG, :, :].rearrange("p c (j t) -> p (c j) t", j=4), ref, b32,
                       ALU.subtract).then_inc(ex_args, 1)
                if tail:
                    dve.wait_ge(st_mm, s)
                    for h in range(AH):
                        r0, cc = 64 * (h % 2), h // 2
                        rows, cols = slice(r0, r0 + 64), slice((h % 2) * P, (h % 2 + 1) * P)
                        last = stt(state[rows, cc, cols], state[rows, cc, cols], dec[rows, cc:cc + 1],
                                   SC1[rows, 256 * cc + (h % 2) * P:256 * cc + (h % 2 + 1) * P], ALU.mult, ALU.add)
                    last.then_inc(st_made, 1)
                if head:
                    dve.wait_ge(v_mm, s + 1)
                    cp(v_sb, PJ0[:, :]).then_inc(v_ev, 1)
                if tail:
                    dve.wait_ge(sg_mm, s)
                    for h in range(AH):
                        c = slice(h * P, (h + 1) * P)
                        stt(y_sb[:, c], SC0[:, c], bsT[:, h:h + 1], u_sb[:, c], ALU.add, ALU.mult)
                    dve.wait_ge(rso_made, s)
                    for h in range(AH):
                        c = slice(h * P, (h + 1) * P)
                        last = stt(y_sb[:, HALF + h * P:HALF + (h + 1) * P], OB[:, c], rso[:, h:h + 1], rg[:, c],
                                   ALU.mult, ALU.mult)
                    last.then_inc(y_made, 1)
                if head:
                    dve.wait_ge(ex_exp, s + 1)
                    dve.wait_ge(qk_ev, s + 1)
                    if tail:
                        dve.wait_ge(st_made, s + 1)
                    link(cp(dec[:, :].rearrange("p (c a) -> p c a", a=1), B[:, :, P - 1:P]))
                    ex4 = [ex[:, a, :, :] for a in range(6)]
                    tt(ex4[A_QI], ex4[A_QI], qT, ALU.mult)
                    tt(ex4[A_KD], ex4[A_KD], kT, ALU.mult)
                    tt(ex4[A_L64][:, :, 64:P], ex4[A_L64][:, :, 64:P], qT[:, :, 64:P], ALU.mult)
                    tt(ex4[A_L64][:, :, 0:64], ex4[A_L64][:, :, 0:64], kT[:, :, 0:64], ALU.mult)
                    q4, k4 = [a.rearrange("p c (j t) -> p c j t", j=2) for a in (qT, kT)]
                    tt(l32[:, :, :, 32:64], l32[:, :, :, 32:64], q4[:, :, :, 32:64], ALU.mult)
                    tt(l32[:, :, :, 0:32], l32[:, :, :, 0:32], k4[:, :, :, 0:32], ALU.mult)
                    tt(ex4[A_QD], ex4[A_QD], qT, ALU.mult)
                    tt(ex4[A_KG], ex4[A_KG], kT, ALU.mult).then_inc(ex_made, 1)
                if nxt:
                    dve.wait_ge(xT_mm, s + 1)
                    x_norm(s + 1)
                if tail:
                    dve.wait_ge(mix_mm, s)
                    dve.wait_ge(xb_in, 16 * s)
                    tt(y_sb[:, 0:HALF], SC0[:, :], g1b[:, 0:HALF], ALU.mult)
                    link(tt(y_sb[:, HALF:D], SC1[:, :], g1b[:, HALF:D], ALU.mult))
                    tt(xb, xb, y_sb, ALU.add).then_inc(x1_made, 1)
                if head:
                    dve.wait_ge(rsv_made, s + 1)
                    stt(av_sb, av_sb, rsv[:, 0:1], vgb[:, :], ALU.mult, ALU.mult).then_inc(vn_made, 1)
                if tail:
                    dve.wait_ge(rs2_made, s)
                    ts(xn2, xb, rs2[:, 0:1], None, ALU.mult).then_inc(xn2_made, 1)
                if nxt:
                    if not first:
                        dve.wait_ge(r_mm, s)
                    modulate_xT(s + 1, 1 - par)
                if tail:
                    dve.wait_ge(h2T_mm, s)
                    for k in range(KT):
                        last = ts(h2T[:, k, :], S4[k // 4][:, k % 4, :], a2[:, k:k + 1], sh2[:, k:k + 1],
                                  ALU.mult, ALU.add)
                    last.then_inc(h2T_ev, 1)
                if head:
                    dve.wait_ge(r_exp, s + 1)
                    link(ts(rtmp, rtmp, 1.0, None, ALU.add))
                    link(v.reciprocal(rtmp, rtmp))
                    link(tt(rtmp, rtmp, PJ1[:, :], ALU.mult))
                    tt(rg, rtmp, ogb[:, :], ALU.mult).then_inc(rg_made, 1)
                if tail:
                    dve.wait_ge(lg_mm, s)
                    tt(lg[:, bass.ds(s - 1, 1), :], OB[:, 0:NLOG].rearrange("p (a n) -> p a n", a=1),
                       brb[:, :].rearrange("p (a n) -> p a n", a=1), ALU.add).then_inc(ob_free, 1)
                    dve.wait_ge(xn2_out, 16 * s)

            x_norm(0)
            v.memset(frs[:, :], 0.0).then_inc(st_made, 1)
            modulate_xT(0, 0)
            step(0, 0, first=True, tail=False)
            with dve.Fori(0, (NT - 2) // 2) as j:
                n0 = chain.base + chain.n
                chain.base, chain.n = n0 + 2 * DVE_STEP * j, 0
                step(2 * j + 1, 1)
                assert chain.n == DVE_STEP, ("DVE_STEP", chain.n)
                chain.base, chain.n = n0 + DVE_STEP + 2 * DVE_STEP * j, 0
                step(2 * j + 2, 0)
            chain.base, chain.n = n0 + (NT - 2) * DVE_STEP, 0
            step(NT - 1, (NT - 1) % 2, nxt=False)
            step(NT, 0, head=False, nxt=False)

            def bc(a, n):
                return a.rearrange("p (i a) -> p i a", a=1).broadcast_to([P, NT, n])

            def first_max(vals, mx, oh, iota, tmp, n):
                link(v.tensor_reduce(mx, vals, AX.X, ALU.max))
                link(tt(tmp, vals, bc(mx, n), ALU.is_equal))
                link(stt(tmp, tmp, -64.0, iota, ALU.mult, ALU.add))
                link(v.tensor_reduce(gs8, tmp, AX.X, ALU.min))
                link(tt(oh, tmp, bc(gs8, n), ALU.is_equal))

            dve.wait_ge(ob_free, NT + 1)
            grp, exl = lg[:, :, 0:NG], lg[:, :, NG:NLOG].rearrange("p i (g e) -> p i g e", g=NG)
            first_max(grp, gm8, ohg, iota4[:, :, :], t4, NG)
            tt(t4, grp, bc(gm8, NG), ALU.subtract).then_inc(route_arg, 1)
            dve.wait_ge(route_arg, 1)
            for i in range(NT):
                last = tt(eprod[:, i, :, :], exl[:, i, :, :],
                          ohg[:, i, :].rearrange("p (g a) -> p g a", a=1).broadcast_to([P, NG, EPG]), ALU.mult)
            link(last)
            link(v.tensor_reduce(esel, eprod.rearrange("p i g e -> p i e g"), AX.X, ALU.add))
            first_max(esel, m1, oh1, iota8[:, :, :], t8, EPG)
            link(stt(e2, oh1, -BIG, esel, ALU.mult, ALU.add))
            first_max(e2, m2, oh2, iota8[:, :, :], t8, EPG)
            link(tt(t8, oh1, oh2, ALU.add))
            for i in range(NT):
                for oh, dst in ((oh1, full1), (oh2, full2), (t8, both.rearrange("p i (g e) -> p i g e", g=NG))):
                    last = tt(dst[:, i, :, :], ohg[:, i, :].rearrange("p (g a) -> p g a", a=1).broadcast_to([P, NG, EPG]),
                              oh[:, i, :].rearrange("p (a e) -> p a e", a=1).broadcast_to([P, NG, EPG]), ALU.mult)
            last.then_inc(both_made, 1)
            tt(rs_arg, m2, m1, ALU.subtract).then_inc(route_arg, 1)
            dve.wait_ge(route_exp, 1)
            link(v.tensor_reduce(pg, t4, AX.X, ALU.add))
            link(v.reciprocal(pg, pg))
            dve.wait_ge(route_exp, 2)
            link(ts(gt1[:, :], rs_arg, 1.0, None, ALU.add))
            link(v.reciprocal(gt1[:, :], gt1[:, :]))
            link(tt(gt1[:, :], gt1[:, :], pg, ALU.mult))
            tt(gt2[:, :], gt1[:, :], rs_arg, ALU.mult)
            dve.wait_ge(rank_mm, 1)
            tot = rank2
            cp(rank, SC0[:, 0:NT * NE].rearrange("p (i e) -> p i e", i=NT))
            cp(tot, SC1[:, 0:NT * NE].rearrange("p (i e) -> p i e", i=NT))
            link(v.memset(prev[:, 0, :], 0.0))
            for i in range(1, NT):
                link(tt(prev[:, i, :], prev[:, i - 1, :], tot[:, i - 1, :], ALU.add))
            link(tt(count, prev[:, NT - 1, :], tot[:, NT - 1, :], ALU.add))
            link(tt(rank, rank, prev, ALU.add))
            link(tt(cmpx, count.rearrange("p (e a) -> p e a", a=1).broadcast_to([P, NE, EPG]),
                    thr[:, :].rearrange("p (a k) -> p a k", a=1).broadcast_to([P, NE, EPG]), ALU.is_gt))
            link(v.tensor_reduce(nex, cmpx, AX.X, ALU.add))
            link(v.tensor_tensor_scan(ebi, ones[:, 0:NE], nex, 0.0, ALU.mult, ALU.add))
            link(tt(base2, ebi, nex, ALU.subtract))
            link(ts(base2, base2, float(P), float((NE - 1) * P), ALU.mult, ALU.add))
            link(tt(count, base1[:, :], base2, ALU.subtract))
            link(ts(prev, rank, float(P), None, ALU.is_lt))
            link(tt(prev, prev, count.rearrange("p (a e) -> p a e", a=1).broadcast_to([P, NT, NE]), ALU.mult))
            link(tt(rank, rank, prev, ALU.add))
            link(tt(rank, rank, base2.rearrange("p (a e) -> p a e", a=1).broadcast_to([P, NT, NE]), ALU.add))
            for j, full in enumerate((full1, full2)):
                link(tt(rank2, rank, full.rearrange("p i g e -> p i (g e)"), ALU.mult))
                link(v.tensor_reduce(sl[:, j, :], rank2, AX.X, ALU.add))
            cp(sli[:, :, :], sl).then_inc(slots_made, 1)
            link(tt(cmpj, iojf[:, :].rearrange("p (j a) -> p j a", a=1).broadcast_to([P, MAXEXTRA, NE]),
                    ebi.rearrange("p (a e) -> p a e", a=1).broadcast_to([P, MAXEXTRA, NE]), ALU.is_ge))
            link(v.tensor_reduce(exf, cmpj, AX.X, ALU.add))
            link(ts(exf, exf, float(NE - 1), None, ALU.min))
            cp(exi[:, :], exf)
            cp(nxi[:, :], ebi[:, NE - 1:NE]).then_inc(extra_made, 1)
            dve.wait_ge(table_mm, 1)
            cp(idx[:, :], SC2[:, 0:NBLK]).then_inc(idx_made, 1)

            def modulate_rows(b, par):
                dve.wait_ge(xg_mm, b + 1)
                for k in range(KT):
                    last = ts(xT[par][:, k, :], T4[k // 4][:, k % 4, :], a2[:, k:k + 1], sh2[:, k:k + 1],
                              ALU.mult, ALU.add)
                last.then_inc(xg_ev, 1)

            def hidden(b, first=False):
                dve.wait_ge(silu_made, b + 1)
                if not first:
                    dve.wait_ge(hidT_mm, b)
                tt(hid, silu_sb, PJ1[:, :], ALU.mult).then_inc(hid_made, 1)

            def hidden_T(b):
                dve.wait_ge(hidT_mm, b + 1)
                cp(hidT, SC2[:, :].rearrange("p (k t) -> p k t", k=FKT)).then_inc(hidT_ev, 1)

            modulate_rows(0, 0)
            hidden(0, True)
            modulate_rows(1, 1)
            hidden_T(0)

            def block_step(b, par, nxt=True):
                hidden(b)
                if nxt:
                    modulate_rows(b + 1, 1 - par)
                hidden_T(b)

            block_step(1, 1)
            with dve.Fori(1, NE // 2 - 1) as q:
                block_step(2 * q, 0)
                block_step(2 * q + 1, 1)
            block_step(NE - 2, 0)
            block_step(NE - 1, 1, nxt=False)
            dve.wait_ge(extra_made, 1)
            n_extra = dve.value_load(nxi[0:1, 0:1], min_val=0, max_val=MAXEXTRA)
            with dve.Fori(0, MAXEXTRA // 2) as q:
                for par in range(2):
                    with dve.If(n_extra > 2 * q + par):
                        b = 2 * q + par + NE
                        modulate_rows(b, par)
                        hidden(b)
                        hidden_T(b)
            dve.nop().then_inc(experts_left, 1)

            dve.wait_ge(fgb_in, 16)
            dve.wait_ge(fx_in, 16)

            def combine(i):
                dve.wait_ge(fy_in[i % 2], 32 * (i // 2 + 1))
                p1, p2 = fy1[i % 2], fy2[i % 2]
                link(ts(p1, p1, gt1[:, i:i + 1], None, ALU.mult))
                link(stt(p1, p2, gt2[:, i:i + 1], p1, ALU.mult, ALU.add))
                link(tt(p1, p1, g2b[:, :], ALU.mult))
                tt(p1, p1, fx[:, i, :], ALU.add).then_inc(x2_made, 1)

            def finish(i):
                dve.wait_ge(frs_made, i + 1)
                if i >= 2:
                    dve.wait_ge(out_out[i % 2], 16 * (i // 2))
                stt(fo[i % 2], fy1[i % 2], frs[:, 0:1], fgb[:, :], ALU.mult, ALU.mult).then_inc(fo_made, 1)

            combine(0)
            for i in range(NT):
                if i + 1 < NT:
                    combine(i + 1)
                finish(i)


_INS = ["x", "c", "w_ada", "b_ada", "norm1_gain", "norm2_gain", "w_in", "a_v_gain", "a_w_s", "a_b_s", "b_w_alpha",
        "b_b_alpha", "b_out_gain", "w_out", "w_group", "b_group", "w_router", "b_router", "w1", "w3", "w2",
        "final_gain"]


def kernel(**inputs):
    import numpy as np
    import concourse.bacc as bacc
    from concourse.bass_utils import run_bass_kernel_spmd

    nc = bacc.Bacc("TRN2", target_bir_lowering=False, num_devices=1)
    arrays, args = {}, []
    for name in _INS:
        a = np.ascontiguousarray(inputs[name])
        arrays[f"in_{name}"] = a
        args.append(nc.dram_tensor(f"in_{name}", a.shape, mybir.dt.from_np(a.dtype), kind="ExternalInput").ap())
    args.append(nc.dram_tensor("out_0", (1, SEQ, D), F32, kind="ExternalOutput").ap())
    trunk(nc, *args)
    result = run_bass_kernel_spmd(nc, [arrays], core_ids=[0])
    return result.results[0]["out_0"]
```

```python
import concourse.bass as bass
from concourse import mybir
from contextlib import ExitStack

F32 = mybir.dt.float32
I32 = mybir.dt.int32
ACT = mybir.ActivationFunctionType
ALU = mybir.AluOpType
AX = mybir.AxisListType

P = 128
D = 1024
SEQ = 1024
NT = SEQ // P
KT = D // P
HALF = 512
AH = 4
BK = 64
RANK = 16
TAU = 16.0
C_U, C_AV, C_Q, C_K, C_V, C_R, C_A, P_IN = 0, 512, 1024, 1280, 1536, 2048, 2560, 2576
NG, EPG, NE = 4, 8, 32
FE = 512
FKT = FE // P
MAXEXTRA = 2 * SEQ // P
NBLK = NE + MAXEXTRA
EPS = 1e-6
NLOG = NG + NE
BIG = 1e30
(A_QI, A_KD, A_L64, A_L32, A_QD, A_KG) = range(6)


def trunk(nc, x, c, w_ada, b_ada, norm1_gain, norm2_gain, w_in, a_v_gain, a_w_s, a_b_s, b_w_alpha,
          b_b_alpha, b_out_gain, w_out, w_group, b_group, w_router, b_router, w1, w3, w2,
          final_gain, out):
    x1_dram = nc.dram_tensor("x1_scratch", (SEQ, D), F32, kind="Internal").ap()
    xn2_dram = nc.dram_tensor("xn2_scratch", (SEQ, D), F32, kind="Internal").ap()
    table_dram = nc.dram_tensor("slot_token_scratch", (NBLK * P, 1), F32, kind="Internal").ap()
    y_dram = nc.dram_tensor("expert_out_scratch", (NBLK * P, D), F32, kind="Internal").ap()

    ctx = ExitStack()
    with ctx:
        def sb(name, shape, dt=F32):
            return ctx.enter_context(nc.sbuf_tensor(name, shape, dt))

        def sem(name):
            return ctx.enter_context(nc.semaphore(name))

        big = sb("big", [P, KT * P_IN + KT * D])
        win = big[:, 0:KT * P_IN].rearrange("p (k n) -> p k n", k=KT)
        wout = big[:, KT * P_IN:KT * P_IN + KT * D].rearrange("p (k n) -> p k n", k=KT)
        ada_w = big[:, KT * P_IN:KT * P_IN + KT * D].rearrange("p (b k n) -> p b k n", b=2, k=KT)
        EW = KT * FE
        W1 = [big[:, (3 * b) * EW:(3 * b + 1) * EW].rearrange("p (k n) -> p k n", k=KT) for b in range(2)]
        W3 = [big[:, (3 * b + 1) * EW:(3 * b + 2) * EW].rearrange("p (k n) -> p k n", k=KT) for b in range(2)]
        W2 = [big[:, (3 * b + 2) * EW:(3 * b + 3) * EW].rearrange("p (k n) -> p k n", k=FKT) for b in range(2)]

        WORK = 17 * 1024
        work = sb("work", [P, WORK])
        at = [0]

        def carve(words):
            at[0] += words
            assert at[0] <= WORK, at[0]
            return work[:, at[0] - words:at[0]]

        xa = carve(D)
        xn = carve(D)
        xb = carve(D)
        hT = [carve(D).rearrange("p (k t) -> p k t", k=KT) for _ in range(2)]
        u_sb = carve(HALF)
        av_sb = carve(HALF)
        v_sb = carve(HALF)
        rg = carve(HALF)
        rtmp = carve(HALF)
        y_sb = carve(D)
        yT = carve(D).rearrange("p (k t) -> p k t", k=KT)
        xn2 = carve(D)
        h2T = yT
        qT = carve(2 * P).rearrange("p (c t) -> p c t", c=2)
        kT = carve(2 * P).rearrange("p (c t) -> p c t", c=2)
        az = carve(2 * P).rearrange("p (c t) -> p c t", c=2)
        zb = carve(2 * P).rearrange("p (c t) -> p c t", c=2)
        lneg = carve(2 * P).rearrange("p (c t) -> p c t", c=2)
        la = carve(2 * P).rearrange("p (c t) -> p c t", c=2)
        ex = carve(6 * 2 * P).rearrange("p (a c t) -> p a c t", a=6, c=2)
        pT = carve(AH * P).rearrange("p (h t) -> p h t", h=AH)
        pT4 = pT.rearrange("p (c l) t -> p c l t", c=2)
        kdT = carve(2 * P).rearrange("p (c k) -> p c k", c=2)
        state = carve(2 * 2 * P).rearrange("p (c v) -> p c v", c=2)
        brow = yT.rearrange("p k t -> p (k t)")[0:1, :]
        at[0] = 0
        xr = [carve(D), carve(D)]
        xT = [carve(D).rearrange("p (k t) -> p k t", k=KT) for _ in range(2)]
        yb = [carve(D), carve(D)]
        silu_sb = carve(FE)
        hid = carve(FE)
        hidT = carve(FE).rearrange("p (k t) -> p k t", k=FKT)
        fx = carve(NT * D).rearrange("p (i n) -> p i n", i=NT)
        fy1 = [big[:, 2 * i * D:(2 * i + 1) * D] for i in range(NT)]
        fy2 = [big[:, (2 * i + 1) * D:(2 * i + 2) * D] for i in range(NT)]
        spare = [6 * EW]

        def route(*shape):
            words = 1
            for d in shape:
                words *= d
            spare[0] += words
            assert spare[0] <= KT * P_IN + KT * D
            v = big[:, spare[0] - words:spare[0]]
            if len(shape) == 2:
                v = v.rearrange("p (a b) -> p a b", a=shape[0])
            if len(shape) == 3:
                v = v.rearrange("p (a b c) -> p a b c", a=shape[0], b=shape[1])
            return v

        t4 = route(NT, NG)
        gs8 = route(NT)
        gm8 = route(NT)
        pg = route(NT)
        ohg = route(NT, NG)
        esel = route(NT, EPG)
        eprod = route(NT, NG, EPG)
        e2 = route(NT, EPG)
        t8 = route(NT, EPG)
        oh1 = route(NT, EPG)
        oh2 = route(NT, EPG)
        m1 = route(NT)
        m2 = route(NT)
        full1 = route(NT, NG, EPG)
        full2 = route(NT, NG, EPG)
        both = route(NT, NE)
        rank = route(NT, NE)
        rank2 = route(NT, NE)
        prev = route(NT, NE)
        count = route(NE)
        nex = route(NE)
        ebi = route(NE)
        base2 = route(NE)
        cmpx = route(NE, EPG)
        cmpj = route(MAXEXTRA, NE)
        sl = route(2, NT)
        exf = route(MAXEXTRA)
        rs_arg = route(NT)

        g1b = sb("gate1_rows", [P, D])
        g2b = sb("gate2_rows", [P, D])
        fgb = g1b
        vgb = sb("v_gain_rows", [P, HALF])
        ogb = sb("out_gain_rows", [P, HALF])
        wsT = sb("spatial_T", [P, AH, P])
        ws_raw = rtmp.rearrange("p (h s) -> p h s", h=AH)
        wal = sb("w_alpha", [RANK, 2 * P])
        alT = sb("a_low_T", [RANK, P])
        wr = sb("w_route", [P, KT, NLOG])
        brb = sb("b_route_rows", [P, NLOG])
        ident = sb("ident", [P, P])
        lstrict = sb("strict_before", [P, P])
        tri = sb("tri32", [P, 32])
        ones = sb("ones", [P, P])
        zeros = sb("zeros", [P, P])
        cT = sb("c_cols", [P, KT])
        cE = sb("c_exp", [P, KT])
        bcols = sb("b_ada_cols", [P, 4, KT])
        gain1 = sb("gain1", [P, KT])
        gain2 = sb("gain2", [P, KT])
        a1 = sb("a1", [P, KT])
        sh1 = sb("sh1", [P, KT])
        a2 = sb("a2", [P, KT])
        sh2 = sb("sh2", [P, KT])
        bal = sb("b_alpha_cols", [P, 2])
        bsT = sb("b_spatial_cols", [P, AH])
        eps = sb("eps", [P, 1])
        junk = sb("unused_squares", [P, D], mybir.dt.bfloat16)
        dec = sb("state_decay", [P, 2])
        ss1 = sb("ss1", [P, 1])
        rs1 = sb("rs1", [P, 1])
        ssv = sb("ssv", [P, 1])
        rsv = sb("rsv", [P, 1])
        sso = sb("sso", [P, AH])
        rso = sb("rso", [P, AH])
        ss2 = sb("ss2", [P, 1])
        rs2 = sb("rs2", [P, 1])
        lg = sb("logits", [P, NT, NLOG])
        iota4 = sb("iota4", [P, NT, NG])
        iota8 = sb("iota8", [P, NT, EPG])
        io4 = sb("io4", [P, NG], I32)
        io8 = sb("io8", [P, EPG], I32)
        ioj = sb("ioj", [P, MAXEXTRA], I32)
        iojf = sb("iojf", [P, MAXEXTRA])
        ioe = sb("ioe", [P, NE], I32)
        base1 = sb("base1", [P, NE])
        iok = sb("iok", [P, EPG], I32)
        thr = sb("thr", [P, EPG])
        toki = sb("token_id_i", [P, NT], I32)
        tokf = sb("token_id", [P, NT])
        gt1 = sb("gate_first", [P, NT])
        gt2 = sb("gate_second", [P, NT])
        sli = sb("slot_i", [P, 2, NT], I32)
        exi = sb("extra_expert", [P, MAXEXTRA], I32)
        nxi = sb("n_extra", [P, 1], I32)
        tbl = sb("table_rows", [NBLK, P])
        idx = sb("block_tokens", [P, NBLK], I32)
        idc = [sb("block_col0", [P, 1], I32), sb("block_col1", [P, 1], I32)]
        idp = sb("block_col_copy", [P, 1], I32)
        fss = sb("fss", [P, NT])
        frs = sb("frs", [P, NT])

        def bank(name):
            return ctx.enter_context(nc.psum_tensor(name, [P, HALF], F32))

        PJ0, PJ1, T0, T1, SC0, SC1, SC2, OB = [bank(n) for n in
                                              ("PJ0", "PJ1", "T0", "T1", "SC0", "SC1", "SC2", "OB")]
        T4 = [T0[:, :].rearrange("p (k t) -> p k t", k=4), T1[:, :].rearrange("p (k t) -> p k t", k=4)]
        S4 = [SC0[:, :].rearrange("p (k t) -> p k t", k=4), SC1[:, :].rearrange("p (k t) -> p k t", k=4)]
        QK = PJ0[:, :].rearrange("p (c t) -> p c t", c=4)
        ALOW = PJ1[0:RANK, 0:P]
        ZA = PJ1[:, P:3 * P].rearrange("p (c t) -> p c t", c=2)
        SCO = [a[:, :].rearrange("p (l c t) -> p l c t", l=2, c=2) for a in (SC0, SC1)]
        L64 = [a[0:64, 0:P].rearrange("p (c t) -> p c t", c=2) for a in (SC2, OB)]
        KDT = SC2[:, 256:512].rearrange("p (c k) -> p c k", c=2)
        mod_sum = [xn2, y_sb, g1b[:, :], xn2, xb, g2b[:, :]]
        GATES = (2, 5)
        PIECES = [(0, 0), (1, 0), (2, 0), (2, 1), (3, 0), (4, 0), (5, 0), (5, 1)]
        N_EARLY = 4

        const_in = sem("const_in")
        norms_in = sem("norms_in")
        adaw_in = [sem("adaw_in0"), sem("adaw_in1")]
        win_in = [sem("win_in_%s" % n) for n in ("qk", "ra", "v", "av", "u")]
        route_in = sem("route_in")
        brow_in = sem("brow_in")
        wout_in = sem("wout_in")
        consts_made = sem("consts_made")
        spatial_made = sem("spatial_made")
        cact_made = sem("cact_made")
        ada_sum = sem("ada_sum")
        ada_spread = sem("ada_spread")
        ada_taken = sem("ada_taken")
        ws_mm = sem("ws_mm")
        xa_in = sem("xa_in")
        xb_in = sem("xb_in")
        rs1_made = sem("rs1_made")
        xn_made = sem("xn_made")
        xT_mm = sem("xT_mm")
        hT_made = sem("hT_made")
        qk_mm = sem("qk_mm")
        qk_ev = sem("qk_ev")
        alow_mm = sem("alow_mm")
        alow_ev = sem("alow_ev")
        za_mm = sem("za_mm")
        za_ev = sem("za_ev")
        ln_made = sem("ln_made")
        ex_args = sem("ex_args")
        ex_exp = sem("ex_exp")
        ex_made = sem("ex_made")
        sc_mm = sem("sc_mm")
        sc_off = sem("sc_off")
        sc_diag = sem("sc_diag")
        kdt_mm = sem("kdt_mm")
        kdt_ev = sem("kdt_ev")
        o_mm = sem("o_mm")
        st_mm = sem("st_mm")
        st_made = sem("st_made")
        sg_mm = sem("sg_mm")
        v_mm = sem("v_mm")
        v_ev = sem("v_ev")
        av_mm = sem("av_mm")
        av_ev = sem("av_ev")
        vn_made = sem("vn_made")
        rsv_made = sem("rsv_made")
        u_mm = sem("u_mm")
        u_ev = sem("u_ev")
        r_mm = sem("r_mm")
        r_exp = sem("r_exp")
        rg_made = sem("rg_made")
        rso_made = sem("rso_made")
        y_made = sem("y_made")
        yT_mm = sem("yT_mm")
        yT_ev = sem("yT_ev")
        mix_mm = sem("mix_mm")
        x1_made = sem("x1_made")
        rs2_made = sem("rs2_made")
        xn2_made = sem("xn2_made")
        x1_out = sem("x1_out")
        xn2_out = sem("xn2_out")
        h2T_mm = sem("h2T_mm")
        h2T_ev = sem("h2T_ev")
        lg_mm = sem("lg_mm")
        ob_free = sem("ob_free")
        dve_done = sem("dve_done")
        act_done = sem("act_done")
        pool_done = sem("pool_done")
        both_made = sem("both_made")
        rank_mm = sem("rank_mm")
        route_arg = sem("route_arg")
        route_exp = sem("route_exp")
        route_arg2 = sem("route_arg2")
        slots_made = sem("slots_made")
        table_zero = sem("table_zero")
        table_out = sem("table_out")
        table_in = sem("table_in")
        table_mm = sem("table_mm")
        idx_made = sem("idx_made")
        extra_made = sem("extra_made")
        w13_in = [sem("w13_in0"), sem("w13_in1")]
        w2_in = [sem("w2_in0"), sem("w2_in1")]
        idc_made = sem("idc_made")
        xg_in = [sem("xg_in0"), sem("xg_in1")]
        xg_mm = sem("xg_mm")
        xg_ev = sem("xg_ev")
        up_mm = sem("up_mm")
        silu_made = sem("silu_made")
        hid_made = sem("hid_made")
        hidT_mm = sem("hidT_mm")
        hidT_ev = sem("hidT_ev")
        dn_mm = sem("dn_mm")
        dn_ev = sem("dn_ev")
        y_zero = sem("y_zero")
        y_out = [sem("y_out0"), sem("y_out1")]
        fy_in = [sem("fy_in%d" % i) for i in range(NT)]
        y1_scaled = sem("y1_scaled")
        fx_in = sem("fx_in")
        experts_left = sem("experts_left")
        fgb_in = sem("fgb_in")
        x2_made = sem("x2_made")
        frs_made = sem("frs_made")
        fo_made = sem("fo_made")
        out_out = sem("out_out")
        block = ctx.enter_context(nc.Block())

        class Chain:

            def __init__(self, eng, done):
                self.eng, self.done, self.base, self.n = eng, done, 0, 0

            def link(self, ins):
                self.n += 1
                ins.then_inc(self.done, 1)
                self.eng.wait_ge(self.done, self.base + self.n)

        N_CONST = 6
        DVE_STEP = 8
        ACT_STEP = 14

        @block.sync
        def _(sp):
            sp.dma_start(cT[:, :], c.rearrange("a (p k) -> (a p) k", k=KT)).then_inc(norms_in, 16)
            sp.dma_start(gain1[:, :], norm1_gain.rearrange("a (p k) -> (a p) k", k=KT)).then_inc(norms_in, 16)
            sp.dma_start(gain2[:, :], norm2_gain.rearrange("a (p k) -> (a p) k", k=KT)).then_inc(norms_in, 16)
            ada_v = w_ada[0, :, :].rearrange("(p k) n -> p k n", k=KT)
            with nc.allow_non_contiguous_dma(reason="small constants"):
                for m, vec in enumerate((0, 1, 3, 4)):
                    sp.dma_start(bcols[:, m, :], b_ada[0, vec * D:(vec + 1) * D].rearrange("(p k) -> p k", k=KT)
                                 ).then_inc(norms_in, 16)

            def load_ada(n):
                if n >= 2:
                    sp.wait_ge(ada_sum, n - 1)
                sp.dma_start(ada_w[:, n % 2, :, :], ada_v[:, :, n * HALF:(n + 1) * HALF]).then_inc(adaw_in[n % 2], 16)

            def load_brow(v):
                sp.dma_start(brow, b_ada[0:1, v * D:(v + 1) * D]).then_inc(brow_in, 16)

            load_ada(0)
            load_ada(1)
            sp.dma_start(xa[:, :], x[0, 0:P, :]).then_inc(xa_in, 16)
            load_ada(2)
            win_v = w_in[0, :, :].rearrange("(p k) n -> p k n", k=KT)
            for n, (c0, c1) in enumerate(((C_Q, C_V), (C_R, P_IN), (C_V, C_R), (C_AV, C_Q), (C_U, C_AV))):
                sp.dma_start(win[:, :, c0:c1], win_v[:, :, c0:c1]).then_inc(win_in[n], 16)
                if n == 0:
                    load_ada(3)
                    with nc.allow_non_contiguous_dma(reason="small constants"):
                        sp.dma_start(bal[:, :], b_b_alpha[0, :].rearrange("(c p) -> p c", p=P)).then_inc(const_in, 16)
                        sp.dma_start(bsT[:, :], a_b_s[0, :, :].rearrange("h t -> t h")).then_inc(const_in, 16)
                    sp.dma_start(wal[:, :], b_w_alpha[0, :, :]).then_inc(const_in, 16)
                if n == 1:
                    sp.dma_start(ws_raw[:, :, :], a_w_s[0, :, :, :].rearrange("h t s -> t h s")).then_inc(const_in, 16)
                    sp.dma_start(vgb[:, :], a_v_gain[0, :].partition_broadcast(P)).then_inc(const_in, 16)
                    sp.dma_start(ogb[:, :], b_out_gain[0, :].partition_broadcast(P)).then_inc(const_in, 16)
            load_brow(2)
            sp.wait_ge(xn_made, 1)
            sp.dma_start(xa[:, :], x[0, P:2 * P, :]).then_inc(xa_in, 16)
            for n in range(N_EARLY, 12):
                load_ada(n)
                if n == 5:
                    with nc.allow_non_contiguous_dma(reason="small constants"):
                        sp.dma_start(wr[:, :, 0:NG], w_group[0, :, :].rearrange("(p k) n -> p k n", k=KT)).then_inc(route_in, 16)
                        sp.dma_start(wr[:, :, NG:NLOG], w_router[0, :, :].rearrange("(p k) n -> p k n", k=KT)).then_inc(route_in, 16)
                    sp.dma_start(brb[:, 0:NG], b_group[0, :].partition_broadcast(P)).then_inc(route_in, 16)
                    sp.dma_start(brb[:, NG:NLOG], b_router[0, :].partition_broadcast(P)).then_inc(route_in, 16)
                if n == 10:
                    sp.wait_ge(ada_spread, 4)
                    load_brow(5)
            sp.wait_ge(ada_sum, 12)
            sp.dma_start(wout, w_out[0, :, :].rearrange("(p k) n -> p k n", k=KT)).then_inc(wout_in, 16)
            sp.wait_ge(ada_spread, 6)
            sp.dma_start(xb[:, :], x[0, 0:P, :]).then_inc(xb_in, 16)

            def load_xa(i):
                sp.wait_ge(xn_made, i)
                sp.dma_start(xa[:, :], x[0, bass.ts(i, P), :]).then_inc(xa_in, 16)

            def tile_out(i, more):
                sp.wait_ge(x1_made, i + 1)
                sp.dma_start(x1_dram[bass.ts(i, P), :], xb[:, :]).then_inc(x1_out, 16)
                sp.wait_ge(xn2_made, i + 1)
                sp.dma_start(xn2_dram[bass.ts(i, P), :], xn2[:, :]).then_inc(xn2_out, 16)
                if more:
                    sp.wait_ge(x1_out, 16 * (i + 1))
                    sp.dma_start(xb[:, :], x[0, bass.ts(i + 1, P), :]).then_inc(xb_in, 16)

            with sp.Fori(0, NT - 2) as i:
                load_xa(i + 2)
                tile_out(i, True)
            tile_out(NT - 2, True)
            tile_out(NT - 1, False)

            def weights(b, r, par, e, first):
                if not first:
                    sp.wait_ge(up_mm, b - 1)
                sp.dma_start(W1[par], w1[0, e, :, :].rearrange("(p k) n -> p k n", k=KT)).then_inc(w13_in[par], 16)
                sp.dma_start(W3[par], w3[0, e, :, :].rearrange("(p k) n -> p k n", k=KT)).then_inc(w13_in[par], 16)
                if not first:
                    sp.wait_ge(dn_mm, b - 1)
                sp.dma_start(W2[par], w2[0, e, :, :].rearrange("(p k) n -> p k n", k=FKT)).then_inc(w2_in[par], 16)

            sp.wait_ge(mix_mm, NT)
            weights(0, 0, 0, 0, True)
            sp.wait_ge(x1_made, NT)
            sp.dma_start(fgb[:, :], final_gain.partition_broadcast(P)).then_inc(fgb_in, 16)
            sp.wait_ge(table_out, 16 * 2 * NT)
            sp.dma_start(tbl[:, :], table_dram.rearrange("(b p) a -> b (p a)", p=P)).then_inc(table_in, 16)
            sp.wait_ge(xg_in[0], 16)
            sp.wait_ge(xg_in[1], 16)
            weights(1, 0, 1, 1, True)
            with sp.Fori(1, NE // 2) as q:
                weights(2 * q, q, 0, 2 * q, False)
                weights(2 * q + 1, q, 1, 2 * q + 1, False)
            sp.wait_ge(x1_out, 16 * NT)
            sp.wait_ge(xn2_out, 16 * NT)
            sp.wait_ge(ob_free, NT + 1)
            sp.dma_start(fx, x1_dram.rearrange("(i p) n -> p i n", p=P)).then_inc(fx_in, 16)
            sp.wait_ge(extra_made, 1)
            n_extra = sp.value_load(nxi[0:1, 0:1], min_val=0, max_val=MAXEXTRA)
            with sp.Fori(0, MAXEXTRA // 2) as q:
                for par in range(2):
                    with sp.If(n_extra > 2 * q + par):
                        e = sp.value_load(exi[0:1, bass.ds(2 * q + par, 1)], min_val=0, max_val=NE - 1)
                        weights(2 * q + par + NE, q + NE // 2, par, e, False)
            sp.wait_ge(out_out, 16 * NT)

        @block.gpsimd
        def _(pool):
            g = nc.gpsimd
            chain = Chain(pool, pool_done)
            link = chain.link
            g.memset(eps[:, :], EPS)
            g.memset(state, 0.0)
            g.memset(pT, 0.0)
            g.memset(ones[:, :], 1.0)
            g.memset(zeros[:, :], 0.0)
            link(g.memset(ident[:, :], 1.0))
            link(g.affine_select(out=ident[:, :], in_=ident[:, :], compare_op=ALU.is_equal, fill=0.0,
                                 base=0, pattern=[[-1, P]], channel_multiplier=1))
            link(g.affine_select(out=lstrict[:, :], in_=ones[:, :], compare_op=ALU.is_gt, fill=0.0,
                                 base=0, pattern=[[1, P]], channel_multiplier=-1))
            for j in range(4):
                link(g.affine_select(out=tri[32 * j:32 * j + 32, :], in_=ones[32 * j:32 * j + 32, 0:32],
                                     compare_op=ALU.is_ge, fill=0.0, base=0, pattern=[[1, 32]],
                                     channel_multiplier=-1))
            g.iota(io4[:, :], [[1, NG]], 0, 0)
            g.iota(io8[:, :], [[1, EPG]], 0, 0)
            g.iota(ioj[:, :], [[1, MAXEXTRA]], 0, 0)
            g.iota(ioe[:, :], [[P, NE]], 0, 0)
            g.iota(iok[:, :], [[P, EPG]], P, 0)
            g.iota(toki[:, :], [[P, NT]], 0, 1).then_inc(consts_made, 1)
            pool.wait_ge(const_in, 16 * N_CONST)
            g.affine_select(out=ws_raw, in_=ws_raw, compare_op=ALU.is_ge, fill=0.0, base=0,
                            pattern=[[0, AH], [-1, P]], channel_multiplier=1).then_inc(spatial_made, 1)
            link(g.memset(tbl[:, :], 0.0))
            pool.dma_start(table_dram.rearrange("(b p) a -> b (p a)", p=P), tbl[:, :]).then_inc(table_zero, 16)
            zero_src = zeros[:, :].rearrange("p (m n) -> p m n", m=1).broadcast_to([P, 4 * D // P, P])
            for j in range(MAXEXTRA // 4):
                pool.wait_ge(xn_made, j + 4)
                dst = y_dram[(NE + 4 * j) * P:(NE + 4 * j + 4) * P, :]
                pool.dma_start(dst.rearrange("(p b) (m n) -> p (b m) n", p=P, n=P), zero_src).then_inc(y_zero, 16)
            pool.wait_ge(table_zero, 16)
            pool.wait_ge(slots_made, 1)
            for i in range(NT):
                for j in range(2):
                    pool.indirect_dma_start(out=table_dram, out_offset=bass.IndirectOffsetOnAxis(
                        ap=sli[:, j, i:i + 1], axis=0), in_=tokf[:, i:i + 1], in_offset=None).then_inc(table_out, 16)

            def gather(b, r, par, first):
                if not first:
                    pool.wait_ge(xg_mm, b - 1)
                    pool.wait_ge(xg_in[par], 16 * r)
                g.tensor_copy(idc[par][:, :], idx[:, bass.ds(b, 1)]).then_inc(idc_made, 1)
                pool.wait_ge(idc_made, b + 1)
                g.tensor_tensor(idp[:, :], idc[par][:, :], idc[par][:, :], ALU.add)
                pool.indirect_dma_start(out=xr[par], out_offset=None, in_=xn2_dram,
                                        in_offset=bass.IndirectOffsetOnAxis(ap=idc[par][:, 0:1], axis=0)
                                        ).then_inc(xg_in[par], 16)

            pool.wait_ge(idx_made, 1)
            pool.wait_ge(xn2_out, 16 * NT)
            gather(0, 0, 0, True)
            gather(1, 0, 1, True)
            with pool.Fori(1, NE // 2) as q:
                gather(2 * q, q, 0, False)
                gather(2 * q + 1, q, 1, False)
            pool.wait_ge(extra_made, 1)
            n_extra = pool.value_load(nxi[0:1, 0:1], min_val=0, max_val=MAXEXTRA)
            with pool.Fori(0, MAXEXTRA // 2) as q:
                for par in range(2):
                    with pool.If(n_extra > 2 * q + par):
                        gather(2 * q + par + NE, q + NE // 2, par, False)
            pool.wait_ge(experts_left, 3)
            for i in range(NT):
                for j, dst in enumerate((fy1, fy2)):
                    pool.indirect_dma_start(out=dst[i], out_offset=None, in_=y_dram,
                                            in_offset=bass.IndirectOffsetOnAxis(ap=sli[:, j, i:i + 1], axis=0)
                                            ).then_inc(fy_in[i], 16)

        @block.tensor
        def _(pe):
            mm = nc.tensor.matmul
            tp = nc.tensor.transpose
            pe.wait_ge(consts_made, 1)

            def spread(piece):
                v, hf = PIECES[piece]
                pe.wait_ge(ada_sum, 2 * v + (hf + 1 if v in GATES else 2))
                if piece:
                    pe.wait_ge(ada_taken, piece)
                if v in GATES:
                    half = slice(hf * HALF, (hf + 1) * HALF)
                    pe.wait_ge(brow_in, 16 * (GATES.index(v) + 1))
                    mm(SC2[:, :], ones[:, :], mod_sum[v][:, half], start=True, stop=False)
                    mm(SC2[:, :], ones[0:1, :], brow[:, half], start=False, stop=True).then_inc(ada_spread, 1)
                else:
                    cols = mod_sum[v].rearrange("q (p k) -> q k p", k=KT)
                    for k in range(KT):
                        last = mm(SC2[:, k:k + 1], cols[:, k, :], ones[:, 0:1], start=True, stop=True)
                    last.then_inc(ada_spread, 1)

            def spatial_transposes():
                pe.wait_ge(spatial_made, 1)
                for h in range(AH):
                    last = tp(OB[:, h * P:(h + 1) * P], ws_raw[:, h, :], ident[:, :])
                last.then_inc(ws_mm, 1)

            def x_transposes(i, first):
                pe.wait_ge(xn_made, i + 1)
                if not first:
                    pe.wait_ge(yT_ev, i - 1)
                cols = xn.rearrange("p (m k) -> p k m", k=KT)
                for k in range(KT):
                    last = tp(T4[k // 4][:, k % 4, :], cols[:, k, :], ident[:, :])
                last.then_inc(xT_mm, 1)

            def project(acc, c0, hTs):
                for k in range(KT):
                    last = mm(acc[:, :], hTs[:, k, :], win[:, k, c0:c0 + HALF], start=(k == 0), stop=(k == KT - 1))
                return last

            def logits(n):
                pe.wait_ge(h2T_ev, n)
                for k in range(KT):
                    last = mm(OB[:, 0:NLOG], h2T[:, k, :], wr[:, k, :], start=(k == 0), stop=(k == KT - 1))
                last.then_inc(lg_mm, 1)

            def step(s, par, first=False, second=False, head=True, tail=True, nxt=True):
                hTs = hT[par]
                def win_piece(n):
                    if first:
                        pe.wait_ge(win_in[n], 16)

                if head:
                    pe.wait_ge(hT_made, s + 1)
                    win_piece(0)
                    if not first:
                        pe.wait_ge(u_ev, s)
                    for m in range(4):
                        for k in range(KT):
                            last = mm(QK[:, m, :], win[:, k, C_Q + m * P:C_Q + (m + 1) * P], hTs[:, k, :],
                                      start=(k == 0), stop=(k == KT - 1))
                    last.then_inc(qk_mm, 1)
                if tail and not second:
                    logits(s - 1)
                if head:
                    if not first:
                        pe.wait_ge(rg_made, s)
                    win_piece(1)
                    for k in range(KT):
                        last = mm(ALOW, win[:, k, C_A:P_IN], hTs[:, k, :], start=(k == 0), stop=(k == KT - 1))
                    last.then_inc(alow_mm, 1)
                if tail:
                    pe.wait_ge(ex_made, s)
                    pe.wait_ge(ob_free, s)
                    if second:
                        pe.wait_ge(ada_taken, 4)
                    for cc in range(2):
                        for half in range(2):
                            rows = slice(64 * half, 64 * half + 64)
                            mm(SCO[half][:, 0, cc, :], ex[rows, A_KG, cc, :], ex[rows, A_QD, cc, :], start=True,
                               stop=True)
                            mm(SCO[half][:, 1, cc, :], ex[rows, A_L32, cc, :], ex[rows, A_L32, cc, :], start=True,
                               stop=True)
                            last = mm(L64[half][:, cc, :], ex[rows, A_L64, cc, 0:64], ex[rows, A_L64, cc, 64:P],
                                      start=True, stop=True)
                    last.then_inc(sc_mm, 1)
                if head:
                    pe.wait_ge(qk_ev, s + 1)
                    win_piece(2)
                    project(PJ0, C_V, hTs).then_inc(v_mm, 1)
                    pe.wait_ge(alow_ev, s + 1)
                    for cc in range(2):
                        last = mm(ZA[:, cc, :], wal[:, cc * P:(cc + 1) * P], alT[:, :], start=True, stop=True)
                    last.then_inc(za_mm, 1)
                if tail:
                    pe.wait_ge(sc_off, s)
                    for cc in range(2):
                        last = tp(KDT[:, cc, :], ex[:, A_KD, cc, :], ident[:, :])
                    last.then_inc(kdt_mm, 1)
                    pe.wait_ge(sc_diag, s)
                    pe.wait_ge(st_made, s)
                    for cc in range(2):
                        mm(OB[:, 256 * cc:256 * cc + 256], ex[:, A_QI, cc, :], state[:, cc, :], start=(cc == 0),
                           stop=False)
                    for h in range(AH):
                        last = mm(OB[:, h * P:(h + 1) * P], pT[:, h, :], v_sb[:, h * P:(h + 1) * P], start=False,
                                  stop=(h == AH - 1))
                    last.then_inc(o_mm, 1)
                    pe.wait_ge(kdt_ev, s)
                    for cc in range(2):
                        last = mm(SC1[:, 256 * cc:256 * cc + 256], kdT[:, cc, :], v_sb[:, 256 * cc:256 * cc + 256],
                                  start=True, stop=True)
                    last.then_inc(st_mm, 1)
                    pe.wait_ge(vn_made, s)
                    for h in range(AH):
                        last = mm(SC0[:, h * P:(h + 1) * P], wsT[:, h, :], av_sb[:, h * P:(h + 1) * P], start=True,
                                  stop=True)
                    last.then_inc(sg_mm, 1)
                if head:
                    if first:
                        spatial_transposes()
                    pe.wait_ge(za_ev, s + 1)
                    win_piece(3)
                    project(PJ1, C_AV, hTs).then_inc(av_mm, 1)
                if tail:
                    pe.wait_ge(y_made, s)
                    cols = y_sb.rearrange("p (m k) -> p k m", k=KT)
                    for k in range(KT):
                        last = tp(T4[k // 4][:, k % 4, :], cols[:, k, :], ident[:, :])
                    last.then_inc(yT_mm, 1)
                if head:
                    pe.wait_ge(v_ev, s + 1)
                    win_piece(4)
                    project(PJ0, C_U, hTs).then_inc(u_mm, 1)
                if second:
                    for piece in range(4, 8):
                        spread(piece)
                    pe.wait_ge(ada_taken, 8)
                    pe.wait_ge(wout_in, 16)
                    pe.wait_ge(route_in, 16 * 4)
                if tail:
                    pe.wait_ge(yT_ev, s)
                    pe.wait_ge(st_made, s + 1)
                    for hf in range(2):
                        for k in range(KT):
                            last = mm((SC0, SC1)[hf][:, :], yT[:, k, :], wout[:, k, hf * HALF:(hf + 1) * HALF],
                                      start=(k == 0), stop=(k == KT - 1))
                    last.then_inc(mix_mm, 1)
                if nxt:
                    x_transposes(s + 1, first)
                if head:
                    pe.wait_ge(av_ev, s + 1)
                    project(PJ1, C_R, hTs).then_inc(r_mm, 1)
                if first:
                    spread(2)
                    spread(3)
                if tail:
                    pe.wait_ge(xn2_made, s)
                    cols = xn2.rearrange("p (m k) -> p k m", k=KT)
                    for k in range(KT):
                        last = tp(S4[k // 4][:, k % 4, :], cols[:, k, :], ident[:, :])
                    last.then_inc(h2T_mm, 1)

            x_transposes(0, True)
            spread(0)
            spread(1)
            step(0, 0, first=True, tail=False)
            step(1, 1, second=True)
            with pe.Fori(1, (NT - 2) // 2) as j:
                step(2 * j, 0)
                step(2 * j + 1, 1)
            step(NT - 2, 0)
            step(NT - 1, (NT - 1) % 2, nxt=False)
            step(NT, 0, head=False, nxt=False)
            logits(NT)

            pe.wait_ge(both_made, 1)
            bothf = both.rearrange("p a b -> p (a b)")
            mm(SC0[:, 0:NT * NE], lstrict[:, :], bothf, start=True, stop=True)
            mm(SC1[:, 0:NT * NE], ones[:, :], bothf, start=True, stop=True).then_inc(rank_mm, 1)
            pe.wait_ge(table_in, 16)
            tp(SC2[:, 0:NBLK], tbl[:, :], ident[0:NBLK, 0:NBLK]).then_inc(table_mm, 1)

            def row_transposes(b, r, par, first=False):
                pe.wait_ge(xg_in[par], 16 * (r + 1))
                if not first:
                    pe.wait_ge(xg_ev, b)
                cols = xr[par].rearrange("p (m k) -> p k m", k=KT)
                for k in range(KT):
                    last = tp(T4[k // 4][:, k % 4, :], cols[:, k, :], ident[:, :])
                last.then_inc(xg_mm, 1)

            def up(b, r, par, first=False):
                pe.wait_ge(xg_ev, b + 1)
                pe.wait_ge(w13_in[par], 32 * (r + 1))
                if not first:
                    pe.wait_ge(hid_made, b)
                for acc, w in ((PJ0, W1[par]), (PJ1, W3[par])):
                    for k in range(KT):
                        last = mm(acc[:, :], xT[par][:, k, :], w[:, k, :], start=(k == 0), stop=(k == KT - 1))
                last.then_inc(up_mm, 1)

            def hidden_transposes(b, r, par):
                pe.wait_ge(hid_made, b + 1)
                cols = hid.rearrange("p (m k) -> p k m", k=FKT)
                for k in range(FKT):
                    last = tp(SC2[:, k * P:(k + 1) * P], cols[:, k, :], ident[:, :])
                last.then_inc(hidT_mm, 1)

            def down(b, r, par, first=False):
                pe.wait_ge(hidT_ev, b + 1)
                pe.wait_ge(w2_in[par], 16 * (r + 1))
                if not first:
                    pe.wait_ge(dn_ev, b)
                for hf in range(2):
                    for k in range(FKT):
                        last = mm((SC0, SC1)[hf][:, :], hidT[:, k, :], W2[par][:, k, hf * HALF:(hf + 1) * HALF],
                                  start=(k == 0), stop=(k == FKT - 1))
                last.then_inc(dn_mm, 1)

            pe.wait_ge(idx_made, 1)
            row_transposes(0, 0, 0, True)
            up(0, 0, 0, True)
            row_transposes(1, 0, 1)
            hidden_transposes(0, 0, 0)

            def block_step(b, r, par, first=False, nxt=True):
                up(b, r, par)
                if nxt:
                    row_transposes(b + 1, r + par, 1 - par)
                down(b - 1, r - 1 + par, 1 - par, first)
                hidden_transposes(b, r, par)

            block_step(1, 0, 1, first=True)
            with pe.Fori(1, NE // 2 - 1) as q:
                block_step(2 * q, q, 0)
                block_step(2 * q + 1, q, 1)
            block_step(NE - 2, NE // 2 - 1, 0)
            block_step(NE - 1, NE // 2 - 1, 1, nxt=False)
            down(NE - 1, NE // 2 - 1, 1)
            pe.wait_ge(extra_made, 1)
            n_extra = pe.value_load(nxi[0:1, 0:1], min_val=0, max_val=MAXEXTRA)
            with pe.Fori(0, MAXEXTRA // 2) as q:
                for par in range(2):
                    with pe.If(n_extra > 2 * q + par):
                        b, r = 2 * q + par + NE, q + NE // 2
                        row_transposes(b, r, par)
                        up(b, r, par)
                        hidden_transposes(b, r, par)
                        down(b, r, par)
            pe.nop().then_inc(experts_left, 1)

        @block.scalar
        def _(act):
            f = nc.scalar.activation
            chain = Chain(act, act_done)
            link = chain.link

            def rstd(ss, rs, width):
                link(f(rs, ss, ACT.Ln, bias=eps[:, :], scale=1.0 / width))
                return f(rs, rs, ACT.Exp, scale=-0.5)

            act.wait_ge(norms_in, 16 * 7)
            act.wait_ge(consts_made, 1)
            f(cE[:, :], cT[:, :], ACT.Exp, scale=-1.0).then_inc(act_done, 1)
            chain.n += 1
            def x_norm(i):
                act.wait_ge(xa_in, 16 * (i + 1))
                link(f(junk[:, :], xa, ACT.Square, accum_out=ss1[:, :]))
                rstd(ss1[:, :], rs1[:, :], D).then_inc(rs1_made, 1)

            def step(s, first=False, second=False, head=True, tail=True, nxt=True):
                if head:
                    act.wait_ge(qk_mm, s + 1)
                    if not first:
                        act.wait_ge(ex_made, s)
                    f(qT, QK[:, 0:2, :], ACT.Copy, scale=BK ** -0.5)
                    f(kT, QK[:, 2:4, :], ACT.Copy).then_inc(qk_ev, 1)
                    act.wait_ge(alow_mm, s + 1)
                    f(alT[:, :], ALOW, ACT.Copy).then_inc(alow_ev, 1)
                if tail:
                    act.wait_ge(sc_diag, s)
                    for half in range(2):
                        f(pT4[0:64, :, half, 64:P], L64[half], ACT.Copy)
                        f(pT4[0:32, :, half, 32:64], SCO[half][0:32, 1, :, 32:64], ACT.Copy)
                        last = f(pT4[64:96, :, half, 96:P], SCO[half][64:96, 1, :, 96:P], ACT.Copy)
                    last.then_inc(sc_off, 1)
                    act.wait_ge(kdt_mm, s)
                    f(kdT, KDT, ACT.Copy).then_inc(kdt_ev, 1)
                if head:
                    act.wait_ge(za_mm, s + 1)
                    for cc in range(2):
                        last = f(zb[:, cc, :], ZA[:, cc, :], ACT.Identity, bias=bal[:, cc:cc + 1])
                    last.then_inc(za_ev, 1)
                    act.wait_ge(za_ev, s + 1)
                    link(f(az, zb, ACT.Abs))
                    link(f(az, az, ACT.Exp, scale=-1.0))
                    f(lneg, az, ACT.Ln, bias=1.0).then_inc(ln_made, 1)
                if tail:
                    act.wait_ge(o_mm, s)
                    for h in range(AH):
                        link(f(junk[:, 0:P], OB[:, h * P:(h + 1) * P], ACT.Square, accum_out=sso[:, h:h + 1]))
                    rstd(sso[:, :], rso[:, :], P).then_inc(rso_made, 1)
                if head:
                    act.wait_ge(ex_args, s + 1)
                    f(ex, ex, ACT.Exp, scale=1.0 / TAU).then_inc(ex_exp, 1)
                    act.wait_ge(av_mm, s + 1)
                    if not first:
                        act.wait_ge(sg_mm, s)
                    f(av_sb, PJ1[:, :], ACT.Copy).then_inc(av_ev, 1)
                if first:
                    act.wait_ge(ws_mm, 1)
                    f(wsT[:, :, :].rearrange("p h t -> p (h t)"), OB[:, :], ACT.Copy).then_inc(ob_free, 1)
                if tail:
                    act.wait_ge(yT_mm, s)
                    if second:
                        act.wait_ge(ada_spread, len(PIECES))
                    f(yT[:, 0:4, :], T4[0], ACT.Copy)
                    f(yT[:, 4:8, :], T4[1], ACT.Copy).then_inc(yT_ev, 1)
                if nxt:
                    x_norm(s + 1)
                if head:
                    act.wait_ge(u_mm, s + 1)
                    if not first:
                        act.wait_ge(y_made, s)
                    f(u_sb, PJ0[:, :], ACT.Gelu_apprx_tanh).then_inc(u_ev, 1)
                    act.wait_ge(av_ev, s + 1)
                    link(f(av_sb, av_sb, ACT.Gelu_apprx_tanh))
                    link(f(junk[:, 0:HALF], av_sb, ACT.Square, accum_out=ssv[:, :]))
                    rstd(ssv[:, :], rsv[:, :], HALF).then_inc(rsv_made, 1)
                if tail:
                    act.wait_ge(x1_made, s)
                    link(f(junk[:, :], xb, ACT.Square, accum_out=ss2[:, :]))
                    rstd(ss2[:, :], rs2[:, :], D).then_inc(rs2_made, 1)
                if head:
                    act.wait_ge(r_mm, s + 1)
                    if not first:
                        act.wait_ge(rg_made, s)
                    f(rtmp, PJ1[:, :], ACT.Exp, scale=-1.0).then_inc(r_exp, 1)

            x_norm(0)
            step(0, first=True, tail=False)
            step(1, second=True)
            n0 = chain.base + chain.n
            with act.Fori(1, (NT - 2) // 2) as j:
                chain.base, chain.n = n0 + 2 * ACT_STEP * (j - 1), 0
                step(2 * j)
                assert chain.n == ACT_STEP, ("ACT_STEP", chain.n)
                chain.base, chain.n = n0 + ACT_STEP + 2 * ACT_STEP * (j - 1), 0
                step(2 * j + 1)
            chain.base, chain.n = n0 + (NT - 4) * ACT_STEP, 0
            step(NT - 2)
            step(NT - 1, nxt=False)
            step(NT, head=False, nxt=False)

            act.wait_ge(route_arg, 1)
            f(t4, t4, ACT.Exp).then_inc(route_exp, 1)
            act.wait_ge(route_arg, 2)
            f(rs_arg, rs_arg, ACT.Exp).then_inc(route_exp, 1)

            def silu(b, first=False):
                act.wait_ge(up_mm, b + 1)
                if not first:
                    act.wait_ge(hid_made, b)
                f(silu_sb, PJ0[:, :], ACT.Silu).then_inc(silu_made, 1)

            def store(b, r, par, first=False):
                act.wait_ge(dn_ev, b + 1)
                act.dma_start(y_dram[bass.ts(b, P), :], yb[par]).then_inc(y_out[par], 16)

            silu(0, True)
            silu(1)
            store(0, 0, 0, True)
            silu(2)
            store(1, 0, 1, True)
            with act.Fori(1, NE // 2 - 1) as q:
                silu(2 * q + 1)
                store(2 * q, q, 0)
                silu(2 * q + 2)
                store(2 * q + 1, q, 1)
            silu(NE - 1)
            store(NE - 2, NE // 2 - 1, 0)
            store(NE - 1, NE // 2 - 1, 1)
            act.wait_ge(extra_made, 1)
            act.wait_ge(y_zero, 16 * (MAXEXTRA // 4))
            n_extra = act.value_load(nxi[0:1, 0:1], min_val=0, max_val=MAXEXTRA)
            with act.Fori(0, MAXEXTRA // 2) as q:
                for par in range(2):
                    with act.If(n_extra > 2 * q + par):
                        b, r = 2 * q + par + NE, q + NE // 2
                        silu(b)
                        store(b, r, par)
                        act.wait_ge(y_out[par], 16 * (r + 1))
                        f(ssv[:, :], eps[:, :], ACT.Copy)
            for par in range(2):
                act.wait_ge(y_out[par], 16 * NE // 2)
            act.nop().then_inc(experts_left, 1)

            def store_out(i):
                act.wait_ge(fo_made, i + 1)
                act.dma_start(out[0, i * P:(i + 1) * P, :], fy1[i]).then_inc(out_out, 16)

            def scale_rows(i):
                act.wait_ge(fy_in[i], 32)
                f(fy1[i], fy1[i], ACT.Copy, scale=gt1[:, i:i + 1]).then_inc(y1_scaled, 1)

            def norm_pair(i):
                for n in (i - 1, i):
                    act.wait_ge(x2_made, n + 1)
                    link(f(junk[:, :], fy1[n], ACT.Square, accum_out=fss[:, n:n + 1]))
                rstd(fss[:, i - 1:i + 1], frs[:, i - 1:i + 1], D).then_inc(frs_made, 1)

            for i in range(NT + 2):
                if i < NT:
                    scale_rows(i)
                if i >= 3 and i % 2 == 1:
                    norm_pair(i - 2)
                if i >= 5 and i % 2 == 1:
                    store_out(i - 5)
                    store_out(i - 4)
            for i in range(NT - 2, NT):
                store_out(i)

        @block.vector
        def _(dve):
            v = nc.vector
            tt, ts, stt, cp = v.tensor_tensor, v.tensor_scalar, v.scalar_tensor_tensor, v.tensor_copy
            chain = Chain(dve, dve_done)
            link = chain.link

            dve.wait_ge(act_done, 1)
            link(ts(cE[:, :], cE[:, :], 1.0, None, ALU.add))
            link(v.reciprocal(cE[:, :], cE[:, :]))
            tt(cT[:, :], cT[:, :], cE[:, :], ALU.mult).then_inc(cact_made, 1)
            dve.wait_ge(cact_made, 1)

            def ada(n):
                dve.wait_ge(adaw_in[n % 2], 16 * (n // 2 + 1))
                acc = mod_sum[n // 2][:, (n % 2) * HALF:(n % 2 + 1) * HALF]
                w = ada_w[:, n % 2, :, :]
                link(ts(acc, w[:, 0, :], cT[:, 0:1], None, ALU.mult))
                for k in range(1, KT - 1):
                    link(stt(acc, w[:, k, :], cT[:, k:k + 1], acc, ALU.mult, ALU.add))
                stt(acc, w[:, KT - 1, :], cT[:, KT - 1:KT], acc, ALU.mult, ALU.add).then_inc(ada_sum, 1)

            def take(piece):
                vec, hf = PIECES[piece]
                dve.wait_ge(ada_spread, piece + 1)
                if vec == 0:
                    last = tt(sh1[:, :], SC2[:, 0:KT], bcols[:, 0, :], ALU.add)
                if vec == 3:
                    last = tt(sh2[:, :], SC2[:, 0:KT], bcols[:, 2, :], ALU.add)
                if vec in (1, 4):
                    a, m, gain = (a1, 1, gain1) if vec == 1 else (a2, 3, gain2)
                    link(tt(a[:, :], SC2[:, 0:KT], bcols[:, m, :], ALU.add))
                    last = stt(a[:, :], a[:, :], 1.0, gain[:, :], ALU.add, ALU.mult)
                if vec in GATES:
                    last = cp((g1b if vec == 2 else g2b)[:, hf * HALF:(hf + 1) * HALF], SC2[:, :])
                last.then_inc(ada_taken, 1)

            dve.wait_ge(consts_made, 1)
            cp(iojf[:, :], ioj[:, :])
            cp(base1[:, :], ioe[:, :])
            cp(thr[:, :], iok[:, :])
            cp(tokf[:, :], toki[:, :])
            for i in range(NT):
                cp(iota4[:, i, :], io4[:, :])
                cp(iota8[:, i, :], io8[:, :])
            link(v.memset(dec[:, :], 1.0))

            def x_norm(i):
                dve.wait_ge(rs1_made, i + 1)
                dve.wait_ge(xa_in, 16 * (i + 1))
                ts(xn, xa, rs1[:, 0:1], None, ALU.mult).then_inc(xn_made, 1)

            def modulate_xT(i, par):
                dve.wait_ge(xT_mm, i + 1)
                for k in range(KT):
                    last = ts(hT[par][:, k, :], T4[k // 4][:, k % 4, :], a1[:, k:k + 1], sh1[:, k:k + 1],
                              ALU.mult, ALU.add)
                last.then_inc(hT_made, 1)

            B = ex[:, A_QI, :, :]

            def logits(n):
                dve.wait_ge(lg_mm, n)
                tt(lg[:, bass.ds(n - 1, 1), :], OB[:, 0:NLOG].rearrange("p (a n) -> p a n", a=1),
                   brb[:, :].rearrange("p (a n) -> p a n", a=1), ALU.add).then_inc(ob_free, 1)

            def step(s, par, first=False, second=False, head=True, tail=True, nxt=True):
                if tail:
                    if not second:
                        logits(s - 1)
                    dve.wait_ge(sc_mm, s)
                    for j in range(4):
                        r = slice(32 * j, 32 * j + 32)
                        for half in range(2):
                            last = tt(pT4[r, :, half, r], SCO[half][r, 0, :, r],
                                      tri[r, :].rearrange("p (a t) -> p a t", a=1).broadcast_to([32, 2, 32]), ALU.mult)
                    last.then_inc(sc_diag, 1)
                if second:
                    ada(8)
                if head:
                    dve.wait_ge(za_ev, s + 1)
                    link(ts(la, zb, 0.0, None, ALU.min))
                    dve.wait_ge(ln_made, s + 1)
                    link(tt(la, la, lneg, ALU.subtract))
                    if not first:
                        dve.wait_ge(o_mm, s)
                    for cc in range(2):
                        last = v.tensor_tensor_scan(B[:, cc, :], ones[:, :], la[:, cc, :], 0.0, ALU.mult, ALU.add)
                    link(last)
                    full = [P, 2, P]
                    tt(ex[:, A_KD, :, :], B[:, :, P - 1:P].broadcast_to(full), B, ALU.subtract)
                    tt(ex[:, A_L64, :, 64:P], B[:, :, 64:P], B[:, :, 63:64].broadcast_to([P, 2, 64]), ALU.subtract)
                    tt(ex[:, A_L64, :, 0:64], B[:, :, 63:64].broadcast_to([P, 2, 64]), B[:, :, 0:64], ALU.subtract)
                    b64 = B.rearrange("p c (j t) -> p c j t", j=2)
                    l32 = ex[:, A_L32, :, :].rearrange("p c (j t) -> p c j t", j=2)
                    mid = b64[:, :, :, 31:32].broadcast_to([P, 2, 2, 32])
                    tt(l32[:, :, :, 32:64], b64[:, :, :, 32:64], mid, ALU.subtract)
                    tt(l32[:, :, :, 0:32], mid, b64[:, :, :, 0:32], ALU.subtract)
                    b32 = B.rearrange("p c (j t) -> p (c j) t", j=4)
                    ref = b32[:, :, 15:16].broadcast_to([P, 8, 32])
                    tt(ex[:, A_QD, :, :].rearrange("p c (j t) -> p (c j) t", j=4), b32, ref, ALU.subtract)
                    tt(ex[:, A_KG, :, :].rearrange("p c (j t) -> p (c j) t", j=4), ref, b32,
                       ALU.subtract).then_inc(ex_args, 1)
                if tail:
                    dve.wait_ge(st_mm, s)
                    for h in range(AH):
                        r0, cc = 64 * (h % 2), h // 2
                        rows, cols = slice(r0, r0 + 64), slice((h % 2) * P, (h % 2 + 1) * P)
                        last = stt(state[rows, cc, cols], state[rows, cc, cols], dec[rows, cc:cc + 1],
                                   SC1[rows, 256 * cc + (h % 2) * P:256 * cc + (h % 2 + 1) * P], ALU.mult, ALU.add)
                    last.then_inc(st_made, 1)
                if head:
                    dve.wait_ge(v_mm, s + 1)
                    cp(v_sb, PJ0[:, :]).then_inc(v_ev, 1)
                if first:
                    ada(4)
                if second:
                    ada(9)
                if tail:
                    dve.wait_ge(sg_mm, s)
                    for h in range(AH):
                        c = slice(h * P, (h + 1) * P)
                        stt(y_sb[:, c], SC0[:, c], bsT[:, h:h + 1], u_sb[:, c], ALU.add, ALU.mult)
                    dve.wait_ge(rso_made, s)
                    for h in range(AH):
                        c = slice(h * P, (h + 1) * P)
                        last = stt(y_sb[:, HALF + h * P:HALF + (h + 1) * P], OB[:, c], rso[:, h:h + 1], rg[:, c],
                                   ALU.mult, ALU.mult)
                    last.then_inc(y_made, 1)
                if second:
                    ada(10)
                if head:
                    dve.wait_ge(ex_exp, s + 1)
                    dve.wait_ge(qk_ev, s + 1)
                    if tail:
                        dve.wait_ge(st_made, s + 1)
                    link(cp(dec[:, :].rearrange("p (c a) -> p c a", a=1), B[:, :, P - 1:P]))
                    ex4 = [ex[:, a, :, :] for a in range(6)]
                    tt(ex4[A_QI], ex4[A_QI], qT, ALU.mult)
                    tt(ex4[A_KD], ex4[A_KD], kT, ALU.mult)
                    tt(ex4[A_L64][:, :, 64:P], ex4[A_L64][:, :, 64:P], qT[:, :, 64:P], ALU.mult)
                    tt(ex4[A_L64][:, :, 0:64], ex4[A_L64][:, :, 0:64], kT[:, :, 0:64], ALU.mult)
                    q4, k4 = [a.rearrange("p c (j t) -> p c j t", j=2) for a in (qT, kT)]
                    tt(l32[:, :, :, 32:64], l32[:, :, :, 32:64], q4[:, :, :, 32:64], ALU.mult)
                    tt(l32[:, :, :, 0:32], l32[:, :, :, 0:32], k4[:, :, :, 0:32], ALU.mult)
                    tt(ex4[A_QD], ex4[A_QD], qT, ALU.mult)
                    tt(ex4[A_KG], ex4[A_KG], kT, ALU.mult).then_inc(ex_made, 1)
                if second:
                    ada(11)
                    for piece in range(4, 8):
                        take(piece)
                    dve.wait_ge(ada_taken, len(PIECES))
                if nxt:
                    dve.wait_ge(xT_mm, s + 1)
                    x_norm(s + 1)
                if first:
                    ada(5)
                if tail:
                    dve.wait_ge(mix_mm, s)
                    dve.wait_ge(xb_in, 16 * s)
                    tt(y_sb[:, 0:HALF], SC0[:, :], g1b[:, 0:HALF], ALU.mult)
                    link(tt(y_sb[:, HALF:D], SC1[:, :], g1b[:, HALF:D], ALU.mult))
                    tt(xb, xb, y_sb, ALU.add).then_inc(x1_made, 1)
                if head:
                    dve.wait_ge(rsv_made, s + 1)
                    stt(av_sb, av_sb, rsv[:, 0:1], vgb[:, :], ALU.mult, ALU.mult).then_inc(vn_made, 1)
                if tail:
                    dve.wait_ge(rs2_made, s)
                    if second:
                        dve.wait_ge(route_in, 16 * 4)
                    else:
                        dve.wait_ge(xn2_out, 16 * (s - 1))
                    ts(xn2, xb, rs2[:, 0:1], None, ALU.mult).then_inc(xn2_made, 1)
                if nxt:
                    if not first:
                        dve.wait_ge(r_mm, s)
                    modulate_xT(s + 1, 1 - par)
                if tail:
                    dve.wait_ge(h2T_mm, s)
                    for k in range(KT):
                        last = ts(h2T[:, k, :], S4[k // 4][:, k % 4, :], a2[:, k:k + 1], sh2[:, k:k + 1],
                                  ALU.mult, ALU.add)
                    last.then_inc(h2T_ev, 1)
                if head:
                    if first:
                        dve.wait_ge(const_in, 16 * N_CONST)
                    dve.wait_ge(r_exp, s + 1)
                    link(ts(rtmp, rtmp, 1.0, None, ALU.add))
                    link(v.reciprocal(rtmp, rtmp))
                    link(tt(rtmp, rtmp, PJ1[:, :], ALU.mult))
                    tt(rg, rtmp, ogb[:, :], ALU.mult).then_inc(rg_made, 1)

            ada(0)
            ada(1)
            ada(2)
            x_norm(0)
            take(0)
            ada(3)
            take(1)
            v.memset(frs[:, :], 0.0).then_inc(st_made, 1)
            dve.wait_ge(ada_taken, 2)
            modulate_xT(0, 0)
            step(0, 0, first=True, tail=False)
            take(2)
            ada(6)
            take(3)
            ada(7)
            step(1, 1, second=True)
            n0 = chain.base + chain.n
            with dve.Fori(1, (NT - 2) // 2) as j:
                chain.base, chain.n = n0 + 2 * DVE_STEP * (j - 1), 0
                step(2 * j, 0)
                assert chain.n == DVE_STEP, ("DVE_STEP", chain.n)
                chain.base, chain.n = n0 + DVE_STEP + 2 * DVE_STEP * (j - 1), 0
                step(2 * j + 1, 1)
            chain.base, chain.n = n0 + (NT - 4) * DVE_STEP, 0
            step(NT - 2, 0)
            step(NT - 1, (NT - 1) % 2, nxt=False)
            step(NT, 0, head=False, nxt=False)
            logits(NT)

            def bc(a, n):
                return a.rearrange("p (i a) -> p i a", a=1).broadcast_to([P, NT, n])

            def first_max(vals, mx, oh, iota, tmp, n):
                link(v.tensor_reduce(mx, vals, AX.X, ALU.max))
                link(tt(tmp, vals, bc(mx, n), ALU.is_equal))
                link(stt(tmp, tmp, -64.0, iota, ALU.mult, ALU.add))
                link(v.tensor_reduce(gs8, tmp, AX.X, ALU.min))
                link(tt(oh, tmp, bc(gs8, n), ALU.is_equal))

            dve.wait_ge(ob_free, NT + 1)
            grp, exl = lg[:, :, 0:NG], lg[:, :, NG:NLOG].rearrange("p i (g e) -> p i g e", g=NG)
            first_max(grp, gm8, ohg, iota4[:, :, :], t4, NG)
            tt(t4, grp, bc(gm8, NG), ALU.subtract).then_inc(route_arg, 1)
            dve.wait_ge(route_arg, 1)
            for i in range(NT):
                last = tt(eprod[:, i, :, :], exl[:, i, :, :],
                          ohg[:, i, :].rearrange("p (g a) -> p g a", a=1).broadcast_to([P, NG, EPG]), ALU.mult)
            link(last)
            link(v.tensor_reduce(esel, eprod.rearrange("p i g e -> p i e g"), AX.X, ALU.add))
            first_max(esel, m1, oh1, iota8[:, :, :], t8, EPG)
            link(stt(e2, oh1, -BIG, esel, ALU.mult, ALU.add))
            first_max(e2, m2, oh2, iota8[:, :, :], t8, EPG)
            link(tt(t8, oh1, oh2, ALU.add))
            for i in range(NT):
                for oh, dst in ((oh1, full1), (oh2, full2), (t8, both.rearrange("p i (g e) -> p i g e", g=NG))):
                    last = tt(dst[:, i, :, :], ohg[:, i, :].rearrange("p (g a) -> p g a", a=1).broadcast_to([P, NG, EPG]),
                              oh[:, i, :].rearrange("p (a e) -> p a e", a=1).broadcast_to([P, NG, EPG]), ALU.mult)
            last.then_inc(both_made, 1)
            tt(rs_arg, m2, m1, ALU.subtract).then_inc(route_arg, 1)
            dve.wait_ge(route_exp, 1)
            link(v.tensor_reduce(pg, t4, AX.X, ALU.add))
            link(v.reciprocal(pg, pg))
            dve.wait_ge(route_exp, 2)
            link(ts(gt1[:, :], rs_arg, 1.0, None, ALU.add))
            link(v.reciprocal(gt1[:, :], gt1[:, :]))
            link(tt(gt1[:, :], gt1[:, :], pg, ALU.mult))
            tt(gt2[:, :], gt1[:, :], rs_arg, ALU.mult)
            dve.wait_ge(rank_mm, 1)
            tot = rank2
            cp(rank, SC0[:, 0:NT * NE].rearrange("p (i e) -> p i e", i=NT))
            cp(tot, SC1[:, 0:NT * NE].rearrange("p (i e) -> p i e", i=NT))
            link(v.memset(prev[:, 0, :], 0.0))
            for i in range(1, NT):
                link(tt(prev[:, i, :], prev[:, i - 1, :], tot[:, i - 1, :], ALU.add))
            link(tt(count, prev[:, NT - 1, :], tot[:, NT - 1, :], ALU.add))
            link(tt(rank, rank, prev, ALU.add))
            link(tt(cmpx, count.rearrange("p (e a) -> p e a", a=1).broadcast_to([P, NE, EPG]),
                    thr[:, :].rearrange("p (a k) -> p a k", a=1).broadcast_to([P, NE, EPG]), ALU.is_gt))
            link(v.tensor_reduce(nex, cmpx, AX.X, ALU.add))
            link(v.tensor_tensor_scan(ebi, ones[:, 0:NE], nex, 0.0, ALU.mult, ALU.add))
            link(tt(base2, ebi, nex, ALU.subtract))
            link(ts(base2, base2, float(P), float((NE - 1) * P), ALU.mult, ALU.add))
            link(tt(count, base1[:, :], base2, ALU.subtract))
            link(ts(prev, rank, float(P), None, ALU.is_lt))
            link(tt(prev, prev, count.rearrange("p (a e) -> p a e", a=1).broadcast_to([P, NT, NE]), ALU.mult))
            link(tt(rank, rank, prev, ALU.add))
            link(tt(rank, rank, base2.rearrange("p (a e) -> p a e", a=1).broadcast_to([P, NT, NE]), ALU.add))
            for j, full in enumerate((full1, full2)):
                link(tt(rank2, rank, full.rearrange("p i g e -> p i (g e)"), ALU.mult))
                link(v.tensor_reduce(sl[:, j, :], rank2, AX.X, ALU.add))
            cp(sli[:, :, :], sl).then_inc(slots_made, 1)
            link(tt(cmpj, iojf[:, :].rearrange("p (j a) -> p j a", a=1).broadcast_to([P, MAXEXTRA, NE]),
                    ebi.rearrange("p (a e) -> p a e", a=1).broadcast_to([P, MAXEXTRA, NE]), ALU.is_ge))
            link(v.tensor_reduce(exf, cmpj, AX.X, ALU.add))
            link(ts(exf, exf, float(NE - 1), None, ALU.min))
            cp(exi[:, :], exf)
            cp(nxi[:, :], ebi[:, NE - 1:NE]).then_inc(extra_made, 1)
            dve.wait_ge(table_mm, 1)
            cp(idx[:, :], SC2[:, 0:NBLK]).then_inc(idx_made, 1)

            def modulate_rows(b, par):
                dve.wait_ge(xg_mm, b + 1)
                for k in range(KT):
                    last = ts(xT[par][:, k, :], T4[k // 4][:, k % 4, :], a2[:, k:k + 1], sh2[:, k:k + 1],
                              ALU.mult, ALU.add)
                last.then_inc(xg_ev, 1)

            def hidden(b, first=False):
                dve.wait_ge(silu_made, b + 1)
                if not first:
                    dve.wait_ge(hidT_mm, b)
                tt(hid, silu_sb, PJ1[:, :], ALU.mult).then_inc(hid_made, 1)

            def gated_rows(b, r, par, first=False):
                dve.wait_ge(dn_mm, b + 1)
                if not first:
                    dve.wait_ge(y_out[par], 16 * r)
                tt(yb[par][:, 0:HALF], SC0[:, :], g2b[:, 0:HALF], ALU.mult)
                tt(yb[par][:, HALF:D], SC1[:, :], g2b[:, HALF:D], ALU.mult).then_inc(dn_ev, 1)

            def hidden_T(b):
                dve.wait_ge(hidT_mm, b + 1)
                cp(hidT, SC2[:, :].rearrange("p (k t) -> p k t", k=FKT)).then_inc(hidT_ev, 1)

            modulate_rows(0, 0)
            hidden(0, True)
            modulate_rows(1, 1)
            hidden_T(0)

            def block_step(b, r, par, first=False, nxt=True):
                hidden(b)
                if nxt:
                    modulate_rows(b + 1, 1 - par)
                gated_rows(b - 1, r - 1 + par, 1 - par, first)
                hidden_T(b)

            block_step(1, 0, 1, first=True)
            block_step(2, 1, 0, first=True)
            block_step(3, 1, 1)
            with dve.Fori(2, NE // 2 - 1) as q:
                block_step(2 * q, q, 0)
                block_step(2 * q + 1, q, 1)
            block_step(NE - 2, NE // 2 - 1, 0)
            block_step(NE - 1, NE // 2 - 1, 1, nxt=False)
            gated_rows(NE - 1, NE // 2 - 1, 1)
            dve.wait_ge(extra_made, 1)
            n_extra = dve.value_load(nxi[0:1, 0:1], min_val=0, max_val=MAXEXTRA)
            with dve.Fori(0, MAXEXTRA // 2) as q:
                for par in range(2):
                    with dve.If(n_extra > 2 * q + par):
                        b, r = 2 * q + par + NE, q + NE // 2
                        modulate_rows(b, par)
                        hidden(b)
                        hidden_T(b)
                        gated_rows(b, r, par)
            dve.nop().then_inc(experts_left, 1)

            dve.wait_ge(fgb_in, 16)
            dve.wait_ge(fx_in, 16)

            def combine(i):
                dve.wait_ge(y1_scaled, i + 1)
                link(stt(fy1[i], fy2[i], gt2[:, i:i + 1], fy1[i], ALU.mult, ALU.add))
                tt(fy1[i], fy1[i], fx[:, i, :], ALU.add).then_inc(x2_made, 1)

            def finish(i):
                dve.wait_ge(frs_made, i // 2 + 1)
                stt(fy1[i], fy1[i], frs[:, i:i + 1], fgb[:, :], ALU.mult, ALU.mult).then_inc(fo_made, 1)

            for i in range(NT + 3):
                if i < NT:
                    combine(i)
                if i >= 3:
                    finish(i - 3)


_INS = ["x", "c", "w_ada", "b_ada", "norm1_gain", "norm2_gain", "w_in", "a_v_gain", "a_w_s", "a_b_s", "b_w_alpha",
        "b_b_alpha", "b_out_gain", "w_out", "w_group", "b_group", "w_router", "b_router", "w1", "w3", "w2",
        "final_gain"]


def kernel(**inputs):
    import numpy as np
    import concourse.bacc as bacc
    from concourse.bass_utils import run_bass_kernel_spmd

    nc = bacc.Bacc("TRN2", target_bir_lowering=False, num_devices=1)
    arrays, args = {}, []
    for name in _INS:
        a = np.ascontiguousarray(inputs[name])
        arrays[f"in_{name}"] = a
        args.append(nc.dram_tensor(f"in_{name}", a.shape, mybir.dt.from_np(a.dtype), kind="ExternalInput").ap())
    args.append(nc.dram_tensor("out_0", (1, SEQ, D), F32, kind="ExternalOutput").ap())
    trunk(nc, *args)
    result = run_bass_kernel_spmd(nc, [arrays], core_ids=[0])
    return result.results[0]["out_0"]
```

```python
import concourse.bass as bass
from concourse import mybir
from contextlib import ExitStack

F32 = mybir.dt.float32
F32R = mybir.dt.float32r
I32 = mybir.dt.int32
ACT = mybir.ActivationFunctionType
ALU = mybir.AluOpType
AX = mybir.AxisListType

P = 128
D = 1024
SEQ = 1024
NT = SEQ // P
KT = D // P
HALF = 512
AH = 4
BK = 64
RANK = 16
TAU = 16.0
C_U, C_AV, C_Q, C_K, C_V, C_R, C_A, P_IN = 0, 512, 1024, 1280, 1536, 2048, 2560, 2576
NG, EPG, NE = 4, 8, 32
FE = 512
FKT = FE // P
MAXEXTRA = 2 * SEQ // P
NBLK = NE + MAXEXTRA
EPS = 1e-6
NLOG = NG + NE
BIG = 1e30
(A_QI, A_KD, A_L64, A_L32, A_QD, A_KG) = range(6)


def trunk(nc, x, c, w_ada, b_ada, norm1_gain, norm2_gain, w_in, a_v_gain, a_w_s, a_b_s, b_w_alpha,
          b_b_alpha, b_out_gain, w_out, w_group, b_group, w_router, b_router, w1, w3, w2,
          final_gain, out):
    x1_dram = nc.dram_tensor("x1_scratch", (SEQ, D), F32, kind="Internal").ap()
    xn2_dram = nc.dram_tensor("xn2_scratch", (SEQ, D), F32, kind="Internal").ap()
    y_dram = nc.dram_tensor("expert_out_scratch", (NBLK * P, D), F32, kind="Internal").ap()

    ctx = ExitStack()
    with ctx:
        def sb(name, shape, dt=F32):
            return ctx.enter_context(nc.sbuf_tensor(name, shape, dt))

        def sem(name):
            return ctx.enter_context(nc.semaphore(name))

        g1b = sb("gate1_rows", [P, D])
        g2b = sb("gate2_rows", [P, D])
        fgb = g1b
        vgb = sb("v_gain_rows", [P, HALF])
        ogb = sb("out_gain_rows", [P, HALF])
        wsT = sb("spatial_T", [P, AH, P])
        wal = sb("w_alpha", [RANK, 2 * P])
        alT = sb("a_low_T", [RANK, P])
        wr = sb("w_route", [P, KT, NLOG])
        brb = sb("b_route_rows", [P, NLOG])
        ident = sb("ident", [P, P])
        lstrict = sb("strict_before", [P, P])
        tri = sb("tri32", [P, 32])
        ones = sb("ones", [P, P])
        zeros = sb("zeros", [P, P])
        cT = sb("c_cols", [P, KT])
        cE = sb("c_exp", [P, KT])
        bcols = sb("b_ada_cols", [P, 4, KT])
        gain1 = sb("gain1", [P, KT])
        gain2 = sb("gain2", [P, KT])
        a1 = sb("a1", [P, KT])
        sh1 = sb("sh1", [P, KT])
        a2 = sb("a2", [P, KT])
        sh2 = sb("sh2", [P, KT])
        bal = sb("b_alpha_cols", [P, 2])
        bsT = sb("b_spatial_cols", [P, AH])
        eps = sb("eps", [P, 1])
        junk = sb("unused_squares", [P, D], mybir.dt.bfloat16)
        dec = sb("state_decay", [P, 2])
        ss1 = sb("ss1", [P, 1])
        rs1 = sb("rs1", [P, 1])
        ssv = sb("ssv", [P, 1])
        rsv = sb("rsv", [P, 1])
        sso = sb("sso", [P, AH])
        rso = sb("rso", [P, AH])
        ss2 = sb("ss2", [P, 1])
        rs2 = sb("rs2", [P, 1])
        lg = sb("logits", [P, NT, NLOG])
        iota4 = sb("iota4", [P, NT, NG])
        iota8 = sb("iota8", [P, NT, EPG])
        io4 = sb("io4", [P, NG], I32)
        io8 = sb("io8", [P, EPG], I32)
        ioj = sb("ioj", [P, MAXEXTRA], I32)
        iojf = sb("iojf", [P, MAXEXTRA])
        ioe = sb("ioe", [P, NE], I32)
        base1 = sb("base1", [P, NE])
        iok = sb("iok", [P, EPG], I32)
        thr = sb("thr", [P, EPG])
        toki = sb("token_id_i", [P, NT], I32)
        tokf = sb("token_id", [P, NT])
        gt1 = sb("gate_first", [P, NT])
        gt2 = sb("gate_second", [P, NT])
        sli = sb("slot_i", [P, 2, NT], I32)
        place_i = sb("place_i", [P, 2, NT], I32)
        exi = sb("extra_expert", [P, MAXEXTRA], I32)
        nxi = sb("n_extra", [P, 3], I32)
        iota_slot = sb("iota_slot", [P, P])
        iota_blk = sb("iota_blk", [P, NBLK])
        idx = sb("block_tokens", [P, NBLK], I32)
        idc = [sb("block_col0", [P, 1], I32), sb("block_col1", [P, 1], I32)]
        idp = sb("block_col_copy", [P, 1], I32)
        fss = sb("fss", [P, NT])
        frs = sb("frs", [P, NT])

        WORK = 17 * 1024
        with nc.sbuf_tensor("mixer_weights", [P, KT * P_IN + KT * D], F32) as big, \
                nc.sbuf_tensor("mixer_tiles", [P, WORK], F32) as work:
            pass
        with nc.sbuf_tensor("iota_i", [P, P + NBLK], I32) as iota_i:
            pass
        win = big[:, 0:KT * P_IN].rearrange("p (k n) -> p k n", k=KT)
        wout = big[:, KT * P_IN:KT * P_IN + KT * D].rearrange("p (k n) -> p k n", k=KT)
        ada_w = big[:, KT * P_IN:KT * P_IN + KT * D].rearrange("p (b k n) -> p b k n", b=2, k=KT)
        EW = KT * FE

        at = [0]

        def carve(words):
            at[0] += words
            assert at[0] <= WORK, at[0]
            return work[:, at[0] - words:at[0]]

        xa = carve(D)
        xn = carve(D)
        xb = carve(D)
        hT = [carve(D).rearrange("p (k t) -> p k t", k=KT) for _ in range(2)]
        u_sb = carve(HALF)
        av_sb = carve(HALF)
        v_sb = carve(HALF)
        rg = carve(HALF)
        rtmp = carve(HALF)
        y_sb = carve(D)
        yT = carve(D).rearrange("p (k t) -> p k t", k=KT)
        xn2 = carve(D)
        h2T = yT
        qT = carve(2 * P).rearrange("p (c t) -> p c t", c=2)
        kT = carve(2 * P).rearrange("p (c t) -> p c t", c=2)
        az = carve(2 * P).rearrange("p (c t) -> p c t", c=2)
        zb = carve(2 * P).rearrange("p (c t) -> p c t", c=2)
        lneg = carve(2 * P).rearrange("p (c t) -> p c t", c=2)
        la = carve(2 * P).rearrange("p (c t) -> p c t", c=2)
        ex = carve(6 * 2 * P).rearrange("p (a c t) -> p a c t", a=6, c=2)
        pT = carve(AH * P).rearrange("p (h t) -> p h t", h=AH)
        pT4 = pT.rearrange("p (c l) t -> p c l t", c=2)
        kdT = carve(2 * P).rearrange("p (c k) -> p c k", c=2)
        state = carve(2 * 2 * P).rearrange("p (c v) -> p c v", c=2)
        brow = yT.rearrange("p k t -> p (k t)")[0:1, :]
        ws_raw = rtmp.rearrange("p (h s) -> p h s", h=AH)
        raw = sb("expert_weights", [P, 3, EW])
        w_hi = sb("expert_weights_high", [P, 3, EW], F32R)
        w_lo = sb("expert_weights_low", [P, 3, EW], F32R)
        xr_t = sb("token_rows", [P, 2, D])
        xr = [xr_t[:, i, :] for i in range(2)]
        xT = sb("rows_T", [P, KT, P])
        x_hi = sb("rows_T_high", [P, KT, P], F32R)
        x_lo = sb("rows_T_low", [P, KT, P], F32R)
        yb_t = sb("expert_out", [P, 2, D])
        yb = [yb_t[:, i, :] for i in range(2)]
        silu_sb = sb("silu", [P, FE])[:, :]
        hid = sb("hidden", [P, FE])[:, :]
        h_hi = sb("hidden_T_high", [P, FKT, P], F32R)
        h_lo = sb("hidden_T_low", [P, FKT, P], F32R)
        fx = big[:, 0:NT * D].rearrange("p (i n) -> p i n", i=NT)
        fy1 = [big[:, (NT + 2 * i) * D:(NT + 2 * i + 1) * D] for i in range(NT)]
        fy2 = [big[:, (NT + 2 * i + 1) * D:(NT + 2 * i + 2) * D] for i in range(NT)]
        B_WORDS = KT * P_IN + KT * D
        spare, limit = [8 * EW - B_WORDS], [9 * EW - B_WORDS]

        def route(*shape):
            words = 1
            for d in shape:
                words *= d
            spare[0] += words
            assert spare[0] <= limit[0], spare[0]
            v = work[:, spare[0] - words:spare[0]]
            if len(shape) == 2:
                v = v.rearrange("p (a b) -> p a b", a=shape[0])
            if len(shape) == 3:
                v = v.rearrange("p (a b c) -> p a b c", a=shape[0], b=shape[1])
            return v

        t4 = route(NT, NG)
        gs8 = route(NT)
        gm8 = route(NT)
        pg = route(NT)
        ohg = route(NT, NG)
        esel = route(NT, EPG)
        eprod = route(NT, NG, EPG)
        e2 = route(NT, EPG)
        t8 = route(NT, EPG)
        oh1 = route(NT, EPG)
        oh2 = route(NT, EPG)
        m1 = route(NT)
        m2 = route(NT)
        full1 = route(NT, NG, EPG)
        full2 = route(NT, NG, EPG)
        both = route(NT, NE)
        rank = route(NT, NE)
        rank2 = route(NT, NE)
        prev = route(NT, NE)
        count = route(NE)
        nex = route(NE)
        ebi = route(NE)
        base2 = route(NE)
        cmpx = route(NE, EPG)
        cmpj = route(MAXEXTRA, NE)
        sl = route(2, NT)
        exf = route(MAXEXTRA)
        n_even_odd = route(2)
        rs_arg = route(NT)
        place = route(2, NT)
        first_slot = route(2, NT)
        spare[0], limit[0] = 9 * EW + 5 * D - B_WORDS, 9 * EW + 7 * D + 2 * FE - B_WORDS
        place_hot = route(2 * NT, P)
        block_token = route(2 * NT, NBLK)

        def bank(name):
            return ctx.enter_context(nc.psum_tensor(name, [P, HALF], F32))

        PJ0, PJ1, T0, T1, SC0, SC1, SC2, OB = [bank(n) for n in
                                              ("PJ0", "PJ1", "T0", "T1", "SC0", "SC1", "SC2", "OB")]
        T4 = [T0[:, :].rearrange("p (k t) -> p k t", k=4), T1[:, :].rearrange("p (k t) -> p k t", k=4)]
        S4 = [SC0[:, :].rearrange("p (k t) -> p k t", k=4), SC1[:, :].rearrange("p (k t) -> p k t", k=4)]
        QK = PJ0[:, :].rearrange("p (c t) -> p c t", c=4)
        ALOW = PJ1[0:RANK, 0:P]
        ZA = PJ1[:, P:3 * P].rearrange("p (c t) -> p c t", c=2)
        SCO = [a[:, :].rearrange("p (l c t) -> p l c t", l=2, c=2) for a in (SC0, SC1)]
        L64 = [a[0:64, 0:P].rearrange("p (c t) -> p c t", c=2) for a in (SC2, OB)]
        KDT = SC2[:, 256:512].rearrange("p (c k) -> p c k", c=2)
        mod_sum = [xn2, y_sb, g1b[:, :], xn2, xb, g2b[:, :]]
        GATES = (2, 5)
        PIECES = [(0, 0), (1, 0), (2, 0), (2, 1), (3, 0), (4, 0), (5, 0), (5, 1)]
        N_EARLY = 4
        ada_bufs = [ada_w[:, 0, :, :], ada_w[:, 1, :, :],
                    work[:, 3 * D:3 * D + EW].rearrange("p (k n) -> p k n", k=KT)]

        def ada_place(n):
            if n < 3:
                return n, 1, 0
            return (n - 1) % 2, (n - 3) // 2 + 2, (n - 2 if n < 5 else n - 1)


        const_in = sem("const_in")
        norms_in = sem("norms_in")
        adaw_in = [sem("adaw_in0"), sem("adaw_in1"), sem("adaw_in2")]
        win_in = [sem("win_in_%s" % n) for n in ("qk", "ra", "v", "av", "u")]
        route_in = sem("route_in")
        brow_in = sem("brow_in")
        wout_in = [sem("wout_in_low_k"), sem("wout_in_high_k")]
        consts_made = sem("consts_made")
        spatial_made = sem("spatial_made")
        cact_made = sem("cact_made")
        ada_sum = sem("ada_sum")
        ada_spread = sem("ada_spread")
        ada_taken = sem("ada_taken")
        ws_mm = sem("ws_mm")
        xa_in = sem("xa_in")
        xb_in = sem("xb_in")
        rs1_made = sem("rs1_made")
        xn_made = sem("xn_made")
        xT_mm = sem("xT_mm")
        hT_made = sem("hT_made")
        qk_mm = sem("qk_mm")
        qk_ev = sem("qk_ev")
        alow_mm = sem("alow_mm")
        alow_ev = sem("alow_ev")
        za_mm = sem("za_mm")
        za_ev = sem("za_ev")
        ln_made = sem("ln_made")
        ex_args = sem("ex_args")
        ex_exp = sem("ex_exp")
        ex_made = sem("ex_made")
        sc_mm = sem("sc_mm")
        sc_off = sem("sc_off")
        sc_diag = sem("sc_diag")
        kdt_mm = sem("kdt_mm")
        kdt_ev = sem("kdt_ev")
        o_mm = sem("o_mm")
        st_mm = sem("st_mm")
        st_made = sem("st_made")
        sg_mm = sem("sg_mm")
        v_mm = sem("v_mm")
        v_ev = sem("v_ev")
        av_mm = sem("av_mm")
        av_ev = sem("av_ev")
        vn_made = sem("vn_made")
        rsv_made = sem("rsv_made")
        u_mm = sem("u_mm")
        u_ev = sem("u_ev")
        r_mm = sem("r_mm")
        r_exp = sem("r_exp")
        rg_made = sem("rg_made")
        rso_made = sem("rso_made")
        y_made = sem("y_made")
        yT_mm = sem("yT_mm")
        yT_ev = sem("yT_ev")
        mix_mm = sem("mix_mm")
        x1_made = sem("x1_made")
        rs2_made = sem("rs2_made")
        xn2_made = sem("xn2_made")
        x1_out = sem("x1_out")
        xn2_out = sem("xn2_out")
        h2T_mm = sem("h2T_mm")
        h2T_ev = sem("h2T_ev")
        lg_mm = sem("lg_mm")
        ob_free = sem("ob_free")
        dve_done = sem("dve_done")
        act_done = sem("act_done")
        pool_done = sem("pool_done")
        both_made = sem("both_made")
        rank_mm = sem("rank_mm")
        route_arg = sem("route_arg")
        route_exp = sem("route_exp")
        slots_made = sem("slots_made")
        table_mm = sem("table_mm")
        idx_made = sem("idx_made")
        extra_made = sem("extra_made")
        names = ("w1", "w3", "w2")
        raw_in = [[sem(n + "_in_low_k"), sem(n + "_in_high_k")] for n in names]
        hi_made = [sem(n + "_high_made") for n in names]
        lo_made = [sem(n + "_low_made") for n in names]
        w_used = [sem(n + "_used") for n in names]
        x_hi_made = sem("x_hi_made")
        x_lo_made = sem("x_lo_made")
        h_hi_made = sem("h_hi_made")
        idc_made = sem("idc_made")
        xg_in = [sem("xg_in0"), sem("xg_in1")]
        xg_mm = sem("xg_mm")
        xg_ev = sem("xg_ev")
        up_mm = w_used[1]
        silu_made = sem("silu_made")
        hid_made = sem("hid_made")
        hidT_mm = sem("hidT_mm")
        hidT_ev = sem("hidT_ev")
        dn_mm = w_used[2]
        dn_ev = sem("dn_ev")
        y_zero = sem("y_zero")
        y_out = [sem("y_out0"), sem("y_out1")]
        fy_in = [sem("fy_in%d" % i) for i in range(NT)]
        y1_scaled = sem("y1_scaled")
        fx_in = sem("fx_in")
        experts_left = sem("experts_left")
        fgb_in = sem("fgb_in")
        x2_made = sem("x2_made")
        rms_made = sem("rms_made")
        fo_made = sem("fo_made")
        out_out = sem("out_out")
        block = ctx.enter_context(nc.Block())

        class Chain:

            def __init__(self, eng, done):
                self.eng, self.done, self.base, self.n = eng, done, 0, 0

            def link(self, ins):
                self.n += 1
                ins.then_inc(self.done, 1)
                self.eng.wait_ge(self.done, self.base + self.n)

        N_CONST = 6
        DVE_STEP = 8
        ACT_STEP = 14

        @block.sync
        def _(sp):
            sp.dma_start(cT[:, :], c.rearrange("a (p k) -> (a p) k", k=KT)).then_inc(norms_in, 16)
            sp.dma_start(gain1[:, :], norm1_gain.rearrange("a (p k) -> (a p) k", k=KT)).then_inc(norms_in, 16)
            sp.dma_start(gain2[:, :], norm2_gain.rearrange("a (p k) -> (a p) k", k=KT)).then_inc(norms_in, 16)
            ada_v = w_ada[0, :, :].rearrange("(p k) n -> p k n", k=KT)
            with nc.allow_non_contiguous_dma(reason="small constants"):
                for m, vec in enumerate((0, 1, 3, 4)):
                    sp.dma_start(bcols[:, m, :], b_ada[0, vec * D:(vec + 1) * D].rearrange("(p k) -> p k", k=KT)
                                 ).then_inc(norms_in, 16)

            def load_ada(n):
                buf, _, before = ada_place(n)
                if before:
                    sp.wait_ge(ada_sum, before)
                sp.dma_start(ada_bufs[buf], ada_v[:, :, n * HALF:(n + 1) * HALF]).then_inc(adaw_in[buf], 16)

            def load_brow(v):
                sp.dma_start(brow, b_ada[0:1, v * D:(v + 1) * D]).then_inc(brow_in, 16)

            load_ada(0)
            load_ada(1)
            sp.dma_start(xa[:, :], x[0, 0:P, :]).then_inc(xa_in, 16)
            load_ada(2)
            load_ada(3)
            win_v = w_in[0, :, :].rearrange("(p k) n -> p k n", k=KT)
            for n, (c0, c1) in enumerate(((C_Q, C_V), (C_R, P_IN), (C_V, C_R), (C_AV, C_Q), (C_U, C_AV))):
                sp.dma_start(win[:, :, c0:c1], win_v[:, :, c0:c1]).then_inc(win_in[n], 16)
                if n == 0:
                    with nc.allow_non_contiguous_dma(reason="small constants"):
                        sp.dma_start(bal[:, :], b_b_alpha[0, :].rearrange("(c p) -> p c", p=P)).then_inc(const_in, 16)
                        sp.dma_start(bsT[:, :], a_b_s[0, :, :].rearrange("h t -> t h")).then_inc(const_in, 16)
                    sp.dma_start(wal[:, :], b_w_alpha[0, :, :]).then_inc(const_in, 16)
                if n == 1:
                    sp.dma_start(ws_raw[:, :, :], a_w_s[0, :, :, :].rearrange("h t s -> t h s")).then_inc(const_in, 16)
                    sp.dma_start(vgb[:, :], a_v_gain[0, :].partition_broadcast(P)).then_inc(const_in, 16)
                    sp.dma_start(ogb[:, :], b_out_gain[0, :].partition_broadcast(P)).then_inc(const_in, 16)
            load_brow(2)
            sp.wait_ge(xn_made, 1)
            sp.dma_start(xa[:, :], x[0, P:2 * P, :]).then_inc(xa_in, 16)
            for n in range(N_EARLY, 12):
                load_ada(n)
                if n == 5:
                    with nc.allow_non_contiguous_dma(reason="small constants"):
                        sp.dma_start(wr[:, :, 0:NG], w_group[0, :, :].rearrange("(p k) n -> p k n", k=KT)).then_inc(route_in, 16)
                        sp.dma_start(wr[:, :, NG:NLOG], w_router[0, :, :].rearrange("(p k) n -> p k n", k=KT)).then_inc(route_in, 16)
                    sp.dma_start(brb[:, 0:NG], b_group[0, :].partition_broadcast(P)).then_inc(route_in, 16)
                    sp.dma_start(brb[:, NG:NLOG], b_router[0, :].partition_broadcast(P)).then_inc(route_in, 16)
                if n == 10:
                    sp.wait_ge(ada_spread, 4)
                    load_brow(5)
            wout_v = w_out[0, :, :].rearrange("(p k) n -> p k n", k=KT)
            for n in (10, 11):
                half = ada_place(n)[0]
                ks = slice(half * KT // 2, (half + 1) * KT // 2)
                sp.wait_ge(ada_sum, n + 1)
                sp.dma_start(wout[:, ks, :], wout_v[:, ks, :]).then_inc(wout_in[half], 16)
            sp.wait_ge(ada_spread, 6)
            sp.dma_start(xb[:, :], x[0, 0:P, :]).then_inc(xb_in, 16)

            def load_xa(i):
                sp.wait_ge(xn_made, i)
                sp.dma_start(xa[:, :], x[0, bass.ts(i, P), :]).then_inc(xa_in, 16)

            def tile_out(i, more):
                sp.wait_ge(x1_made, i + 1)
                sp.dma_start(x1_dram[bass.ts(i, P), :], xb[:, :]).then_inc(x1_out, 16)
                sp.wait_ge(xn2_made, i + 1)
                sp.dma_start(xn2_dram[bass.ts(i, P), :], xn2[:, :]).then_inc(xn2_out, 16)
                if more:
                    sp.wait_ge(x1_out, 16 * (i + 1))
                    sp.dma_start(xb[:, :], x[0, bass.ts(i + 1, P), :]).then_inc(xb_in, 16)

            with sp.Fori(0, NT - 2) as i:
                load_xa(i + 2)
                tile_out(i, True)
            tile_out(NT - 2, True)
            tile_out(NT - 1, False)

            def weights(n, b, e, first=False):
                k = KT if n < 2 else FKT
                src = (w1, w3, w2)[n][0, e, :, :].rearrange("(p k) n -> p k n", k=k)
                dst = raw[:, n, :].rearrange("p (k n) -> p k n", k=k)
                for h in range(2):
                    if not first:
                        sp.wait_ge(lo_made[n], 2 * b - 1 + h)
                    ks = slice(h * k // 2, (h + 1) * k // 2)
                    sp.dma_start(dst[:, ks, :], src[:, ks, :]).then_inc(raw_in[n][h], 16)

            sp.wait_ge(mix_mm, NT)
            for n in range(3):
                weights(n, 0, 0, first=True)
            sp.wait_ge(x1_made, NT)
            sp.dma_start(fgb[:, :], final_gain.partition_broadcast(P)).then_inc(fgb_in, 16)
            weights(0, 1, 1)
            weights(1, 1, 1)
            with sp.Fori(2, NE) as b:
                weights(0, b, b)
                weights(1, b, b)
                weights(2, b - 1, b - 1)
            weights(2, NE - 1, NE - 1)
            sp.wait_ge(extra_made, 1)
            n_extra = sp.value_load(nxi[0:1, 0:1], min_val=0, max_val=MAXEXTRA)
            with sp.Fori(0, MAXEXTRA // 4) as quad:
                with sp.If(n_extra > 4 * quad):
                    with sp.Fori(0, 4) as i:
                        j = 4 * quad + i
                        with sp.If(n_extra > j):
                            e = sp.value_load(exi[0:1, bass.ds(j, 1)], min_val=0, max_val=NE - 1)
                            for n in range(3):
                                weights(n, j + NE, e)
            sp.wait_ge(x1_out, 16 * NT)
            for n in range(3):
                sp.wait_ge(lo_made[n], 2 * n_extra + 2 * NE)
            sp.dma_start(fx, x1_dram.rearrange("(i p) n -> p i n", p=P)).then_inc(fx_in, 16)
            sp.wait_ge(out_out, 16 * NT)

        @block.gpsimd
        def _(pool):
            g = nc.gpsimd
            chain = Chain(pool, pool_done)
            link = chain.link
            g.memset(eps[:, :], EPS)
            g.memset(state, 0.0)
            g.memset(pT, 0.0)
            g.memset(ones[:, :], 1.0)
            g.memset(zeros[:, :], 0.0)
            link(g.memset(ident[:, :], 1.0))
            link(g.affine_select(out=ident[:, :], in_=ident[:, :], compare_op=ALU.is_equal, fill=0.0,
                                 base=0, pattern=[[-1, P]], channel_multiplier=1))
            link(g.affine_select(out=lstrict[:, :], in_=ones[:, :], compare_op=ALU.is_gt, fill=0.0,
                                 base=0, pattern=[[1, P]], channel_multiplier=-1))
            for j in range(4):
                link(g.affine_select(out=tri[32 * j:32 * j + 32, :], in_=ones[32 * j:32 * j + 32, 0:32],
                                     compare_op=ALU.is_ge, fill=0.0, base=0, pattern=[[1, 32]],
                                     channel_multiplier=-1))
            g.iota(io4[:, :], [[1, NG]], 0, 0)
            g.iota(io8[:, :], [[1, EPG]], 0, 0)
            g.iota(ioj[:, :], [[1, MAXEXTRA]], 0, 0)
            g.iota(ioe[:, :], [[P, NE]], 0, 0)
            g.iota(iok[:, :], [[P, EPG]], P, 0)
            g.iota(iota_i[:, 0:P], [[1, P]], 0, 0)
            g.iota(iota_i[:, P:P + NBLK], [[P, NBLK]], 0, 0)
            g.iota(toki[:, :], [[P, NT]], 0, 1).then_inc(consts_made, 1)
            pool.wait_ge(const_in, 16 * N_CONST)
            g.affine_select(out=ws_raw, in_=ws_raw, compare_op=ALU.is_ge, fill=0.0, base=0,
                            pattern=[[0, AH], [-1, P]], channel_multiplier=1).then_inc(spatial_made, 1)
            zero_src = zeros[:, :].rearrange("p (m n) -> p m n", m=1).broadcast_to([P, 4 * D // P, P])
            for j in range(MAXEXTRA // 4):
                pool.wait_ge(xn_made, j + 4)
                dst = y_dram[(NE + 4 * j) * P:(NE + 4 * j + 4) * P, :]
                pool.dma_start(dst.rearrange("(p b) (m n) -> p (b m) n", p=P, n=P), zero_src).then_inc(y_zero, 16)
            pool.wait_ge(x1_out, 16 * NT)
            pool.wait_ge(lg_mm, NT)
            for n in range(2):
                for h in range(2):
                    half = slice(h * EW // 2, (h + 1) * EW // 2)
                    pool.wait_ge(hi_made[n], h + 1)
                    g.tensor_tensor(w_lo[:, n, half], raw[:, n, half], w_hi[:, n, half].bitcast(F32), ALU.subtract
                                    ).then_inc(lo_made[n], 1)

            def gather(b, r, par, first):
                if not first:
                    pool.wait_ge(xg_mm, b - 1)
                    pool.wait_ge(xg_in[par], 16 * r)
                g.tensor_copy(idc[par][:, :], idx[:, bass.ds(b, 1)]).then_inc(idc_made, 1)
                pool.wait_ge(idc_made, b + 1)
                g.tensor_tensor(idp[:, :], idc[par][:, :], idc[par][:, :], ALU.add)
                pool.indirect_dma_start(out=xr[par], out_offset=None, in_=xn2_dram,
                                        in_offset=bass.IndirectOffsetOnAxis(ap=idc[par][:, 0:1], axis=0)
                                        ).then_inc(xg_in[par], 16)

            pool.wait_ge(idx_made, 1)
            pool.wait_ge(xn2_out, 16 * NT)
            pool.wait_ge(x1_out, 16 * NT)
            gather(0, 0, 0, True)
            gather(1, 0, 1, True)
            with pool.Fori(1, NE // 2) as q:
                gather(2 * q, q, 0, False)
                gather(2 * q + 1, q, 1, False)
            pool.wait_ge(extra_made, 1)
            n_extra = pool.value_load(nxi[0:1, 0:1], min_val=0, max_val=MAXEXTRA)
            with pool.Fori(0, MAXEXTRA // 4) as quad:
                with pool.If(n_extra > 4 * quad):
                    with pool.Fori(0, 2) as pair:
                        q = 2 * quad + pair
                        for par in range(2):
                            with pool.If(n_extra > 2 * q + par):
                                gather(2 * q + par + NE, q + NE // 2, par, False)
            pool.wait_ge(experts_left, 3)
            for i in range(NT):
                for j, dst in enumerate((fy1, fy2)):
                    pool.indirect_dma_start(out=dst[i], out_offset=None, in_=y_dram,
                                            in_offset=bass.IndirectOffsetOnAxis(ap=sli[:, j, i:i + 1], axis=0)
                                            ).then_inc(fy_in[i], 16)

        @block.tensor
        def _(pe):
            mm = nc.tensor.matmul
            tp = nc.tensor.transpose
            pe.wait_ge(consts_made, 1)

            def spread(piece):
                v, hf = PIECES[piece]
                pe.wait_ge(ada_sum, 2 * v + (hf + 1 if v in GATES else 2))
                if piece:
                    pe.wait_ge(ada_taken, piece)
                if v in GATES:
                    half = slice(hf * HALF, (hf + 1) * HALF)
                    pe.wait_ge(brow_in, 16 * (GATES.index(v) + 1))
                    mm(SC2[:, :], ones[:, :], mod_sum[v][:, half], start=True, stop=False)
                    mm(SC2[:, :], ones[0:1, :], brow[:, half], start=False, stop=True).then_inc(ada_spread, 1)
                else:
                    cols = mod_sum[v].rearrange("q (p k) -> q k p", k=KT)
                    for k in range(KT):
                        last = mm(SC2[:, k:k + 1], cols[:, k, :], ones[:, 0:1], start=True, stop=True)
                    last.then_inc(ada_spread, 1)

            def spatial_transposes():
                pe.wait_ge(spatial_made, 1)
                for h in range(AH):
                    last = tp(OB[:, h * P:(h + 1) * P], ws_raw[:, h, :], ident[:, :])
                last.then_inc(ws_mm, 1)

            def x_transposes(i, first):
                pe.wait_ge(xn_made, i + 1)
                if not first:
                    pe.wait_ge(yT_ev, i - 1)
                cols = xn.rearrange("p (m k) -> p k m", k=KT)
                for k in range(KT):
                    last = tp(T4[k // 4][:, k % 4, :], cols[:, k, :], ident[:, :])
                last.then_inc(xT_mm, 1)

            def project(acc, c0, hTs):
                for k in range(KT):
                    last = mm(acc[:, :], hTs[:, k, :], win[:, k, c0:c0 + HALF], start=(k == 0), stop=(k == KT - 1))
                return last

            def logits(n):
                pe.wait_ge(h2T_ev, n)
                for k in range(KT):
                    last = mm(OB[:, 0:NLOG], h2T[:, k, :], wr[:, k, :], start=(k == 0), stop=(k == KT - 1))
                last.then_inc(lg_mm, 1)

            def step(s, par, first=False, second=False, head=True, tail=True, nxt=True):
                hTs = hT[par]
                def win_piece(n):
                    if first:
                        pe.wait_ge(win_in[n], 16)

                if head:
                    pe.wait_ge(hT_made, s + 1)
                    win_piece(0)
                    if not first:
                        pe.wait_ge(u_ev, s)
                    for m in range(4):
                        for k in range(KT):
                            last = mm(QK[:, m, :], win[:, k, C_Q + m * P:C_Q + (m + 1) * P], hTs[:, k, :],
                                      start=(k == 0), stop=(k == KT - 1))
                    last.then_inc(qk_mm, 1)
                if tail and not second:
                    logits(s - 1)
                if second:
                    spread(2)
                    spread(3)
                if head:
                    if not first:
                        pe.wait_ge(rg_made, s)
                    win_piece(1)
                    for k in range(KT):
                        last = mm(ALOW, win[:, k, C_A:P_IN], hTs[:, k, :], start=(k == 0), stop=(k == KT - 1))
                    last.then_inc(alow_mm, 1)
                if tail:
                    pe.wait_ge(ex_made, s)
                    pe.wait_ge(ob_free, s)
                    if second:
                        pe.wait_ge(ada_taken, 4)
                    for cc in range(2):
                        for half in range(2):
                            rows = slice(64 * half, 64 * half + 64)
                            mm(SCO[half][:, 0, cc, :], ex[rows, A_KG, cc, :], ex[rows, A_QD, cc, :], start=True,
                               stop=True)
                            mm(SCO[half][:, 1, cc, :], ex[rows, A_L32, cc, :], ex[rows, A_L32, cc, :], start=True,
                               stop=True)
                            last = mm(L64[half][:, cc, :], ex[rows, A_L64, cc, 0:64], ex[rows, A_L64, cc, 64:P],
                                      start=True, stop=True)
                    last.then_inc(sc_mm, 1)
                if head:
                    pe.wait_ge(qk_ev, s + 1)
                    win_piece(2)
                    project(PJ0, C_V, hTs).then_inc(v_mm, 1)
                    pe.wait_ge(alow_ev, s + 1)
                    for cc in range(2):
                        last = mm(ZA[:, cc, :], wal[:, cc * P:(cc + 1) * P], alT[:, :], start=True, stop=True)
                    last.then_inc(za_mm, 1)
                if tail:
                    pe.wait_ge(sc_off, s)
                    for cc in range(2):
                        last = tp(KDT[:, cc, :], ex[:, A_KD, cc, :], ident[:, :])
                    last.then_inc(kdt_mm, 1)
                    pe.wait_ge(sc_diag, s)
                    pe.wait_ge(st_made, s)
                    for cc in range(2):
                        mm(OB[:, 256 * cc:256 * cc + 256], ex[:, A_QI, cc, :], state[:, cc, :], start=(cc == 0),
                           stop=False)
                    for h in range(AH):
                        last = mm(OB[:, h * P:(h + 1) * P], pT[:, h, :], v_sb[:, h * P:(h + 1) * P], start=False,
                                  stop=(h == AH - 1))
                    last.then_inc(o_mm, 1)
                    pe.wait_ge(kdt_ev, s)
                    for cc in range(2):
                        last = mm(SC1[:, 256 * cc:256 * cc + 256], kdT[:, cc, :], v_sb[:, 256 * cc:256 * cc + 256],
                                  start=True, stop=True)
                    last.then_inc(st_mm, 1)
                    pe.wait_ge(vn_made, s)
                    for h in range(AH):
                        last = mm(SC0[:, h * P:(h + 1) * P], wsT[:, h, :], av_sb[:, h * P:(h + 1) * P], start=True,
                                  stop=True)
                    last.then_inc(sg_mm, 1)
                if head:
                    if first:
                        spatial_transposes()
                    pe.wait_ge(za_ev, s + 1)
                    win_piece(3)
                    project(PJ1, C_AV, hTs).then_inc(av_mm, 1)
                if tail:
                    pe.wait_ge(y_made, s)
                    cols = y_sb.rearrange("p (m k) -> p k m", k=KT)
                    for k in range(KT):
                        last = tp(T4[k // 4][:, k % 4, :], cols[:, k, :], ident[:, :])
                    last.then_inc(yT_mm, 1)
                if second:
                    spread(4)
                if head:
                    pe.wait_ge(v_ev, s + 1)
                    win_piece(4)
                    project(PJ0, C_U, hTs).then_inc(u_mm, 1)
                if second:
                    for piece in range(5, 8):
                        spread(piece)
                    pe.wait_ge(ada_taken, 8)
                    pe.wait_ge(route_in, 16 * 4)
                if tail:
                    pe.wait_ge(yT_ev, s)
                    pe.wait_ge(st_made, s + 1)
                    for half in (1, 0):
                        if second:
                            pe.wait_ge(wout_in[half], 16)
                        for hf in range(2):
                            for k in range(half * KT // 2, (half + 1) * KT // 2):
                                last = mm((SC0, SC1)[hf][:, :], yT[:, k, :], wout[:, k, hf * HALF:(hf + 1) * HALF],
                                          start=(k == KT // 2), stop=(k == KT // 2 - 1))
                    last.then_inc(mix_mm, 1)
                if nxt:
                    x_transposes(s + 1, first)
                if head:
                    pe.wait_ge(av_ev, s + 1)
                    project(PJ1, C_R, hTs).then_inc(r_mm, 1)
                if tail:
                    pe.wait_ge(xn2_made, s)
                    cols = xn2.rearrange("p (m k) -> p k m", k=KT)
                    for k in range(KT):
                        last = tp(S4[k // 4][:, k % 4, :], cols[:, k, :], ident[:, :])
                    last.then_inc(h2T_mm, 1)

            x_transposes(0, True)
            spread(0)
            spread(1)
            step(0, 0, first=True, tail=False)
            step(1, 1, second=True)
            with pe.Fori(1, (NT - 2) // 2) as j:
                step(2 * j, 0)
                step(2 * j + 1, 1)
            step(NT - 2, 0)
            step(NT - 1, (NT - 1) % 2, nxt=False)
            step(NT, 0, head=False, nxt=False)
            logits(NT)

            pe.wait_ge(both_made, 1)
            bothf = both.rearrange("p a b -> p (a b)")
            mm(SC0[:, 0:NT * NE], lstrict[:, :], bothf, start=True, stop=True)
            mm(SC1[:, 0:NT * NE], ones[:, :], bothf, start=True, stop=True).then_inc(rank_mm, 1)
            for m in range(2 * NT):
                pe.wait_ge(slots_made, m + 1)
                last = mm(SC2[:, 0:NBLK], place_hot[:, m, :], block_token[:, m, :], start=(m == 0),
                          stop=(m == 2 * NT - 1))
            last.then_inc(table_mm, 1)

            def row_transposes(b, r, par, first=False):
                pe.wait_ge(xg_in[par], 16 * (r + 1))
                if not first:
                    pe.wait_ge(xg_ev, b)
                cols = xr[par].rearrange("p (m k) -> p k m", k=KT)
                for k in range(KT):
                    last = tp(T4[k // 4][:, k % 4, :], cols[:, k, :], ident[:, :])
                last.then_inc(xg_mm, 1)

            def split_product(acc, l_hi, l_lo, n, cols, k_tiles, width):
                hi, lo = [w[:, n, :].rearrange("p (k n) -> p k n", n=width) for w in (w_hi, w_lo)]
                for k in range(k_tiles):
                    for m, (lhs, rhs) in enumerate(((l_hi, hi), (l_hi, lo), (l_lo, hi))):
                        last = mm(acc[:, :], lhs[:, k, :], rhs[:, k, cols], start=(k == 0 and m == 0),
                                  stop=(k == k_tiles - 1 and m == 2))
                return last

            def up(b, first=False):
                pe.wait_ge(x_lo_made, b + 1)
                if not first:
                    pe.wait_ge(hid_made, b)
                for n, acc in enumerate((PJ0, PJ1)):
                    pe.wait_ge(lo_made[n], 2 * b + 2)
                    split_product(acc, x_hi, x_lo, n, slice(0, FE), KT, FE).then_inc(w_used[n], 1)

            def hidden_transposes(b):
                pe.wait_ge(hid_made, b + 1)
                cols = hid.rearrange("p (m k) -> p k m", k=FKT)
                for k in range(FKT):
                    last = tp(SC2[:, k * P:(k + 1) * P], cols[:, k, :], ident[:, :])
                last.then_inc(hidT_mm, 1)

            def down(b, first=False):
                pe.wait_ge(hidT_ev, b + 1)
                pe.wait_ge(lo_made[2], 2 * b + 2)
                if not first:
                    pe.wait_ge(dn_ev, b)
                for hf in range(2):
                    last = split_product((SC0, SC1)[hf], h_hi, h_lo, 2, slice(hf * HALF, (hf + 1) * HALF), FKT, D)
                last.then_inc(w_used[2], 1)

            pe.wait_ge(idx_made, 1)
            row_transposes(0, 0, 0, True)
            up(0, True)
            row_transposes(1, 0, 1)
            hidden_transposes(0)

            def block_step(b, r, par, first=False, nxt=True):
                up(b)
                if nxt:
                    row_transposes(b + 1, r + par, 1 - par)
                down(b - 1, first)
                hidden_transposes(b)

            block_step(1, 0, 1, first=True)
            with pe.Fori(1, NE // 2 - 1) as q:
                block_step(2 * q, q, 0)
                block_step(2 * q + 1, q, 1)
            block_step(NE - 2, NE // 2 - 1, 0)
            block_step(NE - 1, NE // 2 - 1, 1, nxt=False)
            pe.wait_ge(extra_made, 1)
            n_extra = pe.value_load(nxi[0:1, 0:1], min_val=0, max_val=MAXEXTRA)
            with pe.If(n_extra > 0):
                row_transposes(NE, NE // 2, 0)
            down(NE - 1)
            with pe.Fori(0, MAXEXTRA // 4) as quad:
                with pe.If(n_extra > 4 * quad):
                    with pe.Fori(0, 2) as pair:
                        q = 2 * quad + pair
                        for par in range(2):
                            j = 2 * q + par
                            with pe.If(n_extra > j):
                                up(j + NE)
                                hidden_transposes(j + NE)
                            with pe.If(n_extra > j + 1):
                                row_transposes(j + 1 + NE, q + NE // 2 + par, 1 - par)
                            with pe.If(n_extra > j):
                                down(j + NE)
            pe.nop().then_inc(experts_left, 1)

        @block.scalar
        def _(act):
            f = nc.scalar.activation
            chain = Chain(act, act_done)
            link = chain.link

            def rstd(ss, rs, width):
                link(f(rs, ss, ACT.Ln, bias=eps[:, :], scale=1.0 / width))
                return f(rs, rs, ACT.Exp, scale=-0.5)

            act.wait_ge(norms_in, 16 * 7)
            act.wait_ge(consts_made, 1)
            f(cE[:, :], cT[:, :], ACT.Exp, scale=-1.0).then_inc(act_done, 1)
            chain.n += 1
            def x_norm(i):
                act.wait_ge(xa_in, 16 * (i + 1))
                link(f(junk[:, :], xa, ACT.Square, accum_out=ss1[:, :]))
                rstd(ss1[:, :], rs1[:, :], D).then_inc(rs1_made, 1)

            def step(s, first=False, second=False, head=True, tail=True, nxt=True):
                if head:
                    act.wait_ge(qk_mm, s + 1)
                    if not first:
                        act.wait_ge(ex_made, s)
                    f(qT, QK[:, 0:2, :], ACT.Copy, scale=BK ** -0.5)
                    f(kT, QK[:, 2:4, :], ACT.Copy).then_inc(qk_ev, 1)
                    act.wait_ge(alow_mm, s + 1)
                    f(alT[:, :], ALOW, ACT.Copy).then_inc(alow_ev, 1)
                if tail:
                    act.wait_ge(sc_diag, s)
                    for half in range(2):
                        f(pT4[0:64, :, half, 64:P], L64[half], ACT.Copy)
                        f(pT4[0:32, :, half, 32:64], SCO[half][0:32, 1, :, 32:64], ACT.Copy)
                        last = f(pT4[64:96, :, half, 96:P], SCO[half][64:96, 1, :, 96:P], ACT.Copy)
                    last.then_inc(sc_off, 1)
                    act.wait_ge(kdt_mm, s)
                    f(kdT, KDT, ACT.Copy).then_inc(kdt_ev, 1)
                if head:
                    act.wait_ge(za_mm, s + 1)
                    for cc in range(2):
                        last = f(zb[:, cc, :], ZA[:, cc, :], ACT.Identity, bias=bal[:, cc:cc + 1])
                    last.then_inc(za_ev, 1)
                    act.wait_ge(za_ev, s + 1)
                    link(f(az, zb, ACT.Abs))
                    link(f(az, az, ACT.Exp, scale=-1.0))
                    f(lneg, az, ACT.Ln, bias=1.0).then_inc(ln_made, 1)
                if tail:
                    act.wait_ge(o_mm, s)
                    for h in range(AH):
                        link(f(junk[:, 0:P], OB[:, h * P:(h + 1) * P], ACT.Square, accum_out=sso[:, h:h + 1]))
                    rstd(sso[:, :], rso[:, :], P).then_inc(rso_made, 1)
                if head:
                    act.wait_ge(ex_args, s + 1)
                    f(ex, ex, ACT.Exp, scale=1.0 / TAU).then_inc(ex_exp, 1)
                    act.wait_ge(av_mm, s + 1)
                    if not first:
                        act.wait_ge(sg_mm, s)
                    f(av_sb, PJ1[:, :], ACT.Copy).then_inc(av_ev, 1)
                if first:
                    act.wait_ge(ws_mm, 1)
                    f(wsT[:, :, :].rearrange("p h t -> p (h t)"), OB[:, :], ACT.Copy).then_inc(ob_free, 1)
                if tail:
                    act.wait_ge(yT_mm, s)
                    if second:
                        act.wait_ge(ada_spread, len(PIECES))
                    f(yT[:, 0:4, :], T4[0], ACT.Copy)
                    f(yT[:, 4:8, :], T4[1], ACT.Copy).then_inc(yT_ev, 1)
                if nxt:
                    x_norm(s + 1)
                if head:
                    act.wait_ge(u_mm, s + 1)
                    if not first:
                        act.wait_ge(y_made, s)
                    f(u_sb, PJ0[:, :], ACT.Gelu_apprx_tanh).then_inc(u_ev, 1)
                    act.wait_ge(av_ev, s + 1)
                    link(f(av_sb, av_sb, ACT.Gelu_apprx_tanh))
                    link(f(junk[:, 0:HALF], av_sb, ACT.Square, accum_out=ssv[:, :]))
                    rstd(ssv[:, :], rsv[:, :], HALF).then_inc(rsv_made, 1)
                if tail:
                    act.wait_ge(x1_made, s)
                    link(f(junk[:, :], xb, ACT.Square, accum_out=ss2[:, :]))
                    rstd(ss2[:, :], rs2[:, :], D).then_inc(rs2_made, 1)
                if head:
                    act.wait_ge(r_mm, s + 1)
                    if not first:
                        act.wait_ge(rg_made, s)
                    f(rtmp, PJ1[:, :], ACT.Exp, scale=-1.0).then_inc(r_exp, 1)

            x_norm(0)
            step(0, first=True, tail=False)
            step(1, second=True)
            n0 = chain.base + chain.n
            with act.Fori(1, (NT - 2) // 2) as j:
                chain.base, chain.n = n0 + 2 * ACT_STEP * (j - 1), 0
                step(2 * j)
                assert chain.n == ACT_STEP, ("ACT_STEP", chain.n)
                chain.base, chain.n = n0 + ACT_STEP + 2 * ACT_STEP * (j - 1), 0
                step(2 * j + 1)
            chain.base, chain.n = n0 + (NT - 4) * ACT_STEP, 0
            step(NT - 2)
            step(NT - 1, nxt=False)
            step(NT, head=False, nxt=False)


            def high(n, b, first=False, halves=(0, 1)):
                if not first and 0 in halves:
                    act.wait_ge(w_used[n], b)
                for h in halves:
                    act.wait_ge(raw_in[n][h], 16 * (b + 1))
                    half = slice(h * EW // 2, (h + 1) * EW // 2)
                    f(w_hi[:, n, half], raw[:, n, half], ACT.Copy).then_inc(hi_made[n], 1)

            def rows_high(b, first=False):
                act.wait_ge(xg_mm, b + 1)
                if not first:
                    act.wait_ge(x_lo_made, b)
                for k in range(KT):
                    last = f(xT[:, k, :], T4[k // 4][:, k % 4, :], ACT.Identity, scale=a2[:, k:k + 1],
                             bias=sh2[:, k:k + 1])
                last.then_inc(xg_ev, 1)
                act.wait_ge(xg_ev, b + 1)
                f(x_hi[:, :, :], xT[:, :, :], ACT.Copy).then_inc(x_hi_made, 1)

            def silu(b, first=False):
                act.wait_ge(up_mm, b + 1)
                if not first:
                    act.wait_ge(hid_made, b)
                f(silu_sb, PJ0[:, :], ACT.Silu).then_inc(silu_made, 1)

            def hidden_high(b):
                act.wait_ge(hidT_mm, b + 1)
                f(h_hi[:, :, :], SC2[:, :].rearrange("p (k t) -> p k t", k=FKT), ACT.Copy).then_inc(h_hi_made, 1)

            def store(b, par):
                act.wait_ge(dn_ev, b + 1)
                act.dma_start(y_dram[bass.ts(b, P), :], yb[par]).then_inc(y_out[par], 16)

            def block_step(b, par, first=False, nxt=True, nxt2=True):
                silu(b, first)
                if nxt:
                    high(1, b + 1, halves=(0,))
                    rows_high(b + 1)
                    high(1, b + 1, halves=(1,))
                hidden_high(b)
                if not first:
                    store(b - 1, 1 - par)
                high(2, b, first)
                if nxt2:
                    high(0, b + 2)

            high(0, 0, True)
            act.wait_ge(route_arg, 1)
            f(t4, t4, ACT.Exp).then_inc(route_exp, 1)
            high(1, 0, True)
            act.wait_ge(route_arg, 2)
            f(rs_arg, rs_arg, ACT.Exp).then_inc(route_exp, 1)
            act.wait_ge(idx_made, 1)
            act.wait_ge(x1_out, 16 * NT)
            act.wait_ge(xn2_out, 16 * NT)
            rows_high(0, True)
            high(0, 1)
            block_step(0, 0, first=True)
            block_step(1, 1)
            with act.Fori(1, NE // 2 - 1) as q:
                block_step(2 * q, 0)
                block_step(2 * q + 1, 1)
            block_step(NE - 2, 0, nxt2=False)
            block_step(NE - 1, 1, nxt=False, nxt2=False)
            act.wait_ge(y_zero, 16 * (MAXEXTRA // 4))
            n_extra = act.value_load(nxi[0:1, 0:1], min_val=0, max_val=MAXEXTRA)

            def prepare(b):
                high(0, b)
                rows_high(b)
                high(1, b)

            with act.If(n_extra > 0):
                prepare(NE)
            store(NE - 1, 1)
            with act.Fori(0, MAXEXTRA // 4) as quad:
                with act.If(n_extra > 4 * quad):
                    with act.Fori(0, 2) as pair:
                        q = 2 * quad + pair
                        for par in range(2):
                            j = 2 * q + par
                            with act.If(n_extra > j):
                                high(2, j + NE)
                                silu(j + NE)
                                hidden_high(j + NE)
                            with act.If(n_extra > j + 1):
                                prepare(j + 1 + NE)
                            with act.If(n_extra > j):
                                store(j + NE, par)
            for par in range(2):
                n_par = act.value_load(nxi[0:1, par + 1:par + 2], min_val=0, max_val=MAXEXTRA // 2)
                act.wait_ge(y_out[par], 16 * n_par + 16 * NE // 2)
                f((ssv, ss2)[par][:, :], eps[:, :], ACT.Copy)
            act.nop().then_inc(experts_left, 1)

            def store_out(i):
                act.wait_ge(fo_made, i + 1)
                act.dma_start(out[0, i * P:(i + 1) * P, :], fy1[i]).then_inc(out_out, 16)

            def scale_rows(i):
                act.wait_ge(fy_in[i], 32)
                f(fy1[i], fy1[i], ACT.Copy, scale=gt1[:, i:i + 1]).then_inc(y1_scaled, 1)

            def rms(i):
                act.wait_ge(x2_made, i + 1)
                link(f(junk[:, :], fy1[i], ACT.Square, accum_out=fss[:, i:i + 1]))
                f(frs[:, i:i + 1], fss[:, i:i + 1], ACT.Sqrt, bias=eps[:, :], scale=1.0 / D).then_inc(rms_made, 1)

            for i in range(NT + 2):
                if i < NT:
                    scale_rows(i)
                if 1 <= i <= NT:
                    rms(i - 1)
                if i >= 2:
                    store_out(i - 2)

        @block.vector
        def _(dve):
            v = nc.vector
            tt, ts, stt, cp = v.tensor_tensor, v.tensor_scalar, v.scalar_tensor_tensor, v.tensor_copy
            chain = Chain(dve, dve_done)
            link = chain.link

            dve.wait_ge(act_done, 1)
            link(ts(cE[:, :], cE[:, :], 1.0, None, ALU.add))
            link(v.reciprocal(cE[:, :], cE[:, :]))
            tt(cT[:, :], cT[:, :], cE[:, :], ALU.mult).then_inc(cact_made, 1)
            dve.wait_ge(cact_made, 1)

            def ada(n):
                buf, loads, _ = ada_place(n)
                dve.wait_ge(adaw_in[buf], 16 * loads)
                acc = mod_sum[n // 2][:, (n % 2) * HALF:(n % 2 + 1) * HALF]
                w = ada_bufs[buf]
                link(ts(acc, w[:, 0, :], cT[:, 0:1], None, ALU.mult))
                for k in range(1, KT - 1):
                    link(stt(acc, w[:, k, :], cT[:, k:k + 1], acc, ALU.mult, ALU.add))
                stt(acc, w[:, KT - 1, :], cT[:, KT - 1:KT], acc, ALU.mult, ALU.add).then_inc(ada_sum, 1)

            def take(piece):
                vec, hf = PIECES[piece]
                dve.wait_ge(ada_spread, piece + 1)
                if vec == 0:
                    last = tt(sh1[:, :], SC2[:, 0:KT], bcols[:, 0, :], ALU.add)
                if vec == 3:
                    last = tt(sh2[:, :], SC2[:, 0:KT], bcols[:, 2, :], ALU.add)
                if vec in (1, 4):
                    a, m, gain = (a1, 1, gain1) if vec == 1 else (a2, 3, gain2)
                    link(tt(a[:, :], SC2[:, 0:KT], bcols[:, m, :], ALU.add))
                    last = stt(a[:, :], a[:, :], 1.0, gain[:, :], ALU.add, ALU.mult)
                if vec in GATES:
                    last = cp((g1b if vec == 2 else g2b)[:, hf * HALF:(hf + 1) * HALF], SC2[:, :])
                last.then_inc(ada_taken, 1)

            dve.wait_ge(consts_made, 1)
            cp(iojf[:, :], ioj[:, :])
            cp(base1[:, :], ioe[:, :])
            cp(iota_slot[:, :], iota_i[:, 0:P])
            cp(iota_blk[:, :], iota_i[:, P:P + NBLK])
            cp(thr[:, :], iok[:, :])
            cp(tokf[:, :], toki[:, :])
            for i in range(NT):
                cp(iota4[:, i, :], io4[:, :])
                cp(iota8[:, i, :], io8[:, :])
            v.memset(dec[:, :], 1.0).then_inc(st_made, 1)
            dve.wait_ge(st_made, 1)

            def x_norm(i):
                dve.wait_ge(rs1_made, i + 1)
                dve.wait_ge(xa_in, 16 * (i + 1))
                ts(xn, xa, rs1[:, 0:1], None, ALU.mult).then_inc(xn_made, 1)

            def modulate_xT(i, par):
                dve.wait_ge(xT_mm, i + 1)
                for k in range(KT):
                    last = ts(hT[par][:, k, :], T4[k // 4][:, k % 4, :], a1[:, k:k + 1], sh1[:, k:k + 1],
                              ALU.mult, ALU.add)
                last.then_inc(hT_made, 1)

            B = ex[:, A_QI, :, :]

            def logits(n):
                dve.wait_ge(lg_mm, n)
                tt(lg[:, bass.ds(n - 1, 1), :], OB[:, 0:NLOG].rearrange("p (a n) -> p a n", a=1),
                   brb[:, :].rearrange("p (a n) -> p a n", a=1), ALU.add).then_inc(ob_free, 1)

            def step(s, par, first=False, second=False, head=True, tail=True, nxt=True):
                if tail:
                    if not second:
                        logits(s - 1)
                    dve.wait_ge(sc_mm, s)
                    for j in range(4):
                        r = slice(32 * j, 32 * j + 32)
                        for half in range(2):
                            last = tt(pT4[r, :, half, r], SCO[half][r, 0, :, r],
                                      tri[r, :].rearrange("p (a t) -> p a t", a=1).broadcast_to([32, 2, 32]), ALU.mult)
                    last.then_inc(sc_diag, 1)
                if second:
                    ada(8)
                if head:
                    dve.wait_ge(za_ev, s + 1)
                    link(ts(la, zb, 0.0, None, ALU.min))
                    dve.wait_ge(ln_made, s + 1)
                    link(tt(la, la, lneg, ALU.subtract))
                    if not first:
                        dve.wait_ge(o_mm, s)
                    for cc in range(2):
                        last = v.tensor_tensor_scan(B[:, cc, :], ones[:, :], la[:, cc, :], 0.0, ALU.mult, ALU.add)
                    link(last)
                    full = [P, 2, P]
                    tt(ex[:, A_KD, :, :], B[:, :, P - 1:P].broadcast_to(full), B, ALU.subtract)
                    tt(ex[:, A_L64, :, 64:P], B[:, :, 64:P], B[:, :, 63:64].broadcast_to([P, 2, 64]), ALU.subtract)
                    tt(ex[:, A_L64, :, 0:64], B[:, :, 63:64].broadcast_to([P, 2, 64]), B[:, :, 0:64], ALU.subtract)
                    b64 = B.rearrange("p c (j t) -> p c j t", j=2)
                    l32 = ex[:, A_L32, :, :].rearrange("p c (j t) -> p c j t", j=2)
                    mid = b64[:, :, :, 31:32].broadcast_to([P, 2, 2, 32])
                    tt(l32[:, :, :, 32:64], b64[:, :, :, 32:64], mid, ALU.subtract)
                    tt(l32[:, :, :, 0:32], mid, b64[:, :, :, 0:32], ALU.subtract)
                    b32 = B.rearrange("p c (j t) -> p (c j) t", j=4)
                    ref = b32[:, :, 15:16].broadcast_to([P, 8, 32])
                    tt(ex[:, A_QD, :, :].rearrange("p c (j t) -> p (c j) t", j=4), b32, ref, ALU.subtract)
                    tt(ex[:, A_KG, :, :].rearrange("p c (j t) -> p (c j) t", j=4), ref, b32,
                       ALU.subtract).then_inc(ex_args, 1)
                if tail:
                    dve.wait_ge(st_mm, s)
                    for h in range(AH):
                        r0, cc = 64 * (h % 2), h // 2
                        rows, cols = slice(r0, r0 + 64), slice((h % 2) * P, (h % 2 + 1) * P)
                        last = stt(state[rows, cc, cols], state[rows, cc, cols], dec[rows, cc:cc + 1],
                                   SC1[rows, 256 * cc + (h % 2) * P:256 * cc + (h % 2 + 1) * P], ALU.mult, ALU.add)
                    last.then_inc(st_made, 1)
                if head:
                    dve.wait_ge(v_mm, s + 1)
                    cp(v_sb, PJ0[:, :]).then_inc(v_ev, 1)
                if first:
                    ada(4)
                if tail:
                    dve.wait_ge(sg_mm, s)
                    for h in range(AH):
                        c = slice(h * P, (h + 1) * P)
                        stt(y_sb[:, c], SC0[:, c], bsT[:, h:h + 1], u_sb[:, c], ALU.add, ALU.mult)
                    dve.wait_ge(rso_made, s)
                    for h in range(AH):
                        c = slice(h * P, (h + 1) * P)
                        last = stt(y_sb[:, HALF + h * P:HALF + (h + 1) * P], OB[:, c], rso[:, h:h + 1], rg[:, c],
                                   ALU.mult, ALU.mult)
                    last.then_inc(y_made, 1)
                if second:
                    ada(9)
                if head:
                    dve.wait_ge(ex_exp, s + 1)
                    dve.wait_ge(qk_ev, s + 1)
                    if tail:
                        dve.wait_ge(st_made, s + 1)
                    link(cp(dec[:, :].rearrange("p (c a) -> p c a", a=1), B[:, :, P - 1:P]))
                    ex4 = [ex[:, a, :, :] for a in range(6)]
                    tt(ex4[A_QI], ex4[A_QI], qT, ALU.mult)
                    tt(ex4[A_KD], ex4[A_KD], kT, ALU.mult)
                    tt(ex4[A_L64][:, :, 64:P], ex4[A_L64][:, :, 64:P], qT[:, :, 64:P], ALU.mult)
                    tt(ex4[A_L64][:, :, 0:64], ex4[A_L64][:, :, 0:64], kT[:, :, 0:64], ALU.mult)
                    q4, k4 = [a.rearrange("p c (j t) -> p c j t", j=2) for a in (qT, kT)]
                    tt(l32[:, :, :, 32:64], l32[:, :, :, 32:64], q4[:, :, :, 32:64], ALU.mult)
                    tt(l32[:, :, :, 0:32], l32[:, :, :, 0:32], k4[:, :, :, 0:32], ALU.mult)
                    tt(ex4[A_QD], ex4[A_QD], qT, ALU.mult)
                    tt(ex4[A_KG], ex4[A_KG], kT, ALU.mult).then_inc(ex_made, 1)
                if second:
                    take(4)
                    ada(10)
                    take(5)
                    ada(11)
                    take(6)
                    take(7)
                    dve.wait_ge(ada_taken, len(PIECES))
                if nxt:
                    dve.wait_ge(xT_mm, s + 1)
                    x_norm(s + 1)
                if first:
                    ada(5)
                if tail:
                    dve.wait_ge(mix_mm, s)
                    dve.wait_ge(xb_in, 16 * s)
                    tt(y_sb[:, 0:HALF], SC0[:, :], g1b[:, 0:HALF], ALU.mult)
                    link(tt(y_sb[:, HALF:D], SC1[:, :], g1b[:, HALF:D], ALU.mult))
                    tt(xb, xb, y_sb, ALU.add).then_inc(x1_made, 1)
                if head:
                    dve.wait_ge(rsv_made, s + 1)
                    stt(av_sb, av_sb, rsv[:, 0:1], vgb[:, :], ALU.mult, ALU.mult).then_inc(vn_made, 1)
                if nxt:
                    if not first:
                        dve.wait_ge(r_mm, s)
                    modulate_xT(s + 1, 1 - par)
                if tail:
                    dve.wait_ge(rs2_made, s)
                    if second:
                        dve.wait_ge(route_in, 16 * 4)
                    else:
                        dve.wait_ge(xn2_out, 16 * (s - 1))
                    ts(xn2, xb, rs2[:, 0:1], None, ALU.mult).then_inc(xn2_made, 1)
                if tail:
                    dve.wait_ge(h2T_mm, s)
                    for k in range(KT):
                        last = ts(h2T[:, k, :], S4[k // 4][:, k % 4, :], a2[:, k:k + 1], sh2[:, k:k + 1],
                                  ALU.mult, ALU.add)
                    last.then_inc(h2T_ev, 1)
                if head:
                    if first:
                        dve.wait_ge(const_in, 16 * N_CONST)
                    dve.wait_ge(r_exp, s + 1)
                    link(ts(rtmp, rtmp, 1.0, None, ALU.add))
                    link(v.reciprocal(rtmp, rtmp))
                    link(tt(rtmp, rtmp, PJ1[:, :], ALU.mult))
                    tt(rg, rtmp, ogb[:, :], ALU.mult).then_inc(rg_made, 1)

            ada(0)
            ada(1)
            ada(2)
            x_norm(0)
            take(0)
            ada(3)
            take(1)
            dve.wait_ge(ada_taken, 2)
            modulate_xT(0, 0)
            step(0, 0, first=True, tail=False)
            ada(6)
            take(2)
            take(3)
            ada(7)
            step(1, 1, second=True)
            n0 = chain.base + chain.n
            with dve.Fori(1, (NT - 2) // 2) as j:
                chain.base, chain.n = n0 + 2 * DVE_STEP * (j - 1), 0
                step(2 * j, 0)
                assert chain.n == DVE_STEP, ("DVE_STEP", chain.n)
                chain.base, chain.n = n0 + DVE_STEP + 2 * DVE_STEP * (j - 1), 0
                step(2 * j + 1, 1)
            chain.base, chain.n = n0 + (NT - 4) * DVE_STEP, 0
            step(NT - 2, 0)
            step(NT - 1, (NT - 1) % 2, nxt=False)
            step(NT, 0, head=False, nxt=False)
            logits(NT)

            def bc(a, n):
                return a.rearrange("p (i a) -> p i a", a=1).broadcast_to([P, NT, n])

            def first_max(vals, mx, oh, iota, tmp, n):
                link(v.tensor_reduce(mx, vals, AX.X, ALU.max))
                link(tt(tmp, vals, bc(mx, n), ALU.is_equal))
                link(stt(tmp, tmp, -64.0, iota, ALU.mult, ALU.add))
                link(v.tensor_reduce(gs8, tmp, AX.X, ALU.min))
                link(tt(oh, tmp, bc(gs8, n), ALU.is_equal))

            dve.wait_ge(ob_free, NT + 1)
            grp, exl = lg[:, :, 0:NG], lg[:, :, NG:NLOG].rearrange("p i (g e) -> p i g e", g=NG)
            first_max(grp, gm8, ohg, iota4[:, :, :], t4, NG)
            tt(t4, grp, bc(gm8, NG), ALU.subtract).then_inc(route_arg, 1)
            dve.wait_ge(route_arg, 1)
            for i in range(NT):
                last = tt(eprod[:, i, :, :], exl[:, i, :, :],
                          ohg[:, i, :].rearrange("p (g a) -> p g a", a=1).broadcast_to([P, NG, EPG]), ALU.mult)
            link(last)
            link(v.tensor_reduce(esel, eprod.rearrange("p i g e -> p i e g"), AX.X, ALU.add))
            first_max(esel, m1, oh1, iota8[:, :, :], t8, EPG)
            link(stt(e2, oh1, -BIG, esel, ALU.mult, ALU.add))
            first_max(e2, m2, oh2, iota8[:, :, :], t8, EPG)
            link(tt(t8, oh1, oh2, ALU.add))
            for i in range(NT):
                for oh, dst in ((oh1, full1), (oh2, full2), (t8, both.rearrange("p i (g e) -> p i g e", g=NG))):
                    last = tt(dst[:, i, :, :], ohg[:, i, :].rearrange("p (g a) -> p g a", a=1).broadcast_to([P, NG, EPG]),
                              oh[:, i, :].rearrange("p (a e) -> p a e", a=1).broadcast_to([P, NG, EPG]), ALU.mult)
            last.then_inc(both_made, 1)
            tt(rs_arg, m2, m1, ALU.subtract).then_inc(route_arg, 1)
            dve.wait_ge(route_exp, 1)
            link(v.tensor_reduce(pg, t4, AX.X, ALU.add))
            link(v.reciprocal(pg, pg))
            dve.wait_ge(route_exp, 2)
            link(ts(gt1[:, :], rs_arg, 1.0, None, ALU.add))
            link(v.reciprocal(gt1[:, :], gt1[:, :]))
            link(tt(gt1[:, :], gt1[:, :], pg, ALU.mult))
            tt(gt2[:, :], gt1[:, :], rs_arg, ALU.mult)
            dve.wait_ge(rank_mm, 1)
            tot = rank2
            cp(rank, SC0[:, 0:NT * NE].rearrange("p (i e) -> p i e", i=NT))
            cp(tot, SC1[:, 0:NT * NE].rearrange("p (i e) -> p i e", i=NT))
            link(v.memset(prev[:, 0, :], 0.0))
            for i in range(1, NT):
                link(tt(prev[:, i, :], prev[:, i - 1, :], tot[:, i - 1, :], ALU.add))
            link(tt(count, prev[:, NT - 1, :], tot[:, NT - 1, :], ALU.add))
            link(tt(rank, rank, prev, ALU.add))
            link(tt(cmpx, count.rearrange("p (e a) -> p e a", a=1).broadcast_to([P, NE, EPG]),
                    thr[:, :].rearrange("p (a k) -> p a k", a=1).broadcast_to([P, NE, EPG]), ALU.is_gt))
            link(v.tensor_reduce(nex, cmpx, AX.X, ALU.add))
            link(v.tensor_tensor_scan(ebi, ones[:, 0:NE], nex, 0.0, ALU.mult, ALU.add))
            link(tt(base2, ebi, nex, ALU.subtract))
            link(ts(base2, base2, float(P), float((NE - 1) * P), ALU.mult, ALU.add))
            link(tt(count, base1[:, :], base2, ALU.subtract))
            link(ts(prev, rank, float(P), None, ALU.is_lt))
            link(tt(prev, prev, count.rearrange("p (a e) -> p a e", a=1).broadcast_to([P, NT, NE]), ALU.mult))
            link(tt(rank, rank, prev, ALU.add))
            link(tt(rank, rank, base2.rearrange("p (a e) -> p a e", a=1).broadcast_to([P, NT, NE]), ALU.add))
            for j, full in enumerate((full1, full2)):
                link(tt(rank2, rank, full.rearrange("p i g e -> p i (g e)"), ALU.mult))
                link(v.tensor_reduce(sl[:, j, :], rank2, AX.X, ALU.add))
            link(cp(sli[:, :, :], sl))
            link(ts(place_i[:, :, :], sli[:, :, :], P - 1, None, ALU.bitwise_and))
            link(cp(place, place_i[:, :, :]))
            link(tt(first_slot, sl, place, ALU.subtract))
            for i in range(NT):
                for j in range(2):
                    ts(place_hot[:, 2 * i + j, :], iota_slot[:, :], place[:, j, i:i + 1], None, ALU.is_equal)
                    ts(block_token[:, 2 * i + j, :], iota_blk[:, :], first_slot[:, j, i:i + 1], tokf[:, i:i + 1],
                       ALU.is_equal, ALU.mult).then_inc(slots_made, 1)
            link(tt(cmpj, iojf[:, :].rearrange("p (j a) -> p j a", a=1).broadcast_to([P, MAXEXTRA, NE]),
                    ebi.rearrange("p (a e) -> p a e", a=1).broadcast_to([P, MAXEXTRA, NE]), ALU.is_ge))
            link(v.tensor_reduce(exf, cmpj, AX.X, ALU.add))
            link(ts(exf, exf, float(NE - 1), None, ALU.min))
            cp(exi[:, :], exf)
            link(ts(cmpj[:, :, 0], iojf[:, :], ebi[:, NE - 1:NE], None, ALU.is_lt))
            link(v.tensor_reduce(n_even_odd, cmpj[:, :, 0].rearrange("p (j two) -> p two j", two=2), AX.X, ALU.add))
            cp(nxi[:, 1:3], n_even_odd)
            cp(nxi[:, 0:1], ebi[:, NE - 1:NE]).then_inc(extra_made, 1)
            dve.wait_ge(table_mm, 1)
            cp(idx[:, :], SC2[:, 0:NBLK]).then_inc(idx_made, 1)

            def low(n, b, halves=(0, 1)):
                for h in halves:
                    half = slice(h * EW // 2, (h + 1) * EW // 2)
                    dve.wait_ge(hi_made[n], 2 * b + h + 1)
                    tt(w_lo[:, n, half], raw[:, n, half], w_hi[:, n, half].bitcast(F32), ALU.subtract
                       ).then_inc(lo_made[n], 1)

            def rows_low(b):
                dve.wait_ge(x_hi_made, b + 1)
                tt(x_lo[:, :, :], xT[:, :, :], x_hi[:, :, :].bitcast(F32), ALU.subtract).then_inc(x_lo_made, 1)

            def hidden(b, first=False):
                dve.wait_ge(silu_made, b + 1)
                if not first:
                    dve.wait_ge(hidT_mm, b)
                tt(hid, silu_sb, PJ1[:, :], ALU.mult).then_inc(hid_made, 1)

            def gated_rows(b, r, par, first=False):
                dve.wait_ge(dn_mm, b + 1)
                if not first:
                    dve.wait_ge(y_out[par], 16 * r)
                tt(yb[par][:, 0:HALF], SC0[:, :], g2b[:, 0:HALF], ALU.mult)
                tt(yb[par][:, HALF:D], SC1[:, :], g2b[:, HALF:D], ALU.mult).then_inc(dn_ev, 1)

            def hidden_low(b):
                dve.wait_ge(h_hi_made, b + 1)
                tt(h_lo[:, :, :], SC2[:, :].rearrange("p (k t) -> p k t", k=FKT), h_hi[:, :, :].bitcast(F32),
                   ALU.subtract).then_inc(hidT_ev, 1)

            def block_step(b, r, par, first=False, nxt=True, nxt2=True, fresh=False):
                hidden(b, first)
                if nxt:
                    low(1, b + 1, (0,))
                    rows_low(b + 1)
                if not first:
                    gated_rows(b - 1, r - 1 + par, 1 - par, fresh)
                hidden_low(b)
                if nxt:
                    low(1, b + 1, (1,))
                low(2, b)
                if nxt2:
                    low(0, b + 2)

            rows_low(0)
            low(0, 1)
            block_step(0, 0, 0, first=True)
            block_step(1, 0, 1, fresh=True)
            block_step(2, 1, 0, fresh=True)
            block_step(3, 1, 1)
            with dve.Fori(2, NE // 2 - 1) as q:
                block_step(2 * q, q, 0)
                block_step(2 * q + 1, q, 1)
            block_step(NE - 2, NE // 2 - 1, 0, nxt2=False)
            block_step(NE - 1, NE // 2 - 1, 1, nxt=False, nxt2=False)
            dve.wait_ge(extra_made, 1)
            n_extra = dve.value_load(nxi[0:1, 0:1], min_val=0, max_val=MAXEXTRA)

            def prepare(b):
                low(0, b)
                rows_low(b)
                low(1, b)

            with dve.If(n_extra > 0):
                prepare(NE)
            gated_rows(NE - 1, NE // 2 - 1, 1)
            with dve.Fori(0, MAXEXTRA // 4) as quad:
                with dve.If(n_extra > 4 * quad):
                    with dve.Fori(0, 2) as pair:
                        q = 2 * quad + pair
                        for par in range(2):
                            j = 2 * q + par
                            with dve.If(n_extra > j):
                                low(2, j + NE)
                                hidden(j + NE)
                                hidden_low(j + NE)
                            with dve.If(n_extra > j + 1):
                                prepare(j + 1 + NE)
                            with dve.If(n_extra > j):
                                gated_rows(j + NE, q + NE // 2, par)
            dve.nop().then_inc(experts_left, 1)

            dve.wait_ge(fgb_in, 16)
            dve.wait_ge(fx_in, 16)

            def combine(i):
                dve.wait_ge(y1_scaled, i + 1)
                link(stt(fy1[i], fy2[i], gt2[:, i:i + 1], fy1[i], ALU.mult, ALU.add))
                tt(fy1[i], fy1[i], fx[:, i, :], ALU.add).then_inc(x2_made, 1)

            def finish(i):
                dve.wait_ge(rms_made, i + 1)
                link(v.reciprocal(frs[:, i:i + 1], frs[:, i:i + 1]))
                stt(fy1[i], fy1[i], frs[:, i:i + 1], fgb[:, :], ALU.mult, ALU.mult).then_inc(fo_made, 1)

            for i in range(NT + 1):
                if i < NT:
                    combine(i)
                if i:
                    finish(i - 1)


_INS = ["x", "c", "w_ada", "b_ada", "norm1_gain", "norm2_gain", "w_in", "a_v_gain", "a_w_s", "a_b_s", "b_w_alpha",
        "b_b_alpha", "b_out_gain", "w_out", "w_group", "b_group", "w_router", "b_router", "w1", "w3", "w2",
        "final_gain"]


def kernel(**inputs):
    import numpy as np
    import concourse.bacc as bacc
    from concourse.bass_utils import run_bass_kernel_spmd

    nc = bacc.Bacc("TRN2", target_bir_lowering=False, num_devices=1)
    arrays, args = {}, []
    for name in _INS:
        a = np.ascontiguousarray(inputs[name])
        arrays[f"in_{name}"] = a
        args.append(nc.dram_tensor(f"in_{name}", a.shape, mybir.dt.from_np(a.dtype), kind="ExternalInput").ap())
    args.append(nc.dram_tensor("out_0", (1, SEQ, D), F32, kind="ExternalOutput").ap())
    trunk(nc, *args)
    result = run_bass_kernel_spmd(nc, [arrays], core_ids=[0])
    return result.results[0]["out_0"]
```
